# Optimizing a Trainium2 kernel written in Bass

```python
import jax, jax.numpy as jnp
from jax import lax
import numpy as np

D_MODEL = 1024
BATCH = 1
SEQ = 256
DEPTH = 2

CHUNK = 64
MIX_WIDTH = D_MODEL
A_HEADS = 4
A_DK = 128
A_DV = 128
B_HEADS = 4
B_DK = 64
B_DV = 128
GLA_RANK = 16
GLA_TAU = 16.0
C_HEADS = 4
C_DK = 64
C_DV = 128
ROPE_BASE = 10000.0
D_WIDTH = 512
D_BLOCKS = 8
D_BLOCK_DIM = D_WIDTH // D_BLOCKS
D_CONV = 4
RGLRU_C = 8.0
MOE_GROUPS = 4
MOE_EXPERTS_PER_GROUP = 8
MOE_N_EXPERTS = MOE_GROUPS * MOE_EXPERTS_PER_GROUP
MOE_TOPK = 2
MOE_DFF = 512
N_EVEN = (DEPTH + 1) // 2
N_ODD = DEPTH // 2
EPS = 1e-6

EVEN_SPLITS = (A_HEADS * A_DK, A_HEADS * A_DK, A_HEADS * A_DV, A_HEADS * A_DV,
               B_HEADS * B_DK, B_HEADS * B_DK, B_HEADS * B_DV, GLA_RANK, B_HEADS * B_DV)
EVEN_IN = sum(EVEN_SPLITS)
ODD_SPLITS = (C_HEADS * C_DK, C_HEADS * C_DK, C_HEADS * C_DV, C_HEADS * C_DV, D_WIDTH, D_WIDTH)
ODD_IN = sum(ODD_SPLITS)

kernel_name = 'hybrid_hgrn2_gla_retnet_rglru_hmoe'

def rms_norm(x, w):
    xf = x.astype(jnp.float32)
    y = xf * lax.rsqrt(jnp.mean(xf * xf, axis=-1, keepdims=True) + EPS)
    return (y * w.astype(jnp.float32)).astype(x.dtype)

def split_cols(t, sizes):
    return jnp.split(t, [int(c) for c in np.cumsum(sizes)[:-1]], axis=-1)

def split_heads(t, n_heads):
    B, L, _ = t.shape
    return t.reshape(B, L, n_heads, -1).transpose(0, 2, 1, 3)

def merge_heads(t):
    B, H, L, d = t.shape
    return t.transpose(0, 2, 1, 3).reshape(B, L, H * d)

def head_norm(o, w, center):
    if center:
        o = o - jnp.mean(o, axis=-1, keepdims=True)
    o = o * lax.rsqrt(jnp.mean(o * o, axis=-1, keepdims=True) + EPS)
    H, dv = o.shape[1], o.shape[3]
    return o * w.astype(jnp.float32).reshape(1, H, 1, dv)

def rope(t, pos):
    half = t.shape[-1] // 2
    inv = ROPE_BASE ** (-jnp.arange(half, dtype=jnp.float32) / half)
    ang = pos[:, None] * inv[None, :]
    cos, sin = jnp.cos(ang), jnp.sin(ang)
    t1, t2 = t[..., :half], t[..., half:]
    return jnp.concatenate([t1 * cos - t2 * sin, t1 * sin + t2 * cos], axis=-1)

def chunked_gla(q, k, v, log_g):
    B, H, L, dk = q.shape
    dv = v.shape[-1]
    n = L // CHUNK

    def to_chunks(t):
        return jnp.moveaxis(t.astype(jnp.float32).reshape(B, H, n, CHUNK, t.shape[-1]), 2, 0)

    causal = jnp.tril(jnp.ones((CHUNK, CHUNK), dtype=bool))[:, :, None]

    def step(S, blk):
        qc, kc, vc, gc = blk
        b = jnp.cumsum(gc, axis=2)
        b_last = b[:, :, -1:, :]
        o_inter = jnp.einsum('bhtd,bhdv->bhtv', qc * jnp.exp(b), S)
        rel = jnp.where(causal, b[:, :, :, None, :] - b[:, :, None, :, :], -jnp.inf)
        scores = jnp.einsum('bhtd,bhsd,bhtsd->bhts', qc, kc, jnp.exp(rel))
        o_intra = jnp.einsum('bhts,bhsv->bhtv', scores, vc)
        S = jnp.exp(b_last)[:, :, 0, :, None] * S + jnp.einsum(
            'bhsd,bhsv->bhdv', kc * jnp.exp(b_last - b), vc)
        return S, o_inter + o_intra

    S0 = jnp.zeros((B, H, dk, dv), jnp.float32)
    _, o = lax.scan(step, S0, (to_chunks(q), to_chunks(k), to_chunks(v), to_chunks(log_g)))
    return jnp.moveaxis(o, 0, 2).reshape(B, H, L, dv)

def even_mixer(h, w_in, lb, gla_w_up, gla_b_up, hgrn_norm_w, gla_norm_w, w_out):
    proj = (h @ w_in).astype(jnp.float32)
    a_q, a_f, a_i, a_g, b_q, b_k, b_v, b_low, b_r = split_cols(proj, EVEN_SPLITS)
    f = lb + (1.0 - lb) * jax.nn.sigmoid(a_f)
    o_a = chunked_gla(split_heads(a_q, A_HEADS), split_heads(1.0 - f, A_HEADS),
                      split_heads(a_i, A_HEADS), split_heads(jnp.log(f), A_HEADS))
    y_a = merge_heads(head_norm(o_a, hgrn_norm_w, False)) * jax.nn.silu(a_g)
    z = b_low @ gla_w_up + gla_b_up
    log_alpha = jax.nn.log_sigmoid(z) / GLA_TAU
    o_b = chunked_gla(split_heads(b_q * B_DK ** -0.5, B_HEADS), split_heads(b_k, B_HEADS),
                      split_heads(b_v, B_HEADS), split_heads(log_alpha, B_HEADS))
    y_b = merge_heads(head_norm(o_b, gla_norm_w, False)) * jax.nn.silu(b_r)
    y = jnp.concatenate([y_a, y_b], axis=-1).astype(h.dtype)
    return y @ w_out

def odd_mixer(h, w_in, ret_norm_w, conv_w, conv_b, w_r, b_r, w_i, b_i, lam, w_out):
    B, L, _ = h.shape
    proj = (h @ w_in).astype(jnp.float32)
    c_q, c_k, c_v, c_g, d_x, d_gate = split_cols(proj, ODD_SPLITS)
    pos = jnp.arange(L, dtype=jnp.float32)
    q = rope(split_heads(c_q, C_HEADS), pos)
    k = rope(split_heads(c_k, C_HEADS), pos) * C_DK ** -0.5
    log_gamma = jnp.log1p(-jnp.exp2(-5.0 - jnp.arange(C_HEADS, dtype=jnp.float32)))
    log_g = jnp.broadcast_to(log_gamma[None, :, None, None], (B, C_HEADS, L, C_DK))
    o_c = chunked_gla(q, k, split_heads(c_v, C_HEADS), log_g)
    y_c = merge_heads(head_norm(o_c, ret_norm_w, True)) * jax.nn.silu(c_g)
    xp = jnp.pad(d_x, ((0, 0), (D_CONV - 1, 0), (0, 0)))
    xc = conv_b
    for j in range(D_CONV):
        xc = xc + xp[:, j:j + L, :] * conv_w[j]
    xb = xc.reshape(B, L, D_BLOCKS, D_BLOCK_DIM)
    r = jax.nn.sigmoid(jnp.einsum('blnd,nde->blne', xb, w_r).reshape(B, L, D_WIDTH) + b_r)
    i = jax.nn.sigmoid(jnp.einsum('blnd,nde->blne', xb, w_i).reshape(B, L, D_WIDTH) + b_i)
    log_a = -RGLRU_C * r * jax.nn.softplus(-lam)
    a = jnp.exp(log_a)
    u = jnp.sqrt(-jnp.expm1(2.0 * log_a)) * (i * xc)

    def combine(left, right):
        a1, b1 = left
        a2, b2 = right
        return a1 * a2, a2 * b1 + b2

    _, hs = lax.associative_scan(combine, (a, u), axis=1)
    y_d = hs * jax.nn.gelu(d_gate)
    y = jnp.concatenate([y_c, y_d], axis=-1).astype(h.dtype)
    return y @ w_out

def hier_moe(h, w_group, b_group, w_expert, b_expert, w1, w3, w2):
    B, L, D = h.shape
    xt = h.reshape(B * L, D)
    g_logits = (xt @ w_group).astype(jnp.float32) + b_group
    g_prob = jax.nn.softmax(g_logits, axis=-1)
    g_idx = jnp.argmax(g_logits, axis=-1)
    g_w = jnp.take_along_axis(g_prob, g_idx[:, None], axis=-1)
    e_logits = ((xt @ w_expert).astype(jnp.float32) + b_expert).reshape(-1, MOE_GROUPS, MOE_EXPERTS_PER_GROUP)
    e_sel = jnp.take_along_axis(e_logits, g_idx[:, None, None], axis=1)[:, 0]
    top_v, top_i = lax.top_k(e_sel, MOE_TOPK)
    top_w = jax.nn.softmax(top_v, axis=-1)
    e_gate = jnp.sum(jax.nn.one_hot(top_i, MOE_EXPERTS_PER_GROUP) * top_w[..., None], axis=1)
    gate = (jax.nn.one_hot(g_idx, MOE_GROUPS)[:, :, None] * e_gate[:, None, :]
            * g_w[:, :, None]).reshape(-1, MOE_N_EXPERTS)

    def expert_step(acc, p):
        w1e, w3e, w2e, ge = p
        hid = jax.nn.silu(xt @ w1e) * (xt @ w3e)
        return acc + ge[:, None].astype(xt.dtype) * (hid @ w2e), None

    out, _ = lax.scan(expert_step, jnp.zeros_like(xt), (w1, w3, w2, gate.T))
    return out.reshape(B, L, D)

def setup_inputs(seed: int = 0) -> dict:
    key = jax.random.key(seed)
    ks = jax.random.split(key, 32)
    f32 = jnp.float32

    def nrm(k, shape, scale):
        return jax.random.normal(k, shape, f32) * scale

    def gain(k, shape):
        return 1.0 + 0.02 * jax.random.normal(k, shape, f32)

    u = jax.random.uniform(ks[18], (N_ODD, D_WIDTH), f32, minval=0.9, maxval=0.999)
    s = u ** (1.0 / RGLRU_C)
    return {
        'x': nrm(ks[0], (BATCH, SEQ, D_MODEL), 1.0),
        'norm_mix': gain(ks[1], (DEPTH, D_MODEL)),
        'norm_ffn': gain(ks[2], (DEPTH, D_MODEL)),
        'norm_final': gain(ks[3], (D_MODEL,)),
        'even_w_in': nrm(ks[4], (N_EVEN, D_MODEL, EVEN_IN), D_MODEL ** -0.5),
        'hgrn_lb_logits': nrm(ks[5], (DEPTH + 1, A_HEADS * A_DK), 0.5),
        'hgrn_norm_w': gain(ks[6], (N_EVEN, A_HEADS * A_DV)),
        'gla_w_up': nrm(ks[7], (N_EVEN, GLA_RANK, B_HEADS * B_DK), GLA_RANK ** -0.5),
        'gla_b_up': nrm(ks[8], (N_EVEN, B_HEADS * B_DK), 0.02),
        'gla_norm_w': gain(ks[9], (N_EVEN, B_HEADS * B_DV)),
        'even_w_out': nrm(ks[10], (N_EVEN, MIX_WIDTH, D_MODEL), MIX_WIDTH ** -0.5),
        'odd_w_in': nrm(ks[11], (N_ODD, D_MODEL, ODD_IN), D_MODEL ** -0.5),
        'ret_norm_w': gain(ks[12], (N_ODD, C_HEADS * C_DV)),
        'conv_w': nrm(ks[13], (N_ODD, D_CONV, D_WIDTH), D_CONV ** -0.5),
        'conv_b': nrm(ks[14], (N_ODD, D_WIDTH), 0.02),
        'rglru_w_r': nrm(ks[15], (N_ODD, D_BLOCKS, D_BLOCK_DIM, D_BLOCK_DIM), D_BLOCK_DIM ** -0.5),
        'rglru_b_r': nrm(ks[16], (N_ODD, D_WIDTH), 0.02),
        'rglru_w_i': nrm(ks[17], (N_ODD, D_BLOCKS, D_BLOCK_DIM, D_BLOCK_DIM), D_BLOCK_DIM ** -0.5),
        'rglru_b_i': nrm(ks[19], (N_ODD, D_WIDTH), 0.02),
        'rglru_lambda': jnp.log(s) - jnp.log1p(-s),
        'odd_w_out': nrm(ks[20], (N_ODD, MIX_WIDTH, D_MODEL), MIX_WIDTH ** -0.5),
        'moe_w_group': nrm(ks[21], (DEPTH, D_MODEL, MOE_GROUPS), D_MODEL ** -0.5),
        'moe_b_group': nrm(ks[22], (DEPTH, MOE_GROUPS), 0.01),
        'moe_w_expert': nrm(ks[23], (DEPTH, D_MODEL, MOE_N_EXPERTS), D_MODEL ** -0.5),
        'moe_b_expert': nrm(ks[24], (DEPTH, MOE_N_EXPERTS), 0.01),
        'moe_w1': nrm(ks[25], (DEPTH, MOE_N_EXPERTS, D_MODEL, MOE_DFF), D_MODEL ** -0.5),
        'moe_w3': nrm(ks[26], (DEPTH, MOE_N_EXPERTS, D_MODEL, MOE_DFF), D_MODEL ** -0.5),
        'moe_w2': nrm(ks[27], (DEPTH, MOE_N_EXPERTS, MOE_DFF, D_MODEL), MOE_DFF ** -0.5),
    }

def reference(x, norm_mix, norm_ffn, norm_final, even_w_in, hgrn_lb_logits, hgrn_norm_w,
              gla_w_up, gla_b_up, gla_norm_w, even_w_out, odd_w_in, ret_norm_w, conv_w, conv_b,
              rglru_w_r, rglru_b_r, rglru_w_i, rglru_b_i, rglru_lambda, odd_w_out,
              moe_w_group, moe_b_group, moe_w_expert, moe_b_expert, moe_w1, moe_w3, moe_w2):
    lb_table = jnp.cumsum(jax.nn.softmax(hgrn_lb_logits.astype(jnp.float32), axis=0), axis=0)
    for l in range(DEPTH):
        j = l // 2
        hn = rms_norm(x, norm_mix[l])
        if l % 2 == 0:
            mix = even_mixer(hn, even_w_in[j], lb_table[l], gla_w_up[j], gla_b_up[j],
                             hgrn_norm_w[j], gla_norm_w[j], even_w_out[j])
        else:
            mix = odd_mixer(hn, odd_w_in[j], ret_norm_w[j], conv_w[j], conv_b[j],
                            rglru_w_r[j], rglru_b_r[j], rglru_w_i[j], rglru_b_i[j],
                            rglru_lambda[j], odd_w_out[j])
        x = x + mix
        x = x + hier_moe(rms_norm(x, norm_ffn[l]), moe_w_group[l], moe_b_group[l],
                         moe_w_expert[l], moe_b_expert[l], moe_w1[l], moe_w3[l], moe_w2[l])
    return rms_norm(x, norm_final)


_drawn_inputs = setup_inputs


def setup_inputs(seed=0):
    import zlib

    import numpy as np

    out = dict(_drawn_inputs(seed))
    spreads = {}
    factors = {'norm_final': 9.001,
     'gla_b_up': 7.286,
     'ret_norm_w': 4.059,
     'rglru_b_r': 53.472,
     'rglru_b_i': 35.578,
     'moe_b_group': 2.748}
    for name, (base, spread) in spreads.items():
        noise = np.random.default_rng([zlib.crc32(name.encode()), seed]).standard_normal(out[name].shape)
        drawn = base * np.exp(spread * noise) if base else spread * noise
        out[name] = __import__('jax').numpy.asarray(drawn.astype(out[name].dtype))
    for name, factor in factors.items():
        out[name] = (out[name] * factor).astype(out[name].dtype)
    return out
```

```python
from contextlib import ExitStack

import numpy as np

import concourse.bass as bass
from concourse import mybir

F32 = mybir.dt.float32
I32 = mybir.dt.int32
U8 = mybir.dt.uint8
BF16 = mybir.dt.bfloat16
ACT = mybir.ActivationFunctionType
ALU = mybir.AluOpType
AX = mybir.AxisListType

P = 128
T = 256
TT = T // P
D = 1024
KC = D // P
EPS = 1e-6
HEADS = 4
CONV = 4
RG_C = 8.0
NG, NE_G = 4, 8
NE = NG * NE_G
FF = 512
PASS = 32
Q = P // PASS
SLOTS = 3
SLOT = 3 * D * FF // P
PIECE = KC * 512
ORDER = (0, 2, 1)
LEVELS = (64, 32, 16, 8, 4, 2, 1)
BIG1, BIG2 = 1.0e30, 1.0e32
EVEN_COLS = {"a_q": 0, "a_f": 512, "a_i": 1024, "a_g": 1536, "b_qk": 2048, "b_v": 2560, "b_low": 3072, "b_r": 3088}
ODD_COLS = {"c_qk": 0, "c_v": 512, "c_g": 1024, "d_x": 1536, "d_gate": 2048}

SHAPE_CONSTS = {"ident": 128, "before": 128, "ones": 128, "swap": 128, "rope": 1024, "decay": 1536,
                "iota": 256, "down32": 32, "down4": 4}
VECTORS = {"norm_mix": 16, "norm_ffn": 16, "lb": 12, "even_w": 8, "gla_b": 2, "ret_w": 4, "conv_w": 16,
           "conv_b": 4, "b_r": 4, "b_i": 4, "lam": 4, "w_group": 64, "w_expert": 512, "b_group": 8,
           "b_expert": 64}


def places(widths):
    at, out = 0, {}
    for name, w in widths.items():
        out[name] = (at, w)
        at += w
    return out, at


def shape_constants():
    p = np.arange(P)
    half = 32
    inv = np.float32(10000.0) ** (-np.arange(half, dtype=np.float32) / np.float32(half))
    ang = (np.arange(T, dtype=np.float32)[:, None] * inv[None, :]).astype(np.float32)
    cos, sin = np.cos(ang).T.astype(np.float32), np.sin(ang).T.astype(np.float32)
    cos, sin = cos[p % half], sin[p % half] * np.where(p % 64 < half, -1.0, 1.0)[:, None]
    k_scale = 64.0 ** -0.5
    rope = np.concatenate([cos, cos * k_scale, sin, sin * k_scale], axis=1)
    log_gamma = np.log1p(-np.exp2(-5.0 - np.arange(HEADS)))
    decay = np.zeros((P, 2, 3, 2, P))
    for parity in range(2):
        for block in range(3):
            for pair in range(2):
                gap = p[None, :] - p[:, None] + (P if block == 2 else 0)
                decay[:, parity, block, pair] = np.where(gap >= 0, np.exp(np.maximum(gap, 0) * log_gamma[2 * pair + parity]), 0)
    parts = {"ident": np.eye(P), "before": (p[:, None] < p[None, :]), "ones": np.ones((P, P)),
             "swap": (p[:, None] == (p[None, :] ^ half)), "rope": rope, "decay": decay.reshape(P, -1),
             "iota": np.broadcast_to(np.arange(1, T + 1), (P, T)),
             "down32": np.broadcast_to(np.arange(NE, 0, -1), (P, NE)),
             "down4": np.broadcast_to(np.arange(NG, 0, -1), (P, NG))}
    packed = np.concatenate([np.asarray(parts[n], np.float32) for n in SHAPE_CONSTS], axis=1)
    masks = np.stack([(p[:, None] // (2 * h) == p[None, :] // (2 * h)) & (p[:, None] % (2 * h) < h) & (p[None, :] % (2 * h) >= h)
                      for h in LEVELS], axis=1)
    return np.ascontiguousarray(packed), np.ascontiguousarray(masks.astype(np.float32).reshape(P, -1))


class Staged:

    def __init__(self, sem, each):
        self.sem, self.each = sem, each

    def at(self, stage, value):
        return self.sem, self.each * stage + value


def trunk(nc, x_in, even_w_in, even_w_out, odd_w_in, odd_w_out, gla_w_up, rglru_w_r, rglru_w_i,
          moe_w1, moe_w3, moe_w2, norm_final, vectors, shape_consts, masks_in, out):
    const_at, n_const = places(SHAPE_CONSTS)
    vec_at, n_vec = places(VECTORS)

    with ExitStack() as ctx:
        def sb(name, shape, dt=F32):
            return ctx.enter_context(nc.sbuf_tensor(name, shape, dt))

        def sem(name):
            return ctx.enter_context(nc.semaphore(name))

        bank = [ctx.enter_context(nc.psum_tensor(f"bank{i}", [P, 512], F32)) for i in range(8)]

        weights = sb("weights", [P, SLOTS, SLOT])
        consts = sb("consts", [P, n_const])
        vecs = sb("vecs", [P, n_vec])
        masks = sb("masks", [P, len(LEVELS) * P], U8)
        x = sb("x", [P, TT, D])
        act_T = sb("act_T", [P, KC, T])
        y_T = sb("y_T", [P, KC, T])
        tok = sb("tok", [P, TT, D])
        gates = sb("gates", [P, TT, D])
        sums = sb("sums", [P, 2])
        root = sb("root", [P, 2])
        scale = sb("scale", [P, 2])
        lb_e = sb("lb_e", [P, 3, 4])
        lb_t = sb("lb_t", [P, 3, 4])
        head_ss = sb("head_ss", [P, 16])
        head_r = sb("head_r", [P, 16])
        head_m = sb("head_m", [P, 8])
        w_rg = sb("w_rg", [P, 2, 4, P])
        sp = sb("sp", [P, 8, 4])
        nb = sb("nb", [P, 2, 4])
        counts = sb("counts", [1, NE], I32)
        zeros = sb("zeros", [P, 512], BF16)

        def const(name, a=0, b=None):
            at, w = const_at[name]
            return consts[:, at + a:at + (w if b is None else b)]

        def vec(name, a=0, b=None):
            at, w = vec_at[name]
            return vecs[:, at + a:at + (w if b is None else b)]

        ident = const("ident")

        def work(at, size):
            return weights[:, 2, at:at + size]

        qA, kA, bA = (work(i * 1024, 1024) for i in range(3))
        qB, kB, bB = (work(3072 + i * 512, 512) for i in range(3))
        decA = [work(4608 + i * 1024, 1024) for i in range(2)]
        decB = [work(6656 + i * 512, 512) for i in range(2)]
        SA = work(7680, 1536)
        SB = work(9216, 1536)
        low = weights[0:16, 2, 10752:10752 + T]
        w_up = weights[0:16, 2, 11008:11008 + T]
        masks_wide = weights[:, 2, 11264:11264 + len(LEVELS) * P]
        restart = y_T[:, 0:4, :].rearrange("p k t -> p (k t)")
        raw, rot, tmp = (work(i * 1024, 1024) for i in range(3))
        SC = work(3072, 1536)
        DXW = T + 4
        dx = work(4608, 4 * DXW).rearrange("p (m t) -> p m t", m=4)
        o1 = 4608 + 4 * DXW
        xc, rr, ii, th, dg, gl = (work(o1 + i * 1024, 1024) for i in range(6))
        assert o1 + 6 * 1024 <= SLOT

        free = {"y_T": (y_T[:, :, :].rearrange("p k t -> p (k t)"), 0), "gates": (gates[:, :, :].rearrange("p a d -> p (a d)"), 0)}

        def over(host, *shape):
            flat, at = free[host]
            size = int(np.prod(shape))
            free[host] = (flat, at + size)
            assert at + size <= TT * D
            v = flat[:, at:at + size]
            names = "abcd"[:len(shape)]
            return v.rearrange(f"p ({' '.join(names)}) -> p {' '.join(names)}", **dict(zip(names[1:], shape[1:])))

        r_small = over("y_T", 2, 8, 4)
        r_wide = over("y_T", 8, TT, NE)
        chosen = over("y_T", TT, NE)
        gate = over("y_T", TT, NE)
        place = over("y_T", TT, NE)
        pick = over("gates", TT, PASS)
        spread = over("gates", TT, P)
        spread_T = over("gates", TT * P)
        got = over("gates", T)
        got_T = over("gates", 2, Q, PASS)
        silu = over("gates", P)
        hid = over("gates", P)
        hid_T = over("gates", Q, PASS)
        y_tok = over("gates", T)

        x_loaded, consts_loaded, rg_loaded, final_w_loaded = map(sem, ("x_loaded", "consts_loaded", "rg_loaded", "final_w_loaded"))
        piece_loaded = {n: sem(f"loaded_{n}") for n in list(EVEN_COLS) + list(ODD_COLS) + ["even_out", "odd_out"]}
        up_loaded = [sem(f"up_loaded_slot{s}") for s in range(SLOTS)]
        down_loaded = [sem(f"down_loaded_slot{s}") for s in range(SLOTS)]
        masks_loaded = sem("masks_loaded")
        pool_set, vector_step, scalar_step = map(sem, ("pool_set", "vector_step", "scalar_step"))
        squared = Staged(sem("squared"), 2)
        mean_set = Staged(sem("mean_set"), 1)
        rooted = Staged(sem("rooted"), 1)
        normed = Staged(sem("normed"), 2)
        turned = Staged(sem("turned"), 4)
        scaled_v = Staged(sem("scaled_v"), 2)
        scaled_a = Staged(sem("scaled_a"), 4)
        x_added = Staged(sem("x_added"), 4)
        af_ready, aq_ready, bqk_ready, low_ready, z_ready = map(sem, ("af_ready", "aq_ready", "bqk_ready", "low_ready", "z_ready"))
        sig_done, aq_kept, bqk_kept, low_kept, z_taken = map(sem, ("sig_done", "aq_kept", "bqk_kept", "low_kept", "z_taken"))
        f_ready, f_logged, key_ready = map(sem, ("f_ready", "f_logged", "key_ready"))
        z_set, z_abs, z_exped, z_logged, sums_ready = map(sem, ("z_set", "z_abs", "z_exped", "z_logged", "sums_ready"))
        lb_set, lb_exped = map(sem, ("lb_set", "lb_exped"))
        gap_ready, gap_exped, decayed = map(sem, ("gap_ready", "gap_exped", "decayed"))
        scores_ready, scores_kept = sem("scores_ready"), sem("scores_kept")
        qk_ready, qk_kept, swapped, rotated = map(sem, ("qk_ready", "qk_kept", "swapped", "rotated"))
        dx_ready, dx_kept, dg_ready, dg_kept, conv_done = map(sem, ("dx_ready", "dx_kept", "dg_ready", "dg_kept", "conv_done"))
        ret_ready, ret_kept, rg_ready, rg_exped, rg_set = map(sem, ("ret_ready", "ret_kept", "rg_ready", "rg_exped", "rg_set"))
        th_done, th_root, lam_set, lam_exped = map(sem, ("th_done", "th_root", "lam_set", "lam_exped"))
        dg_squared, dg_inner, dg_tanh, yd_ready = map(sem, ("dg_squared", "dg_inner", "dg_tanh", "yd_ready"))
        centred = sem("centred")
        proj_ready = Staged(sem("proj_ready"), 8)
        proj_kept = Staged(sem("proj_kept"), 8)
        gates_open = sem("gates_open")
        heads_ready = Staged(sem("heads_ready"), 4)
        heads_squared = Staged(sem("heads_squared"), 4)
        heads_mean = Staged(sem("heads_mean"), 1)
        heads_root = Staged(sem("heads_root"), 1)
        y_ready = Staged(sem("y_ready"), 16)
        y_turned = Staged(sem("y_turned"), 4)
        y_scaled_v = Staged(sem("y_scaled_v"), 2)
        y_scaled_a = Staged(sem("y_scaled_a"), 4)
        mix_ready = Staged(sem("mix_ready"), 4)
        logits_ready = Staged(sem("logits_ready"), 1)
        group_gap = Staged(sem("group_gap"), 1)
        group_exped = Staged(sem("group_exped"), 1)
        pair_gap = Staged(sem("pair_gap"), 1)
        pair_exped = Staged(sem("pair_exped"), 1)
        chosen_set = Staged(sem("chosen_set"), 1)
        ranks_ready = Staged(sem("ranks_ready"), 1)
        routed = Staged(sem("routed"), 2)
        picked = sem("picked")
        spread_set = sem("spread_set")
        gathered = sem("gathered")
        got_kept = sem("got_kept")
        got_turned = sem("got_turned")
        got_scaled = sem("got_scaled")
        spread_turned = sem("spread_turned")
        spread_kept = sem("spread_kept")
        up_done = sem("up_done")
        silu_done = sem("silu_done")
        hid_ready = sem("hid_ready")
        hid_turned = sem("hid_turned")
        hid_kept = sem("hid_kept")
        down_done = sem("down_done")
        y_kept = sem("y_kept")
        scattered = sem("scattered")
        experts_done = Staged(sem("experts_done"), NE)
        out_stored = sem("out_stored")

        def loads_before(slot, l):
            return l * len([e for e in range(NE) if ORDER[e % 3] == slot])

        pass_count = {}

        def over_experts(eng, l, expert, counts_ready):
            if l == 0:
                pass_count[eng.engine] = eng.alloc_register(f"passes_{eng.engine.name}")
                eng.reg_mov(pass_count[eng.engine], 0)
            n = pass_count[eng.engine]
            counts_ready()

            def one(e, slot, loads):
                tokens = eng.value_load(counts[0:1, bass.ds(e, 1)], min_val=0, max_val=T)

                def passes(body):
                    with eng.Fori(0, tokens, PASS) as base:
                        body(base, eng.snap(n, min_val=0, max_val=2 * NE * T // PASS))
                        eng.reg_add(n, n, 1)

                expert(e, slot, loads, passes)

            with eng.Fori(0, NE // 3) as i:
                for s in range(3):
                    one(3 * i + s, ORDER[s], loads_before(ORDER[s], l) + 1 + i)
            for e in range(NE // 3 * 3, NE):
                one(e, ORDER[e % 3], loads_before(ORDER[e % 3], l) + 1 + e // 3)
            return eng.snap(n, min_val=0, max_val=2 * NE * T // PASS)

        block = ctx.enter_context(nc.Block())

        @block.sync
        def _(sp_q):
            sp_q.dma_start(x[:, :, :], x_in.rearrange("o (a p) d -> p (o a) d", p=P)).then_inc(x_loaded, 16)

            def piece(name, slot, at, w_in, cols, width=512):
                dst = weights[:, slot, at:at + KC * width].rearrange("p (k c) -> p k c", k=KC)
                src = w_in[0, :, cols:cols + width].rearrange("(p k) c -> p k c", k=KC)
                sp_q.dma_start(dst, src).then_inc(piece_loaded[name], 16)

            def out_weights(name, w_out):
                dst = weights[:, 1, 0:KC * D].rearrange("p (k c) -> p k c", k=KC)
                sp_q.dma_start(dst, w_out[0].rearrange("(k p) c -> p k c", p=P)).then_inc(piece_loaded[name], 16)

            def load_expert(l, e, slot):
                up = weights[:, slot, 0:2 * PIECE].rearrange("p (k w f) -> p k w f", k=KC, w=2)
                for w, src in enumerate((moe_w1, moe_w3)):
                    sp_q.dma_start(up[:, :, w, :], src[l, bass.ds(e, 1)].rearrange("o (p k) f -> p (o k) f", k=KC)
                                   ).then_inc(up_loaded[slot], 16)
                down = weights[:, slot, 2 * PIECE:].rearrange("p (c d) -> p c d", c=Q)
                sp_q.dma_start(down, moe_w2[l, bass.ds(e, 1)].rearrange("o (c p) d -> p (o c) d", p=P)
                               ).then_inc(down_loaded[slot], 16)

            def load_experts(l):
                with sp_q.Fori(1, NE // 3) as i:
                    for s in range(3):
                        sp_q.wait_ge(*experts_done.at(l, 3 * i + (s - 2)))
                        load_expert(l, 3 * i + s, ORDER[s])
                for e in range(NE // 3 * 3, NE):
                    sp_q.wait_ge(*experts_done.at(l, e - 2))
                    load_expert(l, e, ORDER[e % 3])

            C = EVEN_COLS
            piece("a_f", 0, 0, even_w_in, C["a_f"])
            piece("a_q", 0, PIECE, even_w_in, C["a_q"])
            piece("b_low", 1, 2 * PIECE, even_w_in, C["b_low"], 16)
            piece("b_qk", 1, 0, even_w_in, C["b_qk"])
            piece("a_i", 1, PIECE, even_w_in, C["a_i"])
            sp_q.wait_ge(aq_ready, 2)
            piece("b_v", 0, 0, even_w_in, C["b_v"])
            piece("a_g", 0, PIECE, even_w_in, C["a_g"])
            piece("b_r", 0, 2 * PIECE, even_w_in, C["b_r"])
            sp_q.wait_ge(*proj_ready.at(0, 2))
            out_weights("even_out", even_w_out)
            sp_q.wait_ge(*proj_ready.at(0, 8))
            load_expert(0, 0, 0)
            sp_q.wait_ge(*y_ready.at(0, 16))
            load_expert(0, 1, 2)
            sp_q.wait_ge(*mix_ready.at(0, 4))
            load_expert(0, 2, 1)
            load_experts(0)
            C = ODD_COLS
            sp_q.wait_ge(*experts_done.at(0, NE - 2))
            piece("c_qk", 1, 0, odd_w_in, C["c_qk"])
            piece("d_x", 1, PIECE, odd_w_in, C["d_x"])
            piece("d_gate", 1, 2 * PIECE, odd_w_in, C["d_gate"])
            sp_q.wait_ge(*experts_done.at(0, NE - 1))
            piece("c_v", 0, 0, odd_w_in, C["c_v"])
            piece("c_g", 0, PIECE, odd_w_in, C["c_g"])
            sp_q.wait_ge(dg_ready, 2)
            out_weights("odd_out", odd_w_out)
            sp_q.wait_ge(*proj_ready.at(1, 4))
            load_expert(1, 0, 0)
            sp_q.wait_ge(*y_ready.at(1, 8))
            sp_q.wait_ge(yd_ready, 4)
            load_expert(1, 1, 2)
            sp_q.wait_ge(*mix_ready.at(1, 4))
            load_expert(1, 2, 1)
            load_experts(1)

        @block.gpsimd
        def _(pool):
            pool.memset(restart, 1.0).then_inc(pool_set, 1)
            pool.wait_ge(pool_set, 1)
            pool.memset(restart.rearrange("p (n t) -> p n t", t=P)[:, :, 0:1], 0.0).then_inc(pool_set, 1)
            pool.memset(zeros[:, :], 0.0).then_inc(pool_set, 1)
            pool.memset(w_rg[:, :, :, :], 0.0).then_inc(pool_set, 1)
            pool.wait_ge(pool_set, 4)
            pool.dma_start(masks_wide, masks_in).then_inc(masks_loaded, 16)
            pool.wait_ge(masks_loaded, 16)
            pool.tensor_copy(masks[:, :], masks_wide).then_inc(pool_set, 1)
            for g, w in enumerate((rglru_w_r, rglru_w_i)):
                for half in range(2):
                    pool.dma_start(w_rg[64 * half:64 * half + 64, g, :, 64 * half:64 * half + 64],
                                   w[0, half:8:2].rearrange("m d e -> d m e")).then_inc(rg_loaded, 16)

        @block.tensor
        def _(pe):
            def wait_norm(s):
                pe.wait_ge(*scaled_v.at(s, 2))
                pe.wait_ge(*scaled_a.at(s, 4))

            def turn_tokens(s):
                pe.wait_ge(*normed.at(s, 2))
                for b in range(4):
                    for k in (2 * b, 2 * b + 1):
                        for a in range(TT):
                            at = (k % 2) * T + a * P
                            ins = pe.transpose(bank[4 + b][:, at:at + P], tok[:, a, k * P:(k + 1) * P], ident)
                    ins.then_inc(turned.sem, 1)

            def by_channel(slot, at, m, width, dst, rows=P):
                for k in range(KC):
                    lhs = weights[:, slot, at + k * width + m * P:at + k * width + m * P + rows]
                    ins = pe.matmul(dst, lhs, act_T[:, k, :], start=(k == 0), stop=(k == KC - 1))
                return ins

            def by_token(slot, at, a, dst):
                for k in range(KC):
                    ins = pe.matmul(dst, act_T[:, k, a * P:(a + 1) * P], weights[:, slot, at + k * 512:at + (k + 1) * 512],
                                    start=(k == 0), stop=(k == KC - 1))
                return ins

            def turn_y(l, chunks):
                for b in range(chunks // 2):
                    for k in (2 * b, 2 * b + 1):
                        for a in range(TT):
                            at = (k % 2) * T + a * P
                            ins = pe.transpose(bank[4 + b][:, at:at + P], gates[:, a, k * P:(k + 1) * P], ident)
                    ins.then_inc(y_turned.sem, 1)

            def project_out(l, name):
                pe.wait_ge(piece_loaded[name], 16)
                for a in range(TT):
                    for h in range(2):
                        for k in range(KC):
                            at = k * D + h * 512
                            ins = pe.matmul(bank[2 * a + h][:, :], y_T[:, k, a * P:(a + 1) * P], weights[:, 1, at:at + 512],
                                            start=(k == 0), stop=(k == KC - 1))
                        ins.then_inc(mix_ready.sem, 1)

            def even_mixer():
                wait_norm(0)
                pe.wait_ge(piece_loaded["a_f"], 16)
                for m in range(4):
                    ins = by_channel(0, 0, m, 512, bank[m // 2][:, m % 2 * T:m % 2 * T + T])
                    if m % 2:
                        ins.then_inc(af_ready, 1)
                pe.wait_ge(piece_loaded["a_q"], 16)
                for m in range(4):
                    ins = by_channel(0, PIECE, m, 512, bank[2 + m // 2][:, m % 2 * T:m % 2 * T + T])
                    if m % 2:
                        ins.then_inc(aq_ready, 1)
                pe.wait_ge(piece_loaded["b_low"], 16)
                by_channel(1, 2 * PIECE, 0, 16, bank[6][0:16, 0:T], rows=16).then_inc(low_ready, 1)
                pe.wait_ge(piece_loaded["b_qk"], 16)
                for m in range(4):
                    ins = by_channel(1, 0, m, 512, bank[4 + m // 2][:, m % 2 * T:m % 2 * T + T])
                    if m % 2:
                        ins.then_inc(bqk_ready, 1)
                pe.wait_ge(low_kept, 1)
                for m in range(2):
                    ins = pe.matmul(bank[7][:, m * T:(m + 1) * T], w_up[:, m * P:(m + 1) * P], low, start=True, stop=True)
                ins.then_inc(z_ready, 1)

                groups = [(1, PIECE, "a_i"), (0, 0, "b_v"), (0, PIECE, "a_g"), (0, 2 * PIECE, "b_r")]

                def project(g):
                    slot, at, name = groups[g // 2]
                    pe.wait_ge(piece_loaded[name], 16)
                    if g < 2:
                        pe.wait_ge(bqk_kept, g + 1)
                    else:
                        pe.wait_ge(*proj_kept.at(0, g - 1))
                    by_token(slot, at, g % 2, bank[4 + g % 2][:, :]).then_inc(proj_ready.sem, 1)

                def scores(i):
                    A = decA[i % 2].rearrange("p (h t) -> p h t", h=HEADS)
                    B = decB[i % 2].rearrange("p (m t) -> p m t", m=2)
                    keysA, keysB, queriesA, queriesB = A, B, A, B
                    if i == 0:
                        keysA, queriesA = (z.rearrange("p (h t) -> p h t", h=HEADS) for z in (kA, qA))
                        keysB, queriesB = (z.rearrange("p (m t) -> p m t", m=2) for z in (kB, qB))
                        pe.wait_ge(key_ready, 1)
                        pe.wait_ge(aq_kept, 2)
                        pe.wait_ge(bqk_kept, 2)
                    else:
                        pe.wait_ge(decayed, 4 * i)
                    cross = i == len(LEVELS) + 1
                    tiles = (0,) if cross else range(TT)
                    for a in tiles:
                        if i:
                            pe.wait_ge(scores_kept, 4 * (i - 1) + a + 1)
                        for h in range(HEADS):
                            t0 = P if cross else a * P
                            ins = pe.matmul(bank[a][:, h * P:(h + 1) * P], keysA[:, h, a * P:(a + 1) * P],
                                            queriesA[:, h, t0:t0 + P], start=True, stop=True)
                        ins.then_inc(scores_ready, 1)
                    if i:
                        pe.wait_ge(scores_kept, 4 * i)
                    for a in tiles:
                        for m in range(2):
                            for parity in range(2):
                                rows = slice(64 * parity, 64 * parity + 64)
                                at = (a * 2 + m) * P
                                t0 = P if cross else a * P
                                ins = pe.matmul(bank[2 + parity][:, at:at + P], keysB[rows, m, a * P:(a + 1) * P],
                                                queriesB[rows, m, t0:t0 + P], start=True, stop=True)
                                if a == tiles[-1] and m == 1:
                                    ins.then_inc(scores_ready, 1)

                for i in range(len(LEVELS) + 2):
                    if i < 8:
                        project(i)
                    scores(i)

                SAv = SA.rearrange("p (b h t) -> p b h t", b=3, h=HEADS)
                SBv = SB.rearrange("p (q b m t) -> p q b m t", q=2, b=3, m=2)
                pe.wait_ge(scores_kept, 4 * 8 + 3)
                pe.wait_ge(*proj_kept.at(0, 8))
                for a in range(TT):
                    for grp in range(2):
                        for h in range(HEADS):
                            blocks = [(0, 0)] if a == 0 else [(2, 0), (1, 1)]
                            for j, (b, src) in enumerate(blocks):
                                S = SAv[:, b, h, :] if grp == 0 else SBv[:, h % 2, b, h // 2, :]
                                v = tok[:, src, grp * 512 + h * P:grp * 512 + (h + 1) * P]
                                ins = pe.matmul(bank[2 * a + grp][:, h * P:(h + 1) * P], S, v,
                                                start=(j == 0), stop=(j == len(blocks) - 1))
                        ins.then_inc(heads_ready.sem, 1)
                pe.wait_ge(*y_ready.at(0, 16))
                turn_y(0, 8)
                pe.wait_ge(*y_scaled_v.at(0, 2))
                pe.wait_ge(*y_scaled_a.at(0, 4))
                project_out(0, "even_out")

            def odd_mixer():
                wait_norm(2)
                pe.wait_ge(piece_loaded["c_qk"], 16)
                for m in range(4):
                    ins = by_channel(1, 0, m, 512, bank[m // 2][:, m % 2 * T:m % 2 * T + T])
                    if m % 2:
                        ins.then_inc(qk_ready, 1)
                pe.wait_ge(piece_loaded["d_x"], 16)
                for m in range(4):
                    ins = by_channel(1, PIECE, m, 512, bank[2 + m // 2][:, m % 2 * T:m % 2 * T + T])
                    if m % 2:
                        ins.then_inc(dx_ready, 1)
                pe.wait_ge(qk_kept, 2)
                for j in range(2):
                    pe.matmul(bank[4 + j][:, :], const("swap"), raw[:, j * 512:(j + 1) * 512],
                              start=True, stop=True).then_inc(swapped, 1)
                pe.wait_ge(piece_loaded["d_gate"], 16)
                for m in range(4):
                    ins = by_channel(1, 2 * PIECE, m, 512, bank[6 + m // 2][:, m % 2 * T:m % 2 * T + T])
                    if m % 2:
                        ins.then_inc(dg_ready, 1)
                rotv = rot.rearrange("p (z m t) -> p z m t", z=2, m=2)
                pe.wait_ge(rotated, 1)
                pe.wait_ge(dx_kept, 2)
                for b, (s0, t0) in enumerate(((0, 0), (P, P), (0, P))):
                    for m in range(2):
                        for parity in range(2):
                            rows = slice(64 * parity, 64 * parity + 64)
                            at = (b % 2 * 2 + m) * P
                            ins = pe.matmul(bank[(2 if b == 2 else 0) + parity][:, at:at + P], rotv[rows, 1, m, s0:s0 + P],
                                            rotv[rows, 0, m, t0:t0 + P], start=True, stop=True)
                            if b and m == 1:
                                ins.then_inc(ret_ready, 1)
                for g in range(2):
                    pe.wait_ge(piece_loaded["c_v"], 16)
                    pe.wait_ge(rotated, 1)
                    by_token(0, 0, g, bank[4 + g][:, :]).then_inc(proj_ready.sem, 1)
                pe.wait_ge(rg_loaded, 64)
                pe.wait_ge(conv_done, 4)
                pe.wait_ge(ret_kept, 4)
                pe.wait_ge(dg_kept, 2)
                for g in range(2):
                    for m in range(4):
                        ins = pe.matmul(bank[(2, 6)[g] + m // 2][:, m % 2 * T:m % 2 * T + T], w_rg[:, g, m, :],
                                        xc[:, m * T:(m + 1) * T], start=True, stop=True)
                    ins.then_inc(rg_ready, 1)
                for g in range(2):
                    pe.wait_ge(piece_loaded["c_g"], 16)
                    pe.wait_ge(*proj_kept.at(1, g + 1))
                    by_token(0, PIECE, g, bank[4 + g][:, :]).then_inc(proj_ready.sem, 1)
                SCv = SC.rearrange("p (q b m t) -> p q b m t", q=2, b=3, m=2)
                for a in range(TT):
                    for h in range(HEADS):
                        blocks = [(0, 0)] if a == 0 else [(2, 0), (1, 1)]
                        for j, (b, src) in enumerate(blocks):
                            ins = pe.matmul(bank[a][:, h * P:(h + 1) * P], SCv[:, h % 2, b, h // 2, :],
                                            tok[:, src, h * P:(h + 1) * P], start=(j == 0), stop=(j == len(blocks) - 1))
                    ins.then_inc(heads_ready.sem, 1)
                pe.wait_ge(*y_ready.at(1, 8))
                pe.wait_ge(*proj_kept.at(1, 4))
                turn_y(1, 4)
                pe.wait_ge(*y_scaled_v.at(1, 1))
                pe.wait_ge(*y_scaled_a.at(1, 2))
                pe.wait_ge(yd_ready, 4)
                project_out(1, "odd_out")

            def route(l):
                wait_norm(2 * l + 1)
                wg = vec("w_group", l * 32, l * 32 + 32).rearrange("p (k g) -> p k g", k=KC)
                we = vec("w_expert", l * 256, l * 256 + 256).rearrange("p (k g) -> p k g", k=KC)
                for a in range(TT):
                    for w, at, width in ((wg, 0, NG), (we, 32, NE)):
                        for k in range(KC):
                            ins = pe.matmul(bank[a][:, at:at + width], act_T[:, k, a * P:(a + 1) * P], w[:, k, :],
                                            start=(k == 0), stop=(k == KC - 1))
                ins.then_inc(logits_ready.sem, 1)
                pe.wait_ge(*chosen_set.at(l, 1))
                pe.matmul(bank[2][:, 0:NE], const("before"), chosen[:, 0, :], start=True, stop=True)
                pe.matmul(bank[2][:, NE:2 * NE], const("before"), chosen[:, 1, :], start=True, stop=False)
                pe.matmul(bank[2][:, NE:2 * NE], const("ones"), chosen[:, 0, :], start=False, stop=True)
                pe.matmul(bank[2][:, 64:64 + NE], const("ones"), chosen[:, 0, :], start=True, stop=False)
                pe.matmul(bank[2][:, 64:64 + NE], const("ones"), chosen[:, 1, :], start=False, stop=True).then_inc(ranks_ready.sem, 1)

            def experts(l):
                def start():
                    pe.wait_ge(*routed.at(l, 2))
                    for q in range(Q):
                        pe.matmul(bank[q][:, :], zeros[:, 0:P], zeros[:, :], start=True, stop=True, skip_group_check=True)

                def expert(e, slot, loads, passes):
                    up = weights[:, slot, 0:2 * PIECE].rearrange("p (k w f) -> p k w f", k=KC, w=2)
                    down = weights[:, slot, 2 * PIECE:].rearrange("p (c d) -> p c d", c=Q)

                    def body(base, n):
                        pe.wait_ge(picked, 2 * n + 2)
                        for a in range(TT):
                            for q in range(Q):
                                ins = pe.matmul(bank[4][PASS * q:PASS * (q + 1), 0:T], pick[:, a, :], tok[:, a, q * T:(q + 1) * T],
                                                start=(a == 0), stop=(a == TT - 1), tile_position=(0, PASS * q), skip_group_check=True)
                        ins.then_inc(gathered, 1)
                        pe.wait_ge(spread_set, 2 * n + 2)
                        for a in range(TT):
                            ins = pe.transpose(bank[7][:, T + a * P:T + (a + 1) * P], spread[:, a, :], ident)
                        ins.then_inc(spread_turned, 1)
                        pe.wait_ge(got_kept, n + 1)
                        for s in range(2):
                            ins = pe.transpose(bank[5][:, s * P:(s + 1) * P], got[:, s * P:(s + 1) * P], ident)
                        ins.then_inc(got_turned, 1)
                        pe.wait_ge(got_scaled, n + 1)
                        pe.wait_ge(up_loaded[slot], 32 * loads)
                        for k in range(KC):
                            for j in range(Q):
                                ins = pe.matmul(bank[6][PASS * j:PASS * (j + 1), 0:T], got_T[:, k % 2, k // 2, :],
                                                up[:, k, :, j * P:(j + 1) * P], start=(k == 0), stop=(k == KC - 1),
                                                tile_position=(0, PASS * j), skip_group_check=True)
                        ins.then_inc(up_done, 1)
                        pe.wait_ge(hid_ready, n + 1)
                        pe.wait_ge(spread_kept, n + 1)
                        pe.transpose(bank[7][:, 0:P], hid[:, :], ident).then_inc(hid_turned, 1)
                        pe.wait_ge(hid_kept, n + 1)
                        pe.wait_ge(down_loaded[slot], 16 * loads)
                        for c in range(Q):
                            for q in range(Q):
                                ins = pe.matmul(bank[7][PASS * q:PASS * (q + 1), T:2 * T], hid_T[:, c, :],
                                                down[:, c, q * T:(q + 1) * T], start=(c == 0), stop=(c == Q - 1),
                                                tile_position=(0, PASS * q), skip_group_check=True)
                        ins.then_inc(down_done, 1)
                        pe.wait_ge(y_kept, n + 1)
                        for a in range(TT):
                            for q in range(Q):
                                rows = slice(PASS * q, PASS * (q + 1))
                                ins = pe.matmul(bank[q][:, a * T:(a + 1) * T], spread_T[rows, a * P:(a + 1) * P], y_tok[rows, :],
                                                start=False, stop=True, tile_position=(PASS * q, 0), skip_group_check=True)
                        ins.then_inc(scattered, 1)

                    passes(body)

                over_experts(pe, l, expert, start)

            pe.wait_ge(consts_loaded, 48)
            pe.wait_ge(pool_set, 4)
            turn_tokens(0)
            even_mixer()
            turn_tokens(1)
            route(0)
            experts(0)
            turn_tokens(2)
            odd_mixer()
            turn_tokens(3)
            route(1)
            experts(1)

        @block.scalar
        def _(act):
            steps = [0]

            def link(ins):
                steps[0] += 1
                ins.then_inc(scalar_step, 1)
                act.wait_ge(scalar_step, steps[0])

            def f(out_, in_, fn, **kw):
                return act.activation(out_, in_, fn, **kw)

            def norm(s):
                for a in range(TT):
                    f(tok[:, a, :], x[:, a, :], ACT.Square, accum_out=sums[:, a:a + 1]).then_inc(squared.sem, 1)
                act.wait_ge(*mean_set.at(s, 1))
                f(root[:, :], sums[:, :], ACT.Sqrt).then_inc(rooted.sem, 1)

            def norm_scale(s, w):
                for b in (2, 3):
                    act.wait_ge(*turned.at(s, b + 1))
                    for k in (2 * b, 2 * b + 1):
                        f(act_T[:, k, :], bank[4 + b][:, k % 2 * T:k % 2 * T + T], ACT.Copy,
                          scale=w[:, k:k + 1]).then_inc(scaled_a.sem, 1)

            def y_scale(l, banks, w):
                for b in banks:
                    act.wait_ge(*y_turned.at(l, b + 1))
                    for k in (2 * b, 2 * b + 1):
                        f(y_T[:, k, :], bank[4 + b][:, k % 2 * T:k % 2 * T + T], ACT.Copy,
                          scale=w[:, k:k + 1]).then_inc(y_scaled_a.sem, 1)

            def even_mixer():
                for b in range(2):
                    act.wait_ge(af_ready, b + 1)
                    f(kA[:, b * 512:(b + 1) * 512], bank[b][:, :], ACT.Sigmoid).then_inc(sig_done, 1)
                for b in range(2):
                    act.wait_ge(aq_ready, b + 1)
                    act.copy(qA[:, b * 512:(b + 1) * 512], bank[2 + b][:, :]).then_inc(aq_kept, 1)
                act.wait_ge(low_ready, 1)
                act.copy(low, bank[6][0:16, 0:T]).then_inc(low_kept, 1)
                act.wait_ge(f_ready, 4)
                f(decA[0], kA, ACT.Ln).then_inc(f_logged, 1)
                act.wait_ge(bqk_ready, 1)
                f(qB, bank[4][:, :], ACT.Copy, scale=64.0 ** -0.5).then_inc(bqk_kept, 1)
                act.wait_ge(bqk_ready, 2)
                act.copy(kB, bank[5][:, :]).then_inc(bqk_kept, 1)
                act.wait_ge(z_set, 2)
                f(decB[0], bB, ACT.Abs).then_inc(z_abs, 1)
                act.wait_ge(z_abs, 1)
                f(decB[0], decB[0], ACT.Exp, scale=-1.0).then_inc(z_exped, 1)
                act.wait_ge(z_exped, 1)
                f(decB[0], decB[0], ACT.Ln, bias=1.0).then_inc(z_logged, 1)

                def keep(g):
                    act.wait_ge(*proj_ready.at(0, g + 1))
                    dst = (tok, tok, gates, gates)[g // 2]
                    at = (0, 512, 0, 512)[g // 2]
                    act.copy(dst[:, g % 2, at:at + 512], bank[4 + g % 2][:, :]).then_inc(proj_kept.sem, 1)

                keep(0)
                for i in range(1, len(LEVELS) + 2):
                    h = (LEVELS + (P,))[i - 1]
                    for buf, b_run, j in ((decA[i % 2], bA, 1), (decB[i % 2], bB, 2)):
                        act.wait_ge(gap_ready, 2 * (i - 1) + j)
                        v = buf.rearrange("p (n c) -> p n c", c=2 * h)
                        if h == P:
                            first, scale_first = v[:, :, 0:h], 1.0
                            second = b_run.rearrange("p (n c) -> p n c", c=2 * h)[:, :, h:]
                        else:
                            first, scale_first, second = v[:, :, 0:h], -1.0, v[:, :, h:]
                        f(v[:, :, h:], second, ACT.Exp).then_inc(gap_exped, 1)
                        f(v[:, :, 0:h], first, ACT.Exp, scale=scale_first).then_inc(gap_exped, 1)
                    if i < 8:
                        keep(i)
                act.wait_ge(*proj_kept.at(0, 8))
                for a in range(TT):
                    f(gates[:, a, :], gates[:, a, :], ACT.Silu).then_inc(gates_open, 1)
                act.wait_ge(scores_ready, 35)
                act.wait_ge(decayed, 32)
                for b in range(4):
                    act.wait_ge(*heads_ready.at(0, b + 1))
                    f(work(4608 + 512 * b, 512), bank[b][:, :], ACT.Square).then_inc(heads_squared.sem, 1)
                act.wait_ge(*heads_mean.at(0, 1))
                f(head_r[:, :], head_ss[:, :], ACT.Sqrt).then_inc(heads_root.sem, 1)
                y_scale(0, (2, 3), vec("even_w"))

            def odd_mixer():
                for b in range(2):
                    act.wait_ge(qk_ready, b + 1)
                    act.copy(raw[:, b * 512:(b + 1) * 512], bank[b][:, :]).then_inc(qk_kept, 1)
                for b in range(2):
                    act.wait_ge(dx_ready, b + 1)
                    act.copy(dx[:, 2 * b:2 * b + 2, 3:3 + T],
                             bank[2 + b][:, :].rearrange("p (m t) -> p m t", m=2)).then_inc(dx_kept, 1)
                for b in range(2):
                    act.wait_ge(dg_ready, b + 1)
                    act.copy(dg[:, b * 512:(b + 1) * 512], bank[6 + b][:, :]).then_inc(dg_kept, 1)
                act.wait_ge(dg_kept, 2)
                f(gl, dg, ACT.Square).then_inc(dg_squared, 1)
                for g in range(2):
                    act.wait_ge(*proj_ready.at(1, g + 1))
                    act.copy(tok[:, g, 0:512], bank[4 + g][:, :]).then_inc(proj_kept.sem, 1)
                for g, dst in enumerate((rr, ii)):
                    act.wait_ge(rg_ready, g + 1)
                    for m in range(4):
                        f(dst[:, m * T:(m + 1) * T], bank[(2, 6)[g] + m // 2][:, m % 2 * T:m % 2 * T + T], ACT.Exp,
                          scale=-1.0, bias=nb[:, g, m:m + 1]).then_inc(rg_exped, 1)
                act.wait_ge(dg_inner, 1)
                f(gl, gl, ACT.Tanh, scale=(2.0 / np.pi) ** 0.5).then_inc(dg_tanh, 1)
                act.wait_ge(rg_set, 1)
                for m in range(4):
                    f(th[:, m * T:(m + 1) * T], rr[:, m * T:(m + 1) * T], ACT.Tanh, scale=sp[:, 0, m:m + 1]).then_inc(th_done, 1)
                act.wait_ge(th_done, 4)
                act.wait_ge(rg_set, 2)
                f(rr, th, ACT.Sqrt).then_inc(th_root, 1)
                for g in range(2):
                    act.wait_ge(*proj_ready.at(1, g + 3))
                    f(gates[:, g, 0:512], bank[4 + g][:, :], ACT.Silu).then_inc(proj_kept.sem, 1)
                for a in range(TT):
                    act.wait_ge(centred, a + 1)
                    f(tmp[:, 0:512] if a == 0 else tmp[:, 512:1024], raw[:, a * 512:(a + 1) * 512], ACT.Square).then_inc(heads_squared.sem, 1)
                act.wait_ge(*heads_mean.at(1, 1))
                f(head_r[:, 0:8], head_ss[:, 0:8], ACT.Sqrt).then_inc(heads_root.sem, 1)
                y_scale(1, (1,), vec("ret_w"))

            def route(l):
                gd = r_small[:, :, 1, :]
                act.wait_ge(*group_gap.at(l, 1))
                f(r_small[:, :, 2, :], gd, ACT.Exp).then_inc(group_exped.sem, 1)
                act.wait_ge(*pair_gap.at(l, 1))
                f(root[:, :], scale[:, :], ACT.Exp).then_inc(pair_exped.sem, 1)

            def experts(l):
                def expert(e, slot, loads, passes):
                    def body(base, n):
                        act.wait_ge(gathered, n + 1)
                        act.copy(got[:, :], bank[4][:, 0:T]).then_inc(got_kept, 1)
                        act.wait_ge(spread_turned, n + 1)
                        act.copy(spread_T[:, :], bank[7][:, T:2 * T]).then_inc(spread_kept, 1)
                        act.wait_ge(up_done, n + 1)
                        f(silu[:, :], bank[6][:, 0:P], ACT.Silu).then_inc(silu_done, 1)
                        act.wait_ge(down_done, n + 1)
                        act.copy(y_tok[:, :], bank[7][:, T:2 * T]).then_inc(y_kept, 1)

                    passes(body)
                    act.sem_inc(experts_done.sem, 1)

                over_experts(act, l, expert, lambda: act.wait_ge(*routed.at(l, 2)))

            act.dma_start(consts[:, :], shape_consts).then_inc(consts_loaded, 16)
            act.dma_start(vecs[:, :], vectors).then_inc(consts_loaded, 16)
            act.dma_start(w_up, gla_w_up[0]).then_inc(consts_loaded, 16)
            act.wait_ge(x_loaded, 16)
            norm(0)
            act.wait_ge(consts_loaded, 48)
            act.wait_ge(lb_set, 1)
            f(lb_e[:, :, :], lb_t[:, :, :], ACT.Exp).then_inc(lb_exped, 1)
            act.wait_ge(lam_set, 1)
            f(sp[:, 1, :], sp[:, 0, :], ACT.Exp, scale=-1.0).then_inc(lam_exped, 1)
            norm_scale(0, vec("norm_mix", 0, 8))
            even_mixer()
            act.wait_ge(*x_added.at(0, 4))
            norm(1)
            norm_scale(1, vec("norm_ffn", 0, 8))
            route(0)
            experts(0)
            act.wait_ge(*x_added.at(1, 4))
            norm(2)
            norm_scale(2, vec("norm_mix", 8, 16))
            odd_mixer()
            act.wait_ge(*x_added.at(2, 4))
            norm(3)
            norm_scale(3, vec("norm_ffn", 8, 16))
            route(1)
            experts(1)
            act.wait_ge(*x_added.at(3, 4))
            act.dma_start(gates[:, 0, :], norm_final.rearrange("(o d) -> o d", o=1).to_broadcast([P, D])).then_inc(final_w_loaded, 16)
            norm(4)
            for a in range(TT):
                act.wait_ge(*normed.at(4, a + 1))
                act.dma_start(out[0, a * P:(a + 1) * P, :], tok[:, a, :]).then_inc(out_stored, 16)
            act.wait_ge(out_stored, 32)

        @block.vector
        def _(dve):
            steps = [0]

            def mark(ins):
                steps[0] += 1
                ins.then_inc(vector_step, 1)

            def link(ins):
                mark(ins)
                dve.wait_ge(vector_step, steps[0])

            ts, stt, tt = dve.tensor_scalar, dve.scalar_tensor_tensor, dve.tensor_tensor

            def norm(s):
                dve.wait_ge(*squared.at(s, 2))
                ts(sums[:, :], sums[:, :], 1.0 / D, EPS, ALU.mult, ALU.add).then_inc(mean_set.sem, 1)
                dve.wait_ge(*rooted.at(s, 1))
                link(dve.reciprocal(scale[:, :], root[:, :]))

            def norm_tokens(s, w):
                norm(s)
                for a in range(TT):
                    ts(tok[:, a, :].rearrange("p (k c) -> p c k", k=KC), x[:, a, :].rearrange("p (c k) -> p c k", k=KC),
                       scale[:, a:a + 1], None, ALU.mult).then_inc(normed.sem, 1)
                for b in (0, 1):
                    dve.wait_ge(*turned.at(s, b + 1))
                    tt(act_T[:, 2 * b:2 * b + 2, :], bank[4 + b][:, :].rearrange("p (k t) -> p k t", k=2),
                       w[:, 2 * b:2 * b + 2].unsqueeze(2).to_broadcast([P, 2, T]), ALU.mult).then_inc(scaled_v.sem, 1)

            def y_scale(l, banks, w):
                for b in banks:
                    dve.wait_ge(*y_turned.at(l, b + 1))
                    tt(y_T[:, 2 * b:2 * b + 2, :], bank[4 + b][:, :].rearrange("p (k t) -> p k t", k=2),
                       w[:, 2 * b:2 * b + 2].unsqueeze(2).to_broadcast([P, 2, T]), ALU.mult).then_inc(y_scaled_v.sem, 1)

            def add_mix(l):
                for a in range(TT):
                    for h in range(2):
                        dve.wait_ge(*mix_ready.at(l, 2 * a + h + 1))
                        tt(x[:, a, h * 512:(h + 1) * 512], x[:, a, h * 512:(h + 1) * 512], bank[2 * a + h][:, :],
                           ALU.add).then_inc(x_added.sem, 1)

            def lower_bound():
                lb = vec("lb").rearrange("p (r h) -> p r h", r=3)
                link(dve.tensor_reduce(lb_e[:, 0, :], lb.rearrange("p r h -> p h r"), AX.X, ALU.max))
                tt(lb_t[:, :, :], lb, lb_e[:, 0:1, :].to_broadcast([P, 3, 4]), ALU.subtract).then_inc(lb_set, 1)
                dve.wait_ge(lb_exped, 1)
                link(dve.tensor_reduce(lb_t[:, 2, :], lb_e[:, :, :].rearrange("p r h -> p h r"), AX.X, ALU.add))
                link(dve.reciprocal(lb_t[:, 2, :], lb_t[:, 2, :]))
                link(tt(lb_t[:, 0, :], lb_e[:, 0, :], lb_t[:, 2, :], ALU.mult))
                link(ts(lb_t[:, 1, :], lb_t[:, 0, :], -1.0, 1.0, ALU.mult, ALU.add))

            def softplus():
                lam = vec("lam")
                link(ts(sp[:, 2, :], lam, -1.0, None, ALU.mult))
                tt(sp[:, 0, :], lam, sp[:, 2, :], ALU.max).then_inc(lam_set, 1)
                dve.wait_ge(lam_exped, 1)
                link(ts(sp[:, 3, :], sp[:, 1, :], 2.0, None, ALU.add))
                link(dve.reciprocal(sp[:, 3, :], sp[:, 3, :]))
                link(tt(sp[:, 3, :], sp[:, 1, :], sp[:, 3, :], ALU.mult))
                link(tt(sp[:, 4, :], sp[:, 3, :], sp[:, 3, :], ALU.mult))
                link(ts(sp[:, 5, :], sp[:, 4, :], 1.0 / 15, 1.0 / 13, ALU.mult, ALU.add))
                for n in (11, 9, 7, 5, 3, 1):
                    link(tt(sp[:, 5, :], sp[:, 5, :], sp[:, 4, :], ALU.mult))
                    link(ts(sp[:, 5, :], sp[:, 5, :], 1.0 / n, None, ALU.add))
                link(tt(sp[:, 5, :], sp[:, 5, :], sp[:, 3, :], ALU.mult))
                link(ts(sp[:, 2, :], sp[:, 2, :], 0.0, None, ALU.max))
                link(stt(sp[:, 0, :], sp[:, 5, :], 2.0, sp[:, 2, :], ALU.mult, ALU.add))
                link(ts(sp[:, 0, :], sp[:, 0, :], RG_C / 2, None, ALU.mult))
                for g, name in enumerate(("b_r", "b_i")):
                    link(ts(nb[:, g, :], vec(name), -1.0, None, ALU.mult))

            def even_mixer():
                dve.wait_ge(sig_done, 2)
                for h in range(HEADS):
                    ts(kA[:, h * T:(h + 1) * T], kA[:, h * T:(h + 1) * T], lb_t[:, 1, h:h + 1], lb_t[:, 0, h:h + 1],
                       ALU.mult, ALU.add).then_inc(f_ready, 1)
                dve.wait_ge(f_logged, 1)
                ts(kA, kA, -1.0, 1.0, ALU.mult, ALU.add).then_inc(key_ready, 1)
                dve.wait_ge(pool_set, 5)
                mark(dve.tensor_tensor_scan(bA, restart, decA[0], 0.0, ALU.mult, ALU.add))
                dve.wait_ge(z_ready, 1)
                for m in range(2):
                    ts(bB[:, m * T:(m + 1) * T], bank[7][:, m * T:(m + 1) * T], vec("gla_b", m, m + 1), None, ALU.add).then_inc(z_set, 1)
                dve.wait_ge(z_logged, 1)
                dve.wait_ge(z_set, 2)
                link(stt(decB[0], bB, 0.0, decB[0], ALU.min, ALU.subtract))
                link(ts(decB[0], decB[0], 1.0 / 16.0, None, ALU.mult))
                link(dve.tensor_tensor_scan(bB, restart[:, 0:512], decB[0], 0.0, ALU.mult, ALU.add))

                maskv = masks[:, :].rearrange("p (l t) -> p l t", l=len(LEVELS))
                SBp = [SB[:, q * 768:(q + 1) * 768] for q in range(2)]

                def keep(i):
                    if i <= len(LEVELS):
                        dsts = [SA[:, 0:512], SA[:, 512:1024], SBp[0][:, 0:512], SBp[1][:, 0:512]]
                        for j, dst in enumerate(dsts):
                            dve.wait_ge(scores_ready, 4 * i + j + 1)
                            if i:
                                dve.wait_ge(scores_kept, 4 * (i - 1) + j + 1)
                            src = bank[j][:, :].rearrange("p (n t) -> p n t", n=4)
                            dst = dst.rearrange("p (n t) -> p n t", n=4)
                            if i == 0:
                                ins = tt(dst, src, ident.unsqueeze(1).to_broadcast([P, 4, P]), ALU.mult)
                            else:
                                ins = dve.copy_predicated(dst, maskv[:, i - 1:i, :].to_broadcast([P, 4, P]), src)
                            ins.then_inc(scores_kept, 1)
                    else:
                        for j, (dst, src) in enumerate(((SA[:, 1024:1536], bank[0][:, :]), (SBp[0][:, 512:768], bank[2][:, 0:256]),
                                                        (SBp[1][:, 512:768], bank[3][:, 0:256]))):
                            dve.wait_ge(scores_ready, 4 * i + j + 1)
                            dve.tensor_copy(dst, src).then_inc(scores_kept, 1)

                for i in range(1, len(LEVELS) + 2):
                    h = (LEVELS + (P,))[i - 1]
                    if i >= 3:
                        dve.wait_ge(scores_ready, 4 * (i - 1))
                    for buf, b_run in ((decA[i % 2], bA), (decB[i % 2], bB)):
                        v, bv = (z.rearrange("p (n c) -> p n c", c=2 * h) for z in (buf, b_run))
                        n = v.shape[1]
                        border = bv[:, :, h - 1:h]
                        if h == P:
                            ins = tt(v[:, :, 0:h], border.to_broadcast([P, n, h]), bv[:, :, 0:h], ALU.subtract)
                        else:
                            ins = tt(v, bv, border.to_broadcast([P, n, 2 * h]), ALU.subtract)
                        ins.then_inc(gap_ready, 1)
                    keep(i - 1)
                    for g, (buf, k_, q_) in enumerate(((decA[i % 2], kA, qA), (decB[i % 2], kB, qB))):
                        if i == 1:
                            dve.wait_ge(aq_kept, 2)
                            dve.wait_ge(bqk_kept, 2)
                        v, kv, qv = (z.rearrange("p (n c) -> p n c", c=2 * h) for z in (buf, k_, q_))
                        dve.wait_ge(gap_exped, 4 * (i - 1) + 2 * g + 2)
                        tt(v[:, :, h:], v[:, :, h:], qv[:, :, h:], ALU.mult).then_inc(decayed, 1)
                        tt(v[:, :, 0:h], v[:, :, 0:h], kv[:, :, 0:h], ALU.mult).then_inc(decayed, 1)
                keep(len(LEVELS) + 1)

                for b in range(4):
                    dve.wait_ge(*heads_squared.at(0, b + 1))
                    ins = dve.tensor_reduce(head_ss[:, 4 * b:4 * b + 4],
                                            work(4608 + 512 * b, 512).rearrange("p (h c) -> p h c", h=HEADS), AX.X, ALU.add)
                    mark(ins)
                dve.wait_ge(vector_step, steps[0])
                ts(head_ss[:, :], head_ss[:, :], 1.0 / P, EPS, ALU.mult, ALU.add).then_inc(heads_mean.sem, 1)
                dve.wait_ge(*heads_root.at(0, 1))
                link(dve.reciprocal(head_r[:, :], head_r[:, :]))
                dve.wait_ge(gates_open, 2)
                for a in range(TT):
                    for g in range(8):
                        y = gates[:, a, g * P:(g + 1) * P]
                        b = 2 * a + g // 4
                        stt(y, bank[b][:, g % 4 * P:(g % 4 + 1) * P], head_r[:, 4 * b + g % 4:4 * b + g % 4 + 1], y,
                            ALU.mult, ALU.mult).then_inc(y_ready.sem, 1)
                y_scale(0, (0, 1), vec("even_w"))
                add_mix(0)

            def odd_mixer():
                mark(dve.memset(dx[:, :, 0:3], 0.0))
                dve.wait_ge(qk_kept, 2)
                tables = const("rope").rearrange("p (w z t) -> p w z t", w=2, z=2)

                def table(w):
                    return tables[:, w].unsqueeze(2).to_broadcast([P, 2, 2, T])

                tmpv, rawv, rotv = (z.rearrange("p (z m t) -> p z m t", z=2, m=2) for z in (tmp, raw, rot))
                mark(tt(tmpv, rawv, table(0), ALU.mult))
                dve.wait_ge(swapped, 2)
                for z in range(2):
                    mark(tt(rotv[:, z], bank[4 + z][:, :].rearrange("p (m t) -> p m t", m=2),
                            tables[:, 1, z:z + 1].to_broadcast([P, 2, T]), ALU.mult))
                dve.wait_ge(vector_step, steps[0])
                tt(rot, rot, tmp, ALU.add).then_inc(rotated, 1)
                dve.wait_ge(dx_kept, 2)
                for m in range(4):
                    o = xc[:, m * T:(m + 1) * T]
                    link(ts(o, dx[:, m, 0:T], vec("conv_w", m, m + 1), vec("conv_b", m, m + 1), ALU.mult, ALU.add))
                    for j in range(1, CONV):
                        ins = stt(o, dx[:, m, j:j + T], vec("conv_w", 4 * j + m, 4 * j + m + 1), o, ALU.mult, ALU.add)
                        if j < CONV - 1:
                            link(ins)
                        else:
                            ins.then_inc(conv_done, 1)
                decay = const("decay").rearrange("p (q c) -> p q c", q=2)
                SCq = SC.rearrange("p (q c) -> p q c", q=2)
                for j, (q, a, b, bk) in enumerate(((0, 0, 512, 0), (1, 0, 512, 1), (0, 512, 768, 2), (1, 512, 768, 3))):
                    dve.wait_ge(ret_ready, j + 1)
                    tt(SCq[:, q, a:b], bank[bk][:, 0:b - a], decay[:, q, a:b], ALU.mult).then_inc(ret_kept, 1)
                dve.wait_ge(dg_squared, 1)
                link(ts(gl, gl, 0.044715, 1.0, ALU.mult, ALU.add))
                tt(gl, gl, dg, ALU.mult).then_inc(dg_inner, 1)
                dve.wait_ge(rg_exped, 4)
                link(ts(rr, rr, 1.0, None, ALU.add))
                dve.reciprocal(rr, rr).then_inc(rg_set, 1)
                dve.wait_ge(rg_exped, 8)
                link(ts(ii, ii, 1.0, None, ALU.add))
                link(dve.reciprocal(ii, ii))
                dve.wait_ge(conv_done, 4)
                link(tt(xc, xc, ii, ALU.mult))
                dve.wait_ge(dg_tanh, 1)
                link(stt(gl, gl, 1.0, dg, ALU.add, ALU.mult))
                dve.wait_ge(th_done, 4)
                ts(ii, th, 1.0, None, ALU.add).then_inc(rg_set, 1)
                dve.wait_ge(rg_set, 2)
                link(dve.reciprocal(ii, ii))
                dve.wait_ge(th_root, 1)
                link(ts(th, th, -1.0, 1.0, ALU.mult, ALU.add))
                mark(tt(th, th, ii, ALU.mult))
                link(stt(rr, rr, 2.0, ii, ALU.mult, ALU.mult))
                link(tt(xc, xc, rr, ALU.mult))
                for m in range(4):
                    part = slice(m * T, (m + 1) * T)
                    mark(dve.tensor_tensor_scan(ii[:, part], th[:, part], xc[:, part], 0.0, ALU.mult, ALU.add))
                dve.wait_ge(vector_step, steps[0])
                for m in range(4):
                    part = slice(m * T, (m + 1) * T)
                    stt(y_T[:, 4 + m, :], ii[:, part], 0.5, gl[:, part], ALU.mult, ALU.mult).then_inc(yd_ready, 1)
                for a in range(TT):
                    dve.wait_ge(*heads_ready.at(1, a + 1))
                    hv = bank[a][:, :].rearrange("p (h c) -> p h c", h=HEADS)
                    mean = head_m[:, 4 * a:4 * a + 4]
                    link(dve.tensor_reduce(mean, hv, AX.X, ALU.add))
                    link(ts(mean, mean, 1.0 / P, None, ALU.mult))
                    tt(raw[:, a * 512:(a + 1) * 512].rearrange("p (h c) -> p h c", h=HEADS), hv,
                       mean.unsqueeze(2).to_broadcast([P, HEADS, P]), ALU.subtract).then_inc(centred, 1)
                for a in range(TT):
                    dve.wait_ge(*heads_squared.at(1, a + 1))
                    mark(dve.tensor_reduce(head_ss[:, 4 * a:4 * a + 4],
                                           tmp[:, a * 512:(a + 1) * 512].rearrange("p (h c) -> p h c", h=HEADS), AX.X, ALU.add))
                dve.wait_ge(vector_step, steps[0])
                ts(head_ss[:, 0:8], head_ss[:, 0:8], 1.0 / P, EPS, ALU.mult, ALU.add).then_inc(heads_mean.sem, 1)
                dve.wait_ge(*heads_root.at(1, 1))
                link(dve.reciprocal(head_r[:, 0:8], head_r[:, 0:8]))
                dve.wait_ge(*proj_kept.at(1, 4))
                for a in range(TT):
                    for h in range(HEADS):
                        y = gates[:, a, h * P:(h + 1) * P]
                        stt(y, raw[:, a * 512 + h * P:a * 512 + (h + 1) * P], head_r[:, 4 * a + h:4 * a + h + 1], y,
                            ALU.mult, ALU.mult).then_inc(y_ready.sem, 1)
                y_scale(1, (0,), vec("ret_w"))
                add_mix(1)

            def route(l):
                small = [r_small[:, :, j, :] for j in range(8)]
                g, gap, e4, eq, pen = small[0], small[1], small[2], small[3], small[4]
                wide = [r_wide[:, j] for j in range(8)]
                lm, eq1, first, second, lm2 = wide[0], wide[1], wide[2], wide[3], wide[4]
                col = [r_wide[:, 5, :, j:j + 1] for j in range(8)]
                dve.wait_ge(*logits_ready.at(l, 1))
                for a in range(TT):
                    mark(tt(g[:, a], bank[a][:, 0:NG], vec("b_group", l * NG, (l + 1) * NG), ALU.add))
                    mark(tt(lm[:, a], bank[a][:, 32:32 + NE], vec("b_expert", l * NE, (l + 1) * NE), ALU.add))
                dve.wait_ge(vector_step, steps[0])

                def one_hot(dst, values, top, ramp, n):
                    link(dve.tensor_reduce(top, values, AX.X, ALU.max))
                    link(tt(dst, values, top.to_broadcast([P, TT, n]), ALU.is_equal))
                    link(tt(dst, dst, ramp.unsqueeze(1).to_broadcast([P, TT, n]), ALU.mult))
                    link(dve.tensor_reduce(col[7], dst, AX.X, ALU.max))
                    link(tt(dst, dst, col[7].to_broadcast([P, TT, n]), ALU.is_equal))

                one_hot(eq, g, col[0], const("down4"), NG)
                tt(gap, g, col[0].to_broadcast([P, TT, NG]), ALU.subtract).then_inc(group_gap.sem, 1)
                link(ts(pen, eq, -1.0, BIG1, ALU.add, ALU.mult))
                for a in range(TT):
                    v = lm[:, a].rearrange("p (g e) -> p g e", g=NG)
                    mark(tt(v, v, pen[:, a].unsqueeze(2).to_broadcast([P, NG, NE_G]), ALU.add))
                dve.wait_ge(vector_step, steps[0])
                one_hot(first, lm, col[1], const("down32"), NE)
                link(stt(lm2, first, -BIG2, lm, ALU.mult, ALU.add))
                one_hot(second, lm2, col[2], const("down32"), NE)
                tt(chosen[:, :, :], first, second, ALU.add).then_inc(chosen_set.sem, 1)
                tt(scale[:, :].unsqueeze(2), col[2], col[1], ALU.subtract).then_inc(pair_gap.sem, 1)
                dve.wait_ge(*group_exped.at(l, 1))
                link(dve.tensor_reduce(col[3], e4, AX.X, ALU.add))
                dve.wait_ge(*pair_exped.at(l, 1))
                link(ts(col[4], root[:, :].unsqueeze(2), 1.0, None, ALU.add))
                link(tt(col[3], col[3], col[4], ALU.mult))
                link(dve.reciprocal(col[3], col[3]))
                link(tt(col[4], root[:, :].unsqueeze(2), col[3], ALU.mult))
                mark(tt(first, first, col[3].to_broadcast([P, TT, NE]), ALU.mult))
                link(tt(second, second, col[4].to_broadcast([P, TT, NE]), ALU.mult))
                link(tt(gate[:, :, :], first, second, ALU.add))
                dve.wait_ge(*ranks_ready.at(l, 1))
                dve.wait_ge(*chosen_set.at(l, 1))
                dve.tensor_copy(counts[0:1, :], bank[2][0:1, 64:64 + NE]).then_inc(routed.sem, 1)
                stt(place[:, :, :], bank[2][:, 0:2 * NE].rearrange("p (a e) -> p a e", a=TT), 1.0, chosen[:, :, :],
                    ALU.add, ALU.mult).then_inc(routed.sem, 1)

            def experts(l, w):
                def expert(e, slot, loads, passes):
                    def body(base, n):
                        numbers = const("iota")[:, bass.ds(base.with_bounds(max_val=T - PASS), PASS)]
                        for a in range(TT):
                            ts(pick[:, a, :], numbers, place[:, a, bass.ds(e, 1)], None, ALU.is_equal).then_inc(picked, 1)
                        for a in range(TT):
                            ts(spread[:, a, :].rearrange("p (q s) -> p q s", q=Q), numbers.unsqueeze(1).to_broadcast([P, Q, PASS]),
                               place[:, a, bass.ds(e, 1)], gate[:, a, bass.ds(e, 1)], ALU.is_equal, ALU.mult).then_inc(spread_set, 1)
                        dve.wait_ge(got_turned, n + 1)
                        tt(got_T[:, :, :, :], bank[5][:, 0:T].rearrange("p (s q t) -> p s q t", s=2, q=Q),
                           w.rearrange("p (q s) -> p s q", s=2).unsqueeze(3).to_broadcast([P, 2, Q, PASS]),
                           ALU.mult).then_inc(got_scaled, 1)
                        dve.wait_ge(silu_done, n + 1)
                        tt(hid[:, :], silu[:, :], bank[6][:, P:2 * P], ALU.mult).then_inc(hid_ready, 1)
                        dve.wait_ge(hid_turned, n + 1)
                        dve.tensor_copy(hid_T[:, :, :].rearrange("p c t -> p (c t)"), bank[7][:, 0:P]).then_inc(hid_kept, 1)

                    passes(body)

                total = over_experts(dve, l, expert, lambda: dve.wait_ge(*routed.at(l, 2)))
                dve.wait_ge(scattered, total)
                for q in range(Q):
                    tt(x[:, :, q * T:(q + 1) * T], x[:, :, q * T:(q + 1) * T], bank[q][:, :].rearrange("p (a c) -> p a c", a=TT),
                       ALU.add).then_inc(x_added.sem, 1)

            dve.wait_ge(consts_loaded, 48)
            dve.wait_ge(x_loaded, 16)
            norm(0)
            for a in range(TT):
                ts(tok[:, a, :].rearrange("p (k c) -> p c k", k=KC), x[:, a, :].rearrange("p (c k) -> p c k", k=KC),
                   scale[:, a:a + 1], None, ALU.mult).then_inc(normed.sem, 1)
            lower_bound()
            softplus()
            for b in (0, 1):
                dve.wait_ge(*turned.at(0, b + 1))
                tt(act_T[:, 2 * b:2 * b + 2, :], bank[4 + b][:, :].rearrange("p (k t) -> p k t", k=2),
                   vec("norm_mix", 2 * b, 2 * b + 2).unsqueeze(2).to_broadcast([P, 2, T]), ALU.mult).then_inc(scaled_v.sem, 1)
            even_mixer()
            norm_tokens(1, vec("norm_ffn", 0, 8))
            route(0)
            experts(0, vec("norm_ffn", 0, 8))
            norm_tokens(2, vec("norm_mix", 8, 16))
            odd_mixer()
            norm_tokens(3, vec("norm_ffn", 8, 16))
            route(1)
            experts(1, vec("norm_ffn", 8, 16))
            norm(4)
            dve.wait_ge(final_w_loaded, 16)
            for a in range(TT):
                stt(tok[:, a, :], x[:, a, :], scale[:, a:a + 1], gates[:, 0, :], ALU.mult, ALU.mult).then_inc(normed.sem, 1)


def kernel(**inputs):
    import concourse.bacc as bacc
    from concourse.bass_utils import run_bass_kernel_spmd

    a = {name: np.ascontiguousarray(v) for name, v in inputs.items()}

    def chunks(v):
        return v.reshape(P, -1)

    def columns(v):
        return v.reshape(-1, P).T

    def everywhere(v):
        return np.broadcast_to(v.reshape(1, -1), (P, v.size))

    parts = {
        "norm_mix": np.concatenate([chunks(v) for v in a["norm_mix"]], 1),
        "norm_ffn": np.concatenate([chunks(v) for v in a["norm_ffn"]], 1),
        "lb": np.concatenate([columns(v) for v in a["hgrn_lb_logits"]], 1),
        "even_w": np.concatenate([columns(a["hgrn_norm_w"]), columns(a["gla_norm_w"])], 1),
        "gla_b": columns(a["gla_b_up"]), "ret_w": columns(a["ret_norm_w"]), "conv_w": columns(a["conv_w"]),
        "conv_b": columns(a["conv_b"]), "b_r": columns(a["rglru_b_r"]), "b_i": columns(a["rglru_b_i"]),
        "lam": columns(a["rglru_lambda"]),
        "w_group": np.concatenate([chunks(v) for v in a["moe_w_group"]], 1),
        "w_expert": np.concatenate([chunks(v) for v in a["moe_w_expert"]], 1),
        "b_group": everywhere(a["moe_b_group"]), "b_expert": everywhere(a["moe_b_expert"]),
    }
    assert all(parts[n].shape == (P, w) for n, w in VECTORS.items())
    packed, masks = shape_constants()
    feeds = {n: a[n] for n in ("x", "even_w_in", "even_w_out", "odd_w_in", "odd_w_out", "gla_w_up", "rglru_w_r",
                               "rglru_w_i", "moe_w1", "moe_w3", "moe_w2", "norm_final")}
    feeds["vectors"] = np.ascontiguousarray(np.concatenate([parts[n] for n in VECTORS], axis=1))
    feeds["shape_consts"] = packed
    feeds["masks"] = masks

    nc = bacc.Bacc("TRN2", target_bir_lowering=False, num_devices=1)
    args, arrays = [], {}
    for name, v in feeds.items():
        arrays[f"in_{name}_dram"] = v
        args.append(nc.dram_tensor(f"in_{name}_dram", v.shape, mybir.dt.from_np(v.dtype), kind="ExternalInput").ap())
    args.append(nc.dram_tensor("out_dram", (1, T, D), F32, kind="ExternalOutput").ap())
    trunk(nc, *args)
    r = run_bass_kernel_spmd(nc, [arrays], core_ids=[0])
    return r.results[0]["out_dram"]
```

```python
from contextlib import ExitStack

import numpy as np

import concourse.bass as bass
from concourse import mybir

F32 = mybir.dt.float32
I32 = mybir.dt.int32
U8 = mybir.dt.uint8
BF16 = mybir.dt.bfloat16
ACT = mybir.ActivationFunctionType
ALU = mybir.AluOpType
AX = mybir.AxisListType

P = 128
T = 256
TT = T // P
D = 1024
KC = D // P
EPS = 1e-6
HEADS = 4
CONV = 4
RG_C = 8.0
NG, NE_G = 4, 8
NE = NG * NE_G
ROUTE = NG + NE
FF = 512
PASS = 32
Q = P // PASS
SLOTS = 3
SLOT = 3 * D * FF // P
PIECE = KC * 512
ORDER = (0, 2, 1)
LEVELS = (64, 32, 16, 8, 4, 2, 1)
OUT_BANKS = ((0, 2, 4, 5), (2, 3, 6, 7))
PROJECT_AT = (0, 1, 2, 3, 4, 5, 7)
BIG1, BIG2 = 1.0e30, 1.0e32
EVEN_COLS = {"a_q": 0, "a_f": 512, "a_i": 1024, "a_g": 1536, "b_qk": 2048, "b_v": 2560, "b_low": 3072, "b_r": 3088}
ODD_COLS = {"c_qk": 0, "c_v": 512, "c_g": 1024, "d_x": 1536, "d_gate": 2048}

SHAPE_CONSTS = {"ident": 128, "before": 128, "ones": 128, "swap": 128, "rope": 1024, "decay": 1536,
                "iota": 256, "down32": 32, "down4": 4}
VECTORS = {"norm_mix": 16, "norm_ffn": 16, "lb": 12, "even_w": 8, "gla_b": 2, "ret_w": 4, "conv_w": 16,
           "conv_b": 4, "b_r": 4, "b_i": 4, "lam": 4, "w_route": 2 * KC * ROUTE, "b_route": 2 * ROUTE}


def places(widths):
    at, out = 0, {}
    for name, w in widths.items():
        out[name] = (at, w)
        at += w
    return out, at


def shape_constants():
    p = np.arange(P)
    half = 32
    inv = np.float32(10000.0) ** (-np.arange(half, dtype=np.float32) / np.float32(half))
    ang = (np.arange(T, dtype=np.float32)[:, None] * inv[None, :]).astype(np.float32)
    cos, sin = np.cos(ang).T.astype(np.float32), np.sin(ang).T.astype(np.float32)
    cos, sin = cos[p % half], sin[p % half] * np.where(p % 64 < half, -1.0, 1.0)[:, None]
    k_scale = 64.0 ** -0.5
    rope = np.concatenate([cos, cos * k_scale, sin, sin * k_scale], axis=1)
    log_gamma = np.log1p(-np.exp2(-5.0 - np.arange(HEADS)))
    decay = np.zeros((P, 2, 3, 2, P))
    for parity in range(2):
        for block in range(3):
            for pair in range(2):
                gap = p[None, :] - p[:, None] + (P if block == 2 else 0)
                decay[:, parity, block, pair] = np.where(gap >= 0, np.exp(np.maximum(gap, 0) * log_gamma[2 * pair + parity]), 0)
    parts = {"ident": np.eye(P), "before": (p[:, None] < p[None, :]), "ones": np.ones((P, P)),
             "swap": (p[:, None] == (p[None, :] ^ half)), "rope": rope, "decay": decay.reshape(P, -1),
             "iota": np.broadcast_to(np.arange(1, T + 1), (P, T)),
             "down32": np.broadcast_to(np.arange(NE, 0, -1), (P, NE)),
             "down4": np.broadcast_to(np.arange(NG, 0, -1), (P, NG))}
    packed = np.concatenate([np.asarray(parts[n], np.float32) for n in SHAPE_CONSTS], axis=1)
    masks = np.stack([(p[:, None] // (2 * h) == p[None, :] // (2 * h)) & (p[:, None] % (2 * h) < h) & (p[None, :] % (2 * h) >= h)
                      for h in LEVELS], axis=1)
    return np.ascontiguousarray(packed), np.ascontiguousarray(masks.astype(np.float32).reshape(P, -1))


class Staged:

    def __init__(self, sem, each):
        self.sem, self.each = sem, each

    def at(self, stage, value):
        return self.sem, self.each * stage + value


def trunk(nc, x_in, even_w_in, even_w_out, odd_w_in, odd_w_out, gla_w_up, rglru_w_r, rglru_w_i,
          moe_w1, moe_w3, moe_w2, norm_final, vectors, shape_consts, masks_in, out):
    const_at, n_const = places(SHAPE_CONSTS)
    vec_at, n_vec = places(VECTORS)

    with ExitStack() as ctx:
        def sb(name, shape, dt=F32):
            return ctx.enter_context(nc.sbuf_tensor(name, shape, dt))

        def sem(name):
            return ctx.enter_context(nc.semaphore(name))

        bank = [ctx.enter_context(nc.psum_tensor(f"bank{i}", [P, 512], F32)) for i in range(8)]

        weights = sb("weights", [P, SLOTS, SLOT])
        consts = sb("consts", [P, n_const])
        vecs = sb("vecs", [P, n_vec])
        masks = sb("masks", [P, len(LEVELS) * P], U8)
        x = sb("x", [P, TT, D])
        act_T = sb("act_T", [P, KC, T])
        y_T = sb("y_T", [P, KC, T])
        tok = sb("tok", [P, TT, D])
        gates = sb("gates", [P, TT, D])
        sums = sb("sums", [P, 2])
        root = sb("root", [P, 2])
        scale = sb("scale", [P, 2])
        lb_e = sb("lb_e", [P, 3, 4])
        lb_t = sb("lb_t", [P, 3, 4])
        head_ss = sb("head_ss", [P, 16])
        head_r = sb("head_r", [P, 16])
        head_m = sb("head_m", [P, 8])
        w_rg = sb("w_rg", [P, 2, 4, P])
        sp = sb("sp", [P, 8, 4])
        nb = sb("nb", [P, 2, 4])
        counts = sb("counts", [1, NE], I32)
        zeros = sb("zeros", [P, 512], BF16)

        def const(name, a=0, b=None):
            at, w = const_at[name]
            return consts[:, at + a:at + (w if b is None else b)]

        def vec(name, a=0, b=None):
            at, w = vec_at[name]
            return vecs[:, at + a:at + (w if b is None else b)]

        ident = const("ident")

        def work(at, size):
            return weights[:, 2, at:at + size]

        qA, kA, bA = (work(i * 1024, 1024) for i in range(3))
        qB, kB, bB = (work(3072 + i * 512, 512) for i in range(3))
        decA = [work(4608 + i * 1024, 1024) for i in range(2)]
        decB = [work(6656 + i * 512, 512) for i in range(2)]
        SA = work(7680, 1536)
        SB = work(9216, 1536)
        low = weights[0:16, 2, 10752:10752 + T]
        w_up = weights[0:16, 2, 11008:11008 + T]
        masks_wide = weights[:, 2, 11264:11264 + len(LEVELS) * P]
        restart = y_T[:, 0:4, :].rearrange("p k t -> p (k t)")
        raw, rot, tmp = (work(i * 1024, 1024) for i in range(3))
        SC = work(3072, 1536)
        DXW = T + 4
        dx = work(4608, 4 * DXW).rearrange("p (m t) -> p m t", m=4)
        o1 = 4608 + 4 * DXW
        xc, rr, ii, th, dg, gl = (work(o1 + i * 1024, 1024) for i in range(6))
        assert o1 + 6 * 1024 <= SLOT

        free = {"y_T": (y_T[:, :, :].rearrange("p k t -> p (k t)"), 0), "gates": (gates[:, :, :].rearrange("p a d -> p (a d)"), 0)}

        def over(host, *shape):
            flat, at = free[host]
            size = int(np.prod(shape))
            free[host] = (flat, at + size)
            assert at + size <= TT * D
            v = flat[:, at:at + size]
            names = "abcd"[:len(shape)]
            return v.rearrange(f"p ({' '.join(names)}) -> p {' '.join(names)}", **dict(zip(names[1:], shape[1:])))

        r_small = over("y_T", 2, 8, 4)
        r_wide = over("y_T", 8, TT, NE)
        chosen = over("y_T", TT, NE)
        gate = over("y_T", TT, NE)
        place = over("y_T", TT, NE)
        pick = over("gates", TT, PASS)
        spread = over("gates", TT, P)
        spread_T = over("gates", TT * P)
        got = over("gates", T)
        got_T = over("gates", 2, Q, PASS)
        silu = over("gates", P)
        hid = over("gates", P)
        hid_T = over("gates", Q, PASS)
        y_tok = over("gates", T)

        ident_loaded, vecs_loaded, w_up_loaded = map(sem, ("ident_loaded", "vecs_loaded", "w_up_loaded"))
        x_loaded, consts_loaded, rg_loaded, final_w_loaded = map(sem, ("x_loaded", "consts_loaded", "rg_loaded", "final_w_loaded"))
        piece_loaded = {n: sem(f"loaded_{n}") for n in list(EVEN_COLS) + list(ODD_COLS) + ["even_out", "odd_out"]}
        up_loaded = [sem(f"up_loaded_slot{s}") for s in range(SLOTS)]
        down_loaded = [sem(f"down_loaded_slot{s}") for s in range(SLOTS)]
        masks_loaded, masks_set = sem("masks_loaded"), sem("masks_set")
        pool_set, vector_step, scalar_step = map(sem, ("pool_set", "vector_step", "scalar_step"))
        squared = Staged(sem("squared"), 2)
        mean_set = Staged(sem("mean_set"), 1)
        rooted = Staged(sem("rooted"), 1)
        normed = Staged(sem("normed"), 2)
        turned = Staged(sem("turned"), 4)
        scaled_v = Staged(sem("scaled_v"), 2)
        scaled_a = Staged(sem("scaled_a"), 4)
        x_added = Staged(sem("x_added"), 4)
        af_ready, aq_ready, bqk_ready, low_ready, z_ready = map(sem, ("af_ready", "aq_ready", "bqk_ready", "low_ready", "z_ready"))
        sig_done, aq_kept, bqk_kept, low_kept, z_taken = map(sem, ("sig_done", "aq_kept", "bqk_kept", "low_kept", "z_taken"))
        f_ready, f_logged, key_ready = map(sem, ("f_ready", "f_logged", "key_ready"))
        z_set, z_abs, z_exped, z_logged, sums_ready = map(sem, ("z_set", "z_abs", "z_exped", "z_logged", "sums_ready"))
        lb_set, lb_exped = map(sem, ("lb_set", "lb_exped"))
        gap_ready, gap_exped, decayed = map(sem, ("gap_ready", "gap_exped", "decayed"))
        scores_ready, scores_kept = sem("scores_ready"), sem("scores_kept")
        qk_ready, qk_kept, swapped, rotated = map(sem, ("qk_ready", "qk_kept", "swapped", "rotated"))
        dx_ready, dx_kept, dg_ready, dg_kept, conv_done = map(sem, ("dx_ready", "dx_kept", "dg_ready", "dg_kept", "conv_done"))
        ret_ready, ret_kept, rg_ready, rg_exped, rg_set = map(sem, ("ret_ready", "ret_kept", "rg_ready", "rg_exped", "rg_set"))
        th_done, th_root, lam_set, lam_exped = map(sem, ("th_done", "th_root", "lam_set", "lam_exped"))
        dg_squared, dg_inner, dg_tanh, yd_ready = map(sem, ("dg_squared", "dg_inner", "dg_tanh", "yd_ready"))
        centred = sem("centred")
        proj_ready = Staged(sem("proj_ready"), 8)
        proj_kept = Staged(sem("proj_kept"), 8)
        gates_open = sem("gates_open")
        heads_ready = Staged(sem("heads_ready"), 4)
        heads_squared = Staged(sem("heads_squared"), 4)
        heads_mean = Staged(sem("heads_mean"), 2)
        heads_root = Staged(sem("heads_root"), 2)
        y_ready = Staged(sem("y_ready"), 16)
        y_turned = Staged(sem("y_turned"), 4)
        y_scaled_v = Staged(sem("y_scaled_v"), 2)
        y_scaled_a = Staged(sem("y_scaled_a"), 4)
        mix_ready = Staged(sem("mix_ready"), 4)
        logits_ready = Staged(sem("logits_ready"), 1)
        group_gap = Staged(sem("group_gap"), 1)
        group_exped = Staged(sem("group_exped"), 1)
        pair_gap = Staged(sem("pair_gap"), 1)
        pair_exped = Staged(sem("pair_exped"), 1)
        chosen_set = Staged(sem("chosen_set"), 1)
        ranks_ready = Staged(sem("ranks_ready"), 1)
        routed = Staged(sem("routed"), 2)
        picked = sem("picked")
        spread_set = sem("spread_set")
        gathered = sem("gathered")
        got_kept = sem("got_kept")
        got_turned = sem("got_turned")
        got_scaled = sem("got_scaled")
        spread_turned = sem("spread_turned")
        spread_kept = sem("spread_kept")
        up_done = sem("up_done")
        silu_done = sem("silu_done")
        hid_ready = sem("hid_ready")
        hid_turned = sem("hid_turned")
        hid_kept = sem("hid_kept")
        down_done = sem("down_done")
        y_kept = sem("y_kept")
        scattered = sem("scattered")
        out_stored = sem("out_stored")

        def loads_before(slot, l):
            return l * len([e for e in range(NE) if ORDER[e % 3] == slot])

        def by_group(heads, grp):
            return heads[:, :].rearrange("p (a g h) -> p a g h", a=TT, g=2)[:, :, grp, :]

        pass_count = {}

        def over_experts(eng, l, expert, counts_ready):
            if l == 0:
                pass_count[eng.engine] = eng.alloc_register(f"passes_{eng.engine.name}")
                eng.reg_mov(pass_count[eng.engine], 0)
            n = pass_count[eng.engine]
            counts_ready()

            def one(e, slot, loads):
                tokens = eng.value_load(counts[0:1, bass.ds(e, 1)], min_val=0, max_val=T)

                def passes(body):
                    with eng.Fori(0, tokens, PASS) as base:
                        body(base, eng.snap(n, min_val=0, max_val=2 * NE * T // PASS))
                        eng.reg_add(n, n, 1)

                expert(e, slot, loads, passes)

            with eng.Fori(0, NE // 3) as i:
                for s in range(3):
                    one(3 * i + s, ORDER[s], loads_before(ORDER[s], l) + 1 + i)
            for e in range(NE // 3 * 3, NE):
                one(e, ORDER[e % 3], loads_before(ORDER[e % 3], l) + 1 + e // 3)
            return eng.snap(n, min_val=0, max_val=2 * NE * T // PASS)

        block = ctx.enter_context(nc.Block())

        @block.sync
        def _(sp_q):
            sp_q.dma_start(x[:, :, :], x_in.rearrange("o (a p) d -> p (o a) d", p=P)).then_inc(x_loaded, 16)

            def piece(name, slot, at, w_in, cols, width=512):
                dst = weights[:, slot, at:at + KC * width].rearrange("p (k c) -> p k c", k=KC)
                src = w_in[0, :, cols:cols + width].rearrange("(p k) c -> p k c", k=KC)
                sp_q.dma_start(dst, src).then_inc(piece_loaded[name], 16)

            def out_weights(name, w_out):
                dst = weights[:, 1, 0:KC * D].rearrange("p (k c) -> p k c", k=KC)
                sp_q.dma_start(dst, w_out[0].rearrange("(k p) c -> p k c", p=P)).then_inc(piece_loaded[name], 16)

            passes = sp_q.alloc_register("passes_SP")
            sp_q.reg_mov(passes, 0)

            def up_to(e):
                tokens = sp_q.value_load(counts[0:1, bass.ds(e, 1)], min_val=0, max_val=T)
                with sp_q.Fori(0, tokens, PASS):
                    sp_q.reg_add(passes, passes, 1)
                return sp_q.snap(passes, min_val=1, max_val=2 * NE * T // PASS)

            def load_expert(l, e, slot, before=None):
                up = weights[:, slot, 0:2 * PIECE].rearrange("p (k w f) -> p k w f", k=KC, w=2)
                if before is not None:
                    sp_q.wait_ge(up_done, before)
                for w, src in enumerate((moe_w1, moe_w3)):
                    sp_q.dma_start(up[:, :, w, :], src[l, bass.ds(e, 1)].rearrange("o (p k) f -> p (o k) f", k=KC)
                                   ).then_inc(up_loaded[slot], 16)
                down = weights[:, slot, 2 * PIECE:].rearrange("p (c d) -> p c d", c=Q)
                if before is not None:
                    sp_q.wait_ge(down_done, before)
                sp_q.dma_start(down, moe_w2[l, bass.ds(e, 1)].rearrange("o (c p) d -> p (o c) d", p=P)
                               ).then_inc(down_loaded[slot], 16)

            def load_experts(l):
                sp_q.wait_ge(*routed.at(l, 2))
                with sp_q.Fori(1, NE // 3) as i:
                    for s in range(3):
                        load_expert(l, 3 * i + s, ORDER[s], up_to(3 * i + (s - 3)))
                for e in range(NE // 3 * 3, NE):
                    load_expert(l, e, ORDER[e % 3], up_to(e - 3))

            C = EVEN_COLS
            sp_q.dma_start(consts[:, 0:P], shape_consts[:, 0:P]).then_inc(ident_loaded, 16)
            sp_q.dma_start(vecs[:, :], vectors).then_inc(vecs_loaded, 16)
            piece("a_f", 0, 0, even_w_in, C["a_f"])
            piece("a_q", 0, PIECE, even_w_in, C["a_q"])
            piece("b_low", 1, 2 * PIECE, even_w_in, C["b_low"], 16)
            sp_q.dma_start(w_up, gla_w_up[0]).then_inc(w_up_loaded, 16)
            piece("b_qk", 1, 0, even_w_in, C["b_qk"])
            sp_q.dma_start(masks_wide, masks_in).then_inc(masks_loaded, 16)
            piece("a_i", 1, PIECE, even_w_in, C["a_i"])
            sp_q.dma_start(consts[:, P:], shape_consts[:, P:]).then_inc(consts_loaded, 16)
            sp_q.wait_ge(aq_ready, 2)
            piece("b_v", 0, 0, even_w_in, C["b_v"])
            piece("a_g", 0, PIECE, even_w_in, C["a_g"])
            piece("b_r", 0, 2 * PIECE, even_w_in, C["b_r"])
            sp_q.wait_ge(*proj_ready.at(0, 2))
            out_weights("even_out", even_w_out)
            sp_q.wait_ge(*proj_ready.at(0, 8))
            load_expert(0, 0, 0)
            sp_q.wait_ge(*y_ready.at(0, 16))
            load_expert(0, 1, 2)
            sp_q.wait_ge(*mix_ready.at(0, 4))
            load_expert(0, 2, 1)
            load_experts(0)
            C = ODD_COLS
            sp_q.wait_ge(down_done, up_to(NE - 3))
            piece("d_x", 1, PIECE, odd_w_in, C["d_x"])
            piece("c_qk", 1, 0, odd_w_in, C["c_qk"])
            piece("d_gate", 1, 2 * PIECE, odd_w_in, C["d_gate"])
            before_30, before_31 = up_to(NE - 2), up_to(NE - 1)
            sp_q.wait_ge(down_done, before_30)
            piece("c_v", 0, 0, odd_w_in, C["c_v"])
            piece("c_g", 0, PIECE, odd_w_in, C["c_g"])
            sp_q.wait_ge(dg_ready, 2)
            out_weights("odd_out", odd_w_out)
            sp_q.wait_ge(*proj_ready.at(1, 4))
            load_expert(1, 0, 0)
            sp_q.wait_ge(*y_ready.at(1, 8))
            sp_q.wait_ge(yd_ready, 4)
            load_expert(1, 1, 2)
            sp_q.wait_ge(*mix_ready.at(1, 4))
            load_expert(1, 2, 1)
            load_experts(1)

        @block.gpsimd
        def _(pool):
            pool.memset(restart, 1.0).then_inc(pool_set, 1)
            pool.wait_ge(pool_set, 1)
            pool.memset(restart.rearrange("p (n t) -> p n t", t=P)[:, :, 0:1], 0.0).then_inc(pool_set, 1)
            pool.memset(zeros[:, :], 0.0).then_inc(pool_set, 1)
            pool.memset(w_rg[:, :, :, :], 0.0).then_inc(pool_set, 1)
            pool.wait_ge(pool_set, 4)
            for g, w in enumerate((rglru_w_r, rglru_w_i)):
                for half in range(2):
                    pool.dma_start(w_rg[64 * half:64 * half + 64, g, :, 64 * half:64 * half + 64],
                                   w[0, half:8:2].rearrange("m d e -> d m e")).then_inc(rg_loaded, 16)
            pool.wait_ge(masks_loaded, 16)
            pool.tensor_copy(masks[:, :], masks_wide).then_inc(masks_set, 1)

        @block.tensor
        def _(pe):
            def wait_norm(s):
                pe.wait_ge(*scaled_v.at(s, 2))
                pe.wait_ge(*scaled_a.at(s, 4))

            def turn_tokens(s):
                pe.wait_ge(*normed.at(s, 2))
                for b in range(4):
                    for k in (2 * b, 2 * b + 1):
                        for a in range(TT):
                            at = (k % 2) * T + a * P
                            ins = pe.transpose(bank[4 + b][:, at:at + P], tok[:, a, k * P:(k + 1) * P], ident)
                    ins.then_inc(turned.sem, 1)

            def by_channel(slot, at, m, width, dst, rows=P):
                for k in range(KC):
                    lhs = weights[:, slot, at + k * width + m * P:at + k * width + m * P + rows]
                    ins = pe.matmul(dst, lhs, act_T[:, k, :], start=(k == 0), stop=(k == KC - 1))
                return ins

            def by_token(slot, at, a, dst):
                for k in range(KC):
                    ins = pe.matmul(dst, act_T[:, k, a * P:(a + 1) * P], weights[:, slot, at + k * 512:at + (k + 1) * 512],
                                    start=(k == 0), stop=(k == KC - 1))
                return ins

            def turn_y(l, first, at_bank):
                for b in range(2):
                    for j in range(2):
                        k = first + 2 * b + j
                        for a in range(TT):
                            at = j * T + a * P
                            ins = pe.transpose(bank[at_bank + b][:, at:at + P], gates[:, a, k * P:(k + 1) * P], ident)
                    ins.then_inc(y_turned.sem, 1)

            def project_out(l, first, start, stop):
                for g in range(4):
                    a, h = g // 2, g % 2
                    for k in range(first, first + 4):
                        at = k * D + h * 512
                        ins = pe.matmul(bank[OUT_BANKS[l][g]][:, :], y_T[:, k, a * P:(a + 1) * P], weights[:, 1, at:at + 512],
                                        start=(start and k == first), stop=(stop and k == first + 3))
                    if stop:
                        ins.then_inc(mix_ready.sem, 1)

            def even_mixer():
                wait_norm(0)
                pe.wait_ge(piece_loaded["a_f"], 16)
                for m in range(4):
                    ins = by_channel(0, 0, m, 512, bank[m // 2][:, m % 2 * T:m % 2 * T + T])
                    if m % 2:
                        ins.then_inc(af_ready, 1)
                pe.wait_ge(piece_loaded["a_q"], 16)
                for m in range(4):
                    ins = by_channel(0, PIECE, m, 512, bank[2 + m // 2][:, m % 2 * T:m % 2 * T + T])
                    if m % 2:
                        ins.then_inc(aq_ready, 1)
                pe.wait_ge(piece_loaded["b_low"], 16)
                by_channel(1, 2 * PIECE, 0, 16, bank[6][0:16, 0:T], rows=16).then_inc(low_ready, 1)
                pe.wait_ge(piece_loaded["b_qk"], 16)
                for m in range(4):
                    ins = by_channel(1, 0, m, 512, bank[4 + m // 2][:, m % 2 * T:m % 2 * T + T])
                    if m % 2:
                        ins.then_inc(bqk_ready, 1)
                pe.wait_ge(low_kept, 1)
                pe.wait_ge(w_up_loaded, 16)
                for m in range(2):
                    ins = pe.matmul(bank[7][:, m * T:(m + 1) * T], w_up[:, m * P:(m + 1) * P], low, start=True, stop=True)
                ins.then_inc(z_ready, 1)

                groups = [(1, PIECE, "a_i"), (0, 0, "b_v"), (0, PIECE, "a_g"), (0, 2 * PIECE, "b_r")]

                def project(g):
                    slot, at, name = groups[g // 2]
                    pe.wait_ge(piece_loaded[name], 16)
                    if g < 2:
                        pe.wait_ge(bqk_kept, g + 1)
                    else:
                        pe.wait_ge(*proj_kept.at(0, g - 1))
                    by_token(slot, at, g % 2, bank[4 + g % 2][:, :]).then_inc(proj_ready.sem, 1)

                def scores(i):
                    A = decA[i % 2].rearrange("p (h t) -> p h t", h=HEADS)
                    B = decB[i % 2].rearrange("p (m t) -> p m t", m=2)
                    keysA, keysB, queriesA, queriesB = A, B, A, B
                    if i == 0:
                        keysA, queriesA = (z.rearrange("p (h t) -> p h t", h=HEADS) for z in (kA, qA))
                        keysB, queriesB = (z.rearrange("p (m t) -> p m t", m=2) for z in (kB, qB))
                        pe.wait_ge(key_ready, 1)
                        pe.wait_ge(aq_kept, 2)
                        pe.wait_ge(bqk_kept, 2)
                    else:
                        pe.wait_ge(decayed, 4 * i)
                    cross = i == len(LEVELS) + 1
                    tiles = (0,) if cross else range(TT)
                    for a in tiles:
                        if i:
                            pe.wait_ge(scores_kept, 4 * (i - 1) + a + 1)
                        for h in range(HEADS):
                            t0 = P if cross else a * P
                            ins = pe.matmul(bank[a][:, h * P:(h + 1) * P], keysA[:, h, a * P:(a + 1) * P],
                                            queriesA[:, h, t0:t0 + P], start=True, stop=True)
                        ins.then_inc(scores_ready, 1)
                    if i:
                        pe.wait_ge(scores_kept, 4 * i)
                    for a in tiles:
                        for m in range(2):
                            for parity in range(2):
                                rows = slice(64 * parity, 64 * parity + 64)
                                at = (a * 2 + m) * P
                                t0 = P if cross else a * P
                                ins = pe.matmul(bank[2 + parity][:, at:at + P], keysB[rows, m, a * P:(a + 1) * P],
                                                queriesB[rows, m, t0:t0 + P], start=True, stop=True)
                                if a == tiles[-1] and m == 1:
                                    ins.then_inc(scores_ready, 1)

                for i in range(len(LEVELS) + 2):
                    if i in PROJECT_AT:
                        project(PROJECT_AT.index(i))
                    scores(i)

                SAv = SA.rearrange("p (b h t) -> p b h t", b=3, h=HEADS)
                SBv = SB.rearrange("p (q b m t) -> p q b m t", q=2, b=3, m=2)
                pe.wait_ge(scores_kept, 4 * 8 + 3)
                pe.wait_ge(*proj_kept.at(0, 4))
                for grp in range(2):
                    for a in range(TT):
                        for h in range(HEADS):
                            blocks = [(0, 0)] if a == 0 else [(2, 0), (1, 1)]
                            for j, (b, src) in enumerate(blocks):
                                S = SAv[:, b, h, :] if grp == 0 else SBv[:, h % 2, b, h // 2, :]
                                v = tok[:, src, grp * 512 + h * P:grp * 512 + (h + 1) * P]
                                ins = pe.matmul(bank[2 * a + grp][:, h * P:(h + 1) * P], S, v,
                                                start=(j == 0), stop=(j == len(blocks) - 1))
                        ins.then_inc(heads_ready.sem, 1)
                project(7)
                pe.wait_ge(piece_loaded["even_out"], 16)
                pe.wait_ge(*y_ready.at(0, 8))
                turn_y(0, 0, 6)
                pe.wait_ge(*y_scaled_v.at(0, 1))
                pe.wait_ge(*y_scaled_a.at(0, 2))
                pe.wait_ge(*proj_kept.at(0, 8))
                project_out(0, 0, True, False)
                pe.wait_ge(*y_ready.at(0, 16))
                turn_y(0, 4, 6)
                pe.wait_ge(*y_scaled_v.at(0, 2))
                pe.wait_ge(*y_scaled_a.at(0, 4))
                project_out(0, 4, False, True)

            def odd_mixer():
                wait_norm(2)
                pe.wait_ge(piece_loaded["d_x"], 16)
                for m in range(4):
                    ins = by_channel(1, PIECE, m, 512, bank[2 + m // 2][:, m % 2 * T:m % 2 * T + T])
                    if m % 2:
                        ins.then_inc(dx_ready, 1)
                pe.wait_ge(piece_loaded["c_qk"], 16)
                for m in range(4):
                    ins = by_channel(1, 0, m, 512, bank[m // 2][:, m % 2 * T:m % 2 * T + T])
                    if m % 2:
                        ins.then_inc(qk_ready, 1)
                pe.wait_ge(rg_loaded, 64)
                pe.wait_ge(conv_done, 4)
                pe.wait_ge(dx_kept, 2)
                for g in range(2):
                    for m in range(4):
                        ins = pe.matmul(bank[(2, 6)[g] + m // 2][:, m % 2 * T:m % 2 * T + T], w_rg[:, g, m, :],
                                        xc[:, m * T:(m + 1) * T], start=True, stop=True)
                    ins.then_inc(rg_ready, 1)
                pe.wait_ge(qk_kept, 2)
                for j in range(2):
                    pe.matmul(bank[4 + j][:, :], const("swap"), raw[:, j * 512:(j + 1) * 512],
                              start=True, stop=True).then_inc(swapped, 1)
                pe.wait_ge(piece_loaded["d_gate"], 16)
                pe.wait_ge(rg_exped, 8)
                for m in range(4):
                    ins = by_channel(1, 2 * PIECE, m, 512, bank[6 + m // 2][:, m % 2 * T:m % 2 * T + T])
                    if m % 2:
                        ins.then_inc(dg_ready, 1)
                rotv = rot.rearrange("p (z m t) -> p z m t", z=2, m=2)
                pe.wait_ge(rotated, 1)
                for b, (s0, t0) in enumerate(((0, 0), (P, P), (0, P))):
                    for m in range(2):
                        for parity in range(2):
                            rows = slice(64 * parity, 64 * parity + 64)
                            at = (b % 2 * 2 + m) * P
                            ins = pe.matmul(bank[(2 if b == 2 else 0) + parity][:, at:at + P], rotv[rows, 1, m, s0:s0 + P],
                                            rotv[rows, 0, m, t0:t0 + P], start=True, stop=True)
                            if b and m == 1:
                                ins.then_inc(ret_ready, 1)
                for g in range(2):
                    pe.wait_ge(piece_loaded["c_v"], 16)
                    pe.wait_ge(rotated, 1)
                    by_token(0, 0, g, bank[4 + g][:, :]).then_inc(proj_ready.sem, 1)
                for g in range(2):
                    pe.wait_ge(piece_loaded["c_g"], 16)
                    pe.wait_ge(*proj_kept.at(1, g + 1))
                    by_token(0, PIECE, g, bank[4 + g][:, :]).then_inc(proj_ready.sem, 1)
                SCv = SC.rearrange("p (q b m t) -> p q b m t", q=2, b=3, m=2)
                pe.wait_ge(ret_kept, 4)
                for a in range(TT):
                    for h in range(HEADS):
                        blocks = [(0, 0)] if a == 0 else [(2, 0), (1, 1)]
                        for j, (b, src) in enumerate(blocks):
                            ins = pe.matmul(bank[a][:, h * P:(h + 1) * P], SCv[:, h % 2, b, h // 2, :],
                                            tok[:, src, h * P:(h + 1) * P], start=(j == 0), stop=(j == len(blocks) - 1))
                    ins.then_inc(heads_ready.sem, 1)
                pe.wait_ge(piece_loaded["odd_out"], 16)
                pe.wait_ge(yd_ready, 4)
                pe.wait_ge(dg_kept, 2)
                project_out(1, 4, True, False)
                pe.wait_ge(*y_ready.at(1, 8))
                pe.wait_ge(*proj_kept.at(1, 4))
                turn_y(1, 0, 4)
                pe.wait_ge(*y_scaled_v.at(1, 1))
                pe.wait_ge(*y_scaled_a.at(1, 2))
                project_out(1, 0, False, True)

            def route(l):
                wait_norm(2 * l + 1)
                w = vec("w_route", l * KC * ROUTE, (l + 1) * KC * ROUTE).rearrange("p (k g) -> p k g", k=KC)
                for a in range(TT):
                    for k in range(KC):
                        ins = pe.matmul(bank[a][:, 0:ROUTE], act_T[:, k, a * P:(a + 1) * P], w[:, k, :],
                                        start=(k == 0), stop=(k == KC - 1))
                ins.then_inc(logits_ready.sem, 1)
                pe.wait_ge(*chosen_set.at(l, 1))
                pe.wait_ge(consts_loaded, 16)
                pe.matmul(bank[2][:, 0:NE], const("before"), chosen[:, 0, :], start=True, stop=True)
                pe.matmul(bank[2][:, NE:2 * NE], const("before"), chosen[:, 1, :], start=True, stop=False)
                pe.matmul(bank[2][:, NE:2 * NE], const("ones"), chosen[:, 0, :], start=False, stop=True)
                pe.matmul(bank[2][:, 64:64 + NE], const("ones"), chosen[:, 0, :], start=True, stop=False)
                pe.matmul(bank[2][:, 64:64 + NE], const("ones"), chosen[:, 1, :], start=False, stop=True).then_inc(ranks_ready.sem, 1)

            def experts(l):
                def start():
                    pe.wait_ge(*routed.at(l, 2))
                    pe.wait_ge(pool_set, 4)
                    for q in range(Q):
                        pe.matmul(bank[q][:, :], zeros[:, 0:P], zeros[:, :], start=True, stop=True, skip_group_check=True)

                def expert(e, slot, loads, passes):
                    up = weights[:, slot, 0:2 * PIECE].rearrange("p (k w f) -> p k w f", k=KC, w=2)
                    down = weights[:, slot, 2 * PIECE:].rearrange("p (c d) -> p c d", c=Q)

                    def body(base, n):
                        pe.wait_ge(picked, 2 * n + 2)
                        for a in range(TT):
                            for q in range(Q):
                                ins = pe.matmul(bank[4][PASS * q:PASS * (q + 1), 0:T], pick[:, a, :], tok[:, a, q * T:(q + 1) * T],
                                                start=(a == 0), stop=(a == TT - 1), tile_position=(0, PASS * q), skip_group_check=True)
                        ins.then_inc(gathered, 1)
                        pe.wait_ge(spread_set, 2 * n + 2)
                        for a in range(TT):
                            ins = pe.transpose(bank[7][:, T + a * P:T + (a + 1) * P], spread[:, a, :], ident)
                        ins.then_inc(spread_turned, 1)
                        pe.wait_ge(got_kept, n + 1)
                        for s in range(2):
                            ins = pe.transpose(bank[5][:, s * P:(s + 1) * P], got[:, s * P:(s + 1) * P], ident)
                        ins.then_inc(got_turned, 1)
                        pe.wait_ge(got_scaled, n + 1)
                        pe.wait_ge(up_loaded[slot], 32 * loads)
                        for k in range(KC):
                            for j in range(Q):
                                ins = pe.matmul(bank[6][PASS * j:PASS * (j + 1), 0:T], got_T[:, k % 2, k // 2, :],
                                                up[:, k, :, j * P:(j + 1) * P], start=(k == 0), stop=(k == KC - 1),
                                                tile_position=(0, PASS * j), skip_group_check=True)
                        ins.then_inc(up_done, 1)
                        pe.wait_ge(hid_ready, n + 1)
                        pe.wait_ge(spread_kept, n + 1)
                        pe.transpose(bank[7][:, 0:P], hid[:, :], ident).then_inc(hid_turned, 1)
                        pe.wait_ge(hid_kept, n + 1)
                        pe.wait_ge(down_loaded[slot], 16 * loads)
                        for c in range(Q):
                            for q in range(Q):
                                ins = pe.matmul(bank[7][PASS * q:PASS * (q + 1), T:2 * T], hid_T[:, c, :],
                                                down[:, c, q * T:(q + 1) * T], start=(c == 0), stop=(c == Q - 1),
                                                tile_position=(0, PASS * q), skip_group_check=True)
                        ins.then_inc(down_done, 1)
                        pe.wait_ge(y_kept, n + 1)
                        for a in range(TT):
                            for q in range(Q):
                                rows = slice(PASS * q, PASS * (q + 1))
                                ins = pe.matmul(bank[q][:, a * T:(a + 1) * T], spread_T[rows, a * P:(a + 1) * P], y_tok[rows, :],
                                                start=False, stop=True, tile_position=(PASS * q, 0), skip_group_check=True)
                        ins.then_inc(scattered, 1)

                    passes(body)

                over_experts(pe, l, expert, start)

            pe.wait_ge(ident_loaded, 16)
            turn_tokens(0)
            even_mixer()
            turn_tokens(1)
            route(0)
            experts(0)
            turn_tokens(2)
            odd_mixer()
            turn_tokens(3)
            route(1)
            experts(1)

        @block.scalar
        def _(act):
            steps = [0]

            def link(ins):
                steps[0] += 1
                ins.then_inc(scalar_step, 1)
                act.wait_ge(scalar_step, steps[0])

            def f(out_, in_, fn, **kw):
                return act.activation(out_, in_, fn, **kw)

            def norm(s):
                for a in range(TT):
                    if s:
                        act.wait_ge(*x_added.at(s - 1, 2 * a + 2))
                    f(tok[:, a, :], x[:, a, :], ACT.Square, accum_out=sums[:, a:a + 1]).then_inc(squared.sem, 1)
                act.wait_ge(*mean_set.at(s, 1))
                f(root[:, :], sums[:, :], ACT.Sqrt).then_inc(rooted.sem, 1)

            def norm_scale(s, w):
                for b in (2, 3):
                    act.wait_ge(*turned.at(s, b + 1))
                    for k in (2 * b, 2 * b + 1):
                        f(act_T[:, k, :], bank[4 + b][:, k % 2 * T:k % 2 * T + T], ACT.Copy,
                          scale=w[:, k:k + 1]).then_inc(scaled_a.sem, 1)

            def y_scale(l, b, at_bank, w):
                act.wait_ge(*y_turned.at(l, b + 1))
                for k in (2 * b, 2 * b + 1):
                    f(y_T[:, k, :], bank[at_bank][:, k % 2 * T:k % 2 * T + T], ACT.Copy,
                      scale=w[:, k:k + 1]).then_inc(y_scaled_a.sem, 1)

            def even_mixer():
                for b in range(2):
                    act.wait_ge(af_ready, b + 1)
                    f(kA[:, b * 512:(b + 1) * 512], bank[b][:, :], ACT.Sigmoid).then_inc(sig_done, 1)
                for b in range(2):
                    act.wait_ge(aq_ready, b + 1)
                    act.copy(qA[:, b * 512:(b + 1) * 512], bank[2 + b][:, :]).then_inc(aq_kept, 1)
                act.wait_ge(low_ready, 1)
                act.copy(low, bank[6][0:16, 0:T]).then_inc(low_kept, 1)
                act.wait_ge(f_ready, 4)
                f(decA[0], kA, ACT.Ln).then_inc(f_logged, 1)
                act.wait_ge(bqk_ready, 1)
                f(qB, bank[4][:, :], ACT.Copy, scale=64.0 ** -0.5).then_inc(bqk_kept, 1)
                act.wait_ge(bqk_ready, 2)
                act.copy(kB, bank[5][:, :]).then_inc(bqk_kept, 1)
                act.wait_ge(z_set, 2)
                f(decB[0], bB, ACT.Abs).then_inc(z_abs, 1)
                act.wait_ge(z_abs, 1)
                f(decB[0], decB[0], ACT.Exp, scale=-1.0).then_inc(z_exped, 1)
                act.wait_ge(z_exped, 1)
                f(decB[0], decB[0], ACT.Ln, bias=1.0).then_inc(z_logged, 1)

                def keep(g):
                    act.wait_ge(*proj_ready.at(0, g + 1))
                    dst = (tok, tok, gates, gates)[g // 2]
                    at = (0, 512, 0, 512)[g // 2]
                    act.copy(dst[:, g % 2, at:at + 512], bank[4 + g % 2][:, :]).then_inc(proj_kept.sem, 1)

                keep(0)
                for i in range(1, len(LEVELS) + 2):
                    h = (LEVELS + (P,))[i - 1]
                    for buf, b_run, j in ((decA[i % 2], bA, 1), (decB[i % 2], bB, 2)):
                        act.wait_ge(gap_ready, 2 * (i - 1) + j)
                        v = buf.rearrange("p (n c) -> p n c", c=2 * h)
                        if h == P:
                            first, scale_first = v[:, :, 0:h], 1.0
                            second = b_run.rearrange("p (n c) -> p n c", c=2 * h)[:, :, h:]
                        else:
                            first, scale_first, second = v[:, :, 0:h], -1.0, v[:, :, h:]
                        f(v[:, :, h:], second, ACT.Exp).then_inc(gap_exped, 1)
                        f(v[:, :, 0:h], first, ACT.Exp, scale=scale_first).then_inc(gap_exped, 1)
                    if i in PROJECT_AT:
                        keep(PROJECT_AT.index(i))
                act.wait_ge(*proj_kept.at(0, 7))
                for part in (gates[:, :, 0:512], gates[:, 0:1, 512:1024]):
                    f(part, part, ACT.Silu).then_inc(gates_open, 1)
                act.wait_ge(scores_ready, 35)
                act.wait_ge(decayed, 32)
                for j, b in enumerate((0, 2, 1, 3)):
                    act.wait_ge(*heads_ready.at(0, j + 1))
                    f(work(4608 + 512 * b, 512), bank[b][:, :], ACT.Square).then_inc(heads_squared.sem, 1)
                act.wait_ge(*proj_ready.at(0, 8))
                f(gates[:, 1, 512:1024], bank[5][:, :], ACT.Silu).then_inc(proj_kept.sem, 1)
                for grp in range(2):
                    act.wait_ge(*heads_mean.at(0, grp + 1))
                    f(by_group(head_r, grp), by_group(head_ss, grp), ACT.Sqrt).then_inc(heads_root.sem, 1)
                for grp in range(2):
                    y_scale(0, 2 * grp + 1, 7, vec("even_w"))

            def odd_mixer():
                for b in range(2):
                    act.wait_ge(dx_ready, b + 1)
                    act.copy(dx[:, 2 * b:2 * b + 2, 3:3 + T],
                             bank[2 + b][:, :].rearrange("p (m t) -> p m t", m=2)).then_inc(dx_kept, 1)
                for b in range(2):
                    act.wait_ge(qk_ready, b + 1)
                    act.copy(raw[:, b * 512:(b + 1) * 512], bank[b][:, :]).then_inc(qk_kept, 1)
                for g, dst in enumerate((rr, ii)):
                    act.wait_ge(rg_ready, g + 1)
                    for m in range(4):
                        f(dst[:, m * T:(m + 1) * T], bank[(2, 6)[g] + m // 2][:, m % 2 * T:m % 2 * T + T], ACT.Exp,
                          scale=-1.0, bias=nb[:, g, m:m + 1]).then_inc(rg_exped, 1)
                act.wait_ge(rg_set, 1)
                for m in range(4):
                    f(th[:, m * T:(m + 1) * T], rr[:, m * T:(m + 1) * T], ACT.Tanh, scale=sp[:, 0, m:m + 1]).then_inc(th_done, 1)
                act.wait_ge(th_done, 4)
                f(rr, th, ACT.Sqrt).then_inc(th_root, 1)
                for b in range(2):
                    act.wait_ge(dg_ready, b + 1)
                    act.copy(dg[:, b * 512:(b + 1) * 512], bank[6 + b][:, :]).then_inc(dg_kept, 1)
                act.wait_ge(dg_kept, 2)
                f(gl, dg, ACT.Square).then_inc(dg_squared, 1)
                act.wait_ge(dg_inner, 1)
                f(gl, gl, ACT.Tanh, scale=(2.0 / np.pi) ** 0.5).then_inc(dg_tanh, 1)
                for g in range(2):
                    act.wait_ge(*proj_ready.at(1, g + 1))
                    act.copy(tok[:, g, 0:512], bank[4 + g][:, :]).then_inc(proj_kept.sem, 1)
                for g in range(2):
                    act.wait_ge(*proj_ready.at(1, g + 3))
                    f(gates[:, g, 0:512], bank[4 + g][:, :], ACT.Silu).then_inc(proj_kept.sem, 1)
                for a in range(TT):
                    act.wait_ge(centred, a + 1)
                    f(tmp[:, a * 512:(a + 1) * 512], raw[:, a * 512:(a + 1) * 512], ACT.Square).then_inc(heads_squared.sem, 1)
                act.wait_ge(*heads_mean.at(1, 1))
                f(head_r[:, 0:8], head_ss[:, 0:8], ACT.Sqrt).then_inc(heads_root.sem, 1)
                y_scale(1, 1, 5, vec("ret_w"))

            def route(l):
                gd = r_small[:, :, 1, :]
                act.wait_ge(*group_gap.at(l, 1))
                f(r_small[:, :, 2, :], gd, ACT.Exp).then_inc(group_exped.sem, 1)
                act.wait_ge(*pair_gap.at(l, 1))
                f(root[:, :], scale[:, :], ACT.Exp).then_inc(pair_exped.sem, 1)

            def experts(l):
                def expert(e, slot, loads, passes):
                    def body(base, n):
                        act.wait_ge(gathered, n + 1)
                        act.copy(got[:, :], bank[4][:, 0:T]).then_inc(got_kept, 1)
                        act.wait_ge(spread_turned, n + 1)
                        act.copy(spread_T[:, :], bank[7][:, T:2 * T]).then_inc(spread_kept, 1)
                        act.wait_ge(up_done, n + 1)
                        f(silu[:, :], bank[6][:, 0:P], ACT.Silu).then_inc(silu_done, 1)
                        act.wait_ge(down_done, n + 1)
                        act.copy(y_tok[:, :], bank[7][:, T:2 * T]).then_inc(y_kept, 1)

                    passes(body)

                over_experts(act, l, expert, lambda: act.wait_ge(*routed.at(l, 2)))

            act.wait_ge(x_loaded, 16)
            norm(0)
            act.wait_ge(vecs_loaded, 16)
            norm_scale(0, vec("norm_mix", 0, 8))
            act.wait_ge(lb_set, 1)
            f(lb_e[:, :, :], lb_t[:, :, :], ACT.Exp).then_inc(lb_exped, 1)
            act.wait_ge(lam_set, 1)
            f(sp[:, 1, :], sp[:, 0, :], ACT.Exp, scale=-1.0).then_inc(lam_exped, 1)
            even_mixer()
            norm(1)
            norm_scale(1, vec("norm_ffn", 0, 8))
            route(0)
            experts(0)
            norm(2)
            norm_scale(2, vec("norm_mix", 8, 16))
            odd_mixer()
            norm(3)
            norm_scale(3, vec("norm_ffn", 8, 16))
            route(1)
            experts(1)
            act.wait_ge(*x_added.at(3, 1))
            act.dma_start(gates[:, 0, :], norm_final.rearrange("(o d) -> o d", o=1).to_broadcast([P, D])).then_inc(final_w_loaded, 16)
            norm(4)
            for a in range(TT):
                act.wait_ge(*normed.at(4, a + 1))
                act.dma_start(out[0, a * P:(a + 1) * P, :], tok[:, a, :]).then_inc(out_stored, 16)
            act.wait_ge(out_stored, 32)

        @block.vector
        def _(dve):
            steps = [0]

            def mark(ins):
                steps[0] += 1
                ins.then_inc(vector_step, 1)

            def link(ins):
                mark(ins)
                dve.wait_ge(vector_step, steps[0])

            ts, stt, tt = dve.tensor_scalar, dve.scalar_tensor_tensor, dve.tensor_tensor

            def norm(s):
                dve.wait_ge(*squared.at(s, 2))
                ts(sums[:, :], sums[:, :], 1.0 / D, EPS, ALU.mult, ALU.add).then_inc(mean_set.sem, 1)
                dve.wait_ge(*rooted.at(s, 1))
                link(dve.reciprocal(scale[:, :], root[:, :]))

            def norm_tokens(s, w):
                norm(s)
                for a in range(TT):
                    ts(tok[:, a, :].rearrange("p (k c) -> p c k", k=KC), x[:, a, :].rearrange("p (c k) -> p c k", k=KC),
                       scale[:, a:a + 1], None, ALU.mult).then_inc(normed.sem, 1)
                for b in (0, 1):
                    dve.wait_ge(*turned.at(s, b + 1))
                    tt(act_T[:, 2 * b:2 * b + 2, :], bank[4 + b][:, :].rearrange("p (k t) -> p k t", k=2),
                       w[:, 2 * b:2 * b + 2].unsqueeze(2).to_broadcast([P, 2, T]), ALU.mult).then_inc(scaled_v.sem, 1)

            def y_scale(l, b, at_bank, w):
                dve.wait_ge(*y_turned.at(l, b + 1))
                tt(y_T[:, 2 * b:2 * b + 2, :], bank[at_bank][:, :].rearrange("p (k t) -> p k t", k=2),
                   w[:, 2 * b:2 * b + 2].unsqueeze(2).to_broadcast([P, 2, T]), ALU.mult).then_inc(y_scaled_v.sem, 1)

            def add_mix(l):
                for a in range(TT):
                    for h in range(2):
                        dve.wait_ge(*mix_ready.at(l, 2 * a + h + 1))
                        part = x[:, a, h * 512:(h + 1) * 512]
                        tt(part, part, bank[OUT_BANKS[l][2 * a + h]][:, :], ALU.add).then_inc(x_added.sem, 1)

            def lower_bound():
                lb = vec("lb").rearrange("p (r h) -> p r h", r=3)
                link(dve.tensor_reduce(lb_e[:, 0, :], lb.rearrange("p r h -> p h r"), AX.X, ALU.max))
                tt(lb_t[:, :, :], lb, lb_e[:, 0:1, :].to_broadcast([P, 3, 4]), ALU.subtract).then_inc(lb_set, 1)
                dve.wait_ge(lb_exped, 1)
                link(dve.tensor_reduce(lb_t[:, 2, :], lb_e[:, :, :].rearrange("p r h -> p h r"), AX.X, ALU.add))
                link(dve.reciprocal(lb_t[:, 2, :], lb_t[:, 2, :]))
                link(tt(lb_t[:, 0, :], lb_e[:, 0, :], lb_t[:, 2, :], ALU.mult))
                link(ts(lb_t[:, 1, :], lb_t[:, 0, :], -1.0, 1.0, ALU.mult, ALU.add))

            def softplus():
                lam = vec("lam")
                link(ts(sp[:, 2, :], lam, -1.0, None, ALU.mult))
                tt(sp[:, 0, :], lam, sp[:, 2, :], ALU.max).then_inc(lam_set, 1)
                dve.wait_ge(lam_exped, 1)
                link(ts(sp[:, 3, :], sp[:, 1, :], 2.0, None, ALU.add))
                link(dve.reciprocal(sp[:, 3, :], sp[:, 3, :]))
                link(tt(sp[:, 3, :], sp[:, 1, :], sp[:, 3, :], ALU.mult))
                link(tt(sp[:, 4, :], sp[:, 3, :], sp[:, 3, :], ALU.mult))
                link(ts(sp[:, 5, :], sp[:, 4, :], 1.0 / 15, 1.0 / 13, ALU.mult, ALU.add))
                for n in (11, 9, 7, 5, 3, 1):
                    link(tt(sp[:, 5, :], sp[:, 5, :], sp[:, 4, :], ALU.mult))
                    link(ts(sp[:, 5, :], sp[:, 5, :], 1.0 / n, None, ALU.add))
                link(tt(sp[:, 5, :], sp[:, 5, :], sp[:, 3, :], ALU.mult))
                link(ts(sp[:, 2, :], sp[:, 2, :], 0.0, None, ALU.max))
                link(stt(sp[:, 0, :], sp[:, 5, :], 2.0, sp[:, 2, :], ALU.mult, ALU.add))
                link(ts(sp[:, 0, :], sp[:, 0, :], RG_C / 2, None, ALU.mult))
                for g, name in enumerate(("b_r", "b_i")):
                    link(ts(nb[:, g, :], vec(name), -1.0, None, ALU.mult))

            def even_mixer():
                dve.wait_ge(sig_done, 2)
                for h in range(HEADS):
                    ts(kA[:, h * T:(h + 1) * T], kA[:, h * T:(h + 1) * T], lb_t[:, 1, h:h + 1], lb_t[:, 0, h:h + 1],
                       ALU.mult, ALU.add).then_inc(f_ready, 1)
                dve.wait_ge(f_logged, 1)
                ts(kA, kA, -1.0, 1.0, ALU.mult, ALU.add).then_inc(key_ready, 1)
                dve.wait_ge(pool_set, 2)
                mark(dve.tensor_tensor_scan(bA, restart, decA[0], 0.0, ALU.mult, ALU.add))
                dve.wait_ge(z_ready, 1)
                for m in range(2):
                    ts(bB[:, m * T:(m + 1) * T], bank[7][:, m * T:(m + 1) * T], vec("gla_b", m, m + 1), None, ALU.add).then_inc(z_set, 1)
                dve.wait_ge(z_logged, 1)
                dve.wait_ge(z_set, 2)
                link(stt(decB[0], bB, 0.0, decB[0], ALU.min, ALU.subtract))
                link(ts(decB[0], decB[0], 1.0 / 16.0, None, ALU.mult))
                link(dve.tensor_tensor_scan(bB, restart[:, 0:512], decB[0], 0.0, ALU.mult, ALU.add))

                maskv = masks[:, :].rearrange("p (l t) -> p l t", l=len(LEVELS))
                SBp = [SB[:, q * 768:(q + 1) * 768] for q in range(2)]

                def keep(i):
                    if i <= len(LEVELS):
                        dsts = [SA[:, 0:512], SA[:, 512:1024], SBp[0][:, 0:512], SBp[1][:, 0:512]]
                        if i == 1:
                            dve.wait_ge(masks_set, 1)
                        for j, dst in enumerate(dsts):
                            dve.wait_ge(scores_ready, 4 * i + j + 1)
                            if i:
                                dve.wait_ge(scores_kept, 4 * (i - 1) + j + 1)
                            src = bank[j][:, :].rearrange("p (n t) -> p n t", n=4)
                            dst = dst.rearrange("p (n t) -> p n t", n=4)
                            if i == 0:
                                ins = tt(dst, src, ident.unsqueeze(1).to_broadcast([P, 4, P]), ALU.mult)
                            else:
                                ins = dve.copy_predicated(dst, maskv[:, i - 1:i, :].to_broadcast([P, 4, P]), src)
                            ins.then_inc(scores_kept, 1)
                    else:
                        for j, (dst, src) in enumerate(((SA[:, 1024:1536], bank[0][:, :]), (SBp[0][:, 512:768], bank[2][:, 0:256]),
                                                        (SBp[1][:, 512:768], bank[3][:, 0:256]))):
                            dve.wait_ge(scores_ready, 4 * i + j + 1)
                            dve.tensor_copy(dst, src).then_inc(scores_kept, 1)

                for i in range(1, len(LEVELS) + 2):
                    h = (LEVELS + (P,))[i - 1]
                    if i >= 3:
                        dve.wait_ge(scores_ready, 4 * (i - 1))
                    for buf, b_run in ((decA[i % 2], bA), (decB[i % 2], bB)):
                        v, bv = (z.rearrange("p (n c) -> p n c", c=2 * h) for z in (buf, b_run))
                        n = v.shape[1]
                        border = bv[:, :, h - 1:h]
                        if h == P:
                            ins = tt(v[:, :, 0:h], border.to_broadcast([P, n, h]), bv[:, :, 0:h], ALU.subtract)
                        else:
                            ins = tt(v, bv, border.to_broadcast([P, n, 2 * h]), ALU.subtract)
                        ins.then_inc(gap_ready, 1)
                    keep(i - 1)
                    for g, (buf, k_, q_) in enumerate(((decA[i % 2], kA, qA), (decB[i % 2], kB, qB))):
                        if i == 1:
                            dve.wait_ge(aq_kept, 2)
                            dve.wait_ge(bqk_kept, 2)
                        v, kv, qv = (z.rearrange("p (n c) -> p n c", c=2 * h) for z in (buf, k_, q_))
                        dve.wait_ge(gap_exped, 4 * (i - 1) + 2 * g + 2)
                        tt(v[:, :, h:], v[:, :, h:], qv[:, :, h:], ALU.mult).then_inc(decayed, 1)
                        tt(v[:, :, 0:h], v[:, :, 0:h], kv[:, :, 0:h], ALU.mult).then_inc(decayed, 1)
                keep(len(LEVELS) + 1)

                for grp in range(2):
                    for a in range(TT):
                        b = 2 * a + grp
                        dve.wait_ge(*heads_squared.at(0, 2 * grp + a + 1))
                        mark(dve.tensor_reduce(head_ss[:, 4 * b:4 * b + 4],
                                               work(4608 + 512 * b, 512).rearrange("p (h c) -> p h c", h=HEADS), AX.X, ALU.add))
                    dve.wait_ge(vector_step, steps[0])
                    part = by_group(head_ss, grp)
                    ts(part, part, 1.0 / P, EPS, ALU.mult, ALU.add).then_inc(heads_mean.sem, 1)
                for grp in range(2):
                    dve.wait_ge(*heads_root.at(0, grp + 1))
                    part = by_group(head_r, grp)
                    link(dve.reciprocal(part, part))
                    dve.wait_ge(gates_open, 2)
                    if grp:
                        dve.wait_ge(*proj_kept.at(0, 8))
                    for a in range(TT):
                        b = 2 * a + grp
                        for h in range(HEADS):
                            y = gates[:, a, grp * 512 + h * P:grp * 512 + (h + 1) * P]
                            stt(y, bank[b][:, h * P:(h + 1) * P], head_r[:, 4 * b + h:4 * b + h + 1], y,
                                ALU.mult, ALU.mult).then_inc(y_ready.sem, 1)
                    if grp == 0:
                        y_scale(0, 0, 6, vec("even_w"))
                y_scale(0, 2, 6, vec("even_w"))
                add_mix(0)

            def odd_mixer():
                mark(dve.memset(dx[:, :, 0:3], 0.0))
                dve.wait_ge(vector_step, steps[0])
                for j in range(CONV):
                    for m in range(4):
                        if j == 0:
                            dve.wait_ge(dx_kept, m // 2 + 1)
                        o = xc[:, m * T:(m + 1) * T]
                        w = vec("conv_w", 4 * j + m, 4 * j + m + 1)
                        if j == 0:
                            mark(ts(o, dx[:, m, 0:T], w, vec("conv_b", m, m + 1), ALU.mult, ALU.add))
                        else:
                            dve.wait_ge(vector_step, steps[0] - (3 if j < CONV - 1 else 3 - m))
                            ins = stt(o, dx[:, m, j:j + T], w, o, ALU.mult, ALU.add)
                            if j < CONV - 1:
                                mark(ins)
                            else:
                                ins.then_inc(conv_done, 1)
                dve.wait_ge(qk_kept, 2)
                tables = const("rope").rearrange("p (w z t) -> p w z t", w=2, z=2)
                tmpv, rawv, rotv = (z.rearrange("p (z m t) -> p z m t", z=2, m=2) for z in (tmp, raw, rot))
                mark(tt(tmpv, rawv, tables[:, 0].unsqueeze(2).to_broadcast([P, 2, 2, T]), ALU.mult))
                dve.wait_ge(rg_exped, 4)
                link(ts(rr, rr, 1.0, None, ALU.add))
                dve.reciprocal(rr, rr).then_inc(rg_set, 1)
                dve.wait_ge(swapped, 2)
                for z in range(2):
                    mark(tt(rotv[:, z], bank[4 + z][:, :].rearrange("p (m t) -> p m t", m=2),
                            tables[:, 1, z:z + 1].to_broadcast([P, 2, T]), ALU.mult))
                dve.wait_ge(vector_step, steps[0])
                tt(rot, rot, tmp, ALU.add).then_inc(rotated, 1)
                dve.wait_ge(rg_exped, 8)
                link(ts(ii, ii, 1.0, None, ALU.add))
                link(dve.reciprocal(ii, ii))
                dve.wait_ge(conv_done, 4)
                link(tt(xc, xc, ii, ALU.mult))
                dve.wait_ge(th_done, 4)
                link(ts(ii, th, 1.0, None, ALU.add))
                link(dve.reciprocal(ii, ii))
                dve.wait_ge(th_root, 1)
                link(ts(th, th, -1.0, 1.0, ALU.mult, ALU.add))
                mark(tt(th, th, ii, ALU.mult))
                link(stt(rr, rr, 2.0, ii, ALU.mult, ALU.mult))
                link(tt(xc, xc, rr, ALU.mult))
                for m in range(4):
                    part = slice(m * T, (m + 1) * T)
                    mark(dve.tensor_tensor_scan(ii[:, part], th[:, part], xc[:, part], 0.0, ALU.mult, ALU.add))
                decay = const("decay").rearrange("p (q c) -> p q c", q=2)
                SCq = SC.rearrange("p (q c) -> p q c", q=2)
                for j, (q, a, b, bk) in enumerate(((0, 0, 512, 0), (1, 0, 512, 1), (0, 512, 768, 2), (1, 512, 768, 3))):
                    dve.wait_ge(ret_ready, j + 1)
                    tt(SCq[:, q, a:b], bank[bk][:, 0:b - a], decay[:, q, a:b], ALU.mult).then_inc(ret_kept, 1)
                dve.wait_ge(dg_squared, 1)
                link(ts(gl, gl, 0.044715, 1.0, ALU.mult, ALU.add))
                tt(gl, gl, dg, ALU.mult).then_inc(dg_inner, 1)
                dve.wait_ge(dg_tanh, 1)
                link(stt(gl, gl, 1.0, dg, ALU.add, ALU.mult))
                for m in range(4):
                    part = slice(m * T, (m + 1) * T)
                    stt(y_T[:, 4 + m, :], ii[:, part], 0.5, gl[:, part], ALU.mult, ALU.mult).then_inc(yd_ready, 1)
                for a in range(TT):
                    dve.wait_ge(*heads_ready.at(1, a + 1))
                    hv = bank[a][:, :].rearrange("p (h c) -> p h c", h=HEADS)
                    mean = head_m[:, 4 * a:4 * a + 4]
                    link(dve.tensor_reduce(mean, hv, AX.X, ALU.add))
                    link(ts(mean, mean, 1.0 / P, None, ALU.mult))
                    tt(raw[:, a * 512:(a + 1) * 512].rearrange("p (h c) -> p h c", h=HEADS), hv,
                       mean.unsqueeze(2).to_broadcast([P, HEADS, P]), ALU.subtract).then_inc(centred, 1)
                for a in range(TT):
                    dve.wait_ge(*heads_squared.at(1, a + 1))
                    mark(dve.tensor_reduce(head_ss[:, 4 * a:4 * a + 4],
                                           tmp[:, a * 512:(a + 1) * 512].rearrange("p (h c) -> p h c", h=HEADS), AX.X, ALU.add))
                dve.wait_ge(vector_step, steps[0])
                ts(head_ss[:, 0:8], head_ss[:, 0:8], 1.0 / P, EPS, ALU.mult, ALU.add).then_inc(heads_mean.sem, 1)
                dve.wait_ge(*heads_root.at(1, 1))
                link(dve.reciprocal(head_r[:, 0:8], head_r[:, 0:8]))
                dve.wait_ge(*proj_kept.at(1, 4))
                for a in range(TT):
                    for h in range(HEADS):
                        y = gates[:, a, h * P:(h + 1) * P]
                        stt(y, raw[:, a * 512 + h * P:a * 512 + (h + 1) * P], head_r[:, 4 * a + h:4 * a + h + 1], y,
                            ALU.mult, ALU.mult).then_inc(y_ready.sem, 1)
                y_scale(1, 0, 4, vec("ret_w"))
                add_mix(1)

            def route(l):
                small = [r_small[:, :, j, :] for j in range(8)]
                g, gap, e4, eq, pen = small[0], small[1], small[2], small[3], small[4]
                wide = [r_wide[:, j] for j in range(8)]
                lm, eq1, first, second, lm2 = wide[0], wide[1], wide[2], wide[3], wide[4]
                col = [r_wide[:, 5, :, j:j + 1] for j in range(8)]
                dve.wait_ge(*logits_ready.at(l, 1))
                dve.wait_ge(consts_loaded, 16)
                for a in range(TT):
                    bias = vec("b_route", l * ROUTE, (l + 1) * ROUTE)
                    mark(tt(g[:, a], bank[a][:, 0:NG], bias[:, 0:NG], ALU.add))
                    mark(tt(lm[:, a], bank[a][:, NG:ROUTE], bias[:, NG:ROUTE], ALU.add))
                dve.wait_ge(vector_step, steps[0])

                def one_hot(dst, values, top, ramp, n):
                    link(dve.tensor_reduce(top, values, AX.X, ALU.max))
                    link(tt(dst, values, top.to_broadcast([P, TT, n]), ALU.is_equal))
                    link(tt(dst, dst, ramp.unsqueeze(1).to_broadcast([P, TT, n]), ALU.mult))
                    link(dve.tensor_reduce(col[7], dst, AX.X, ALU.max))
                    link(tt(dst, dst, col[7].to_broadcast([P, TT, n]), ALU.is_equal))

                one_hot(eq, g, col[0], const("down4"), NG)
                tt(gap, g, col[0].to_broadcast([P, TT, NG]), ALU.subtract).then_inc(group_gap.sem, 1)
                link(ts(pen, eq, -1.0, BIG1, ALU.add, ALU.mult))
                for a in range(TT):
                    v = lm[:, a].rearrange("p (g e) -> p g e", g=NG)
                    mark(tt(v, v, pen[:, a].unsqueeze(2).to_broadcast([P, NG, NE_G]), ALU.add))
                dve.wait_ge(vector_step, steps[0])
                one_hot(first, lm, col[1], const("down32"), NE)
                link(stt(lm2, first, -BIG2, lm, ALU.mult, ALU.add))
                one_hot(second, lm2, col[2], const("down32"), NE)
                tt(chosen[:, :, :], first, second, ALU.add).then_inc(chosen_set.sem, 1)
                tt(scale[:, :].unsqueeze(2), col[2], col[1], ALU.subtract).then_inc(pair_gap.sem, 1)
                dve.wait_ge(*group_exped.at(l, 1))
                link(dve.tensor_reduce(col[3], e4, AX.X, ALU.add))
                dve.wait_ge(*pair_exped.at(l, 1))
                link(ts(col[4], root[:, :].unsqueeze(2), 1.0, None, ALU.add))
                link(tt(col[3], col[3], col[4], ALU.mult))
                link(dve.reciprocal(col[3], col[3]))
                link(tt(col[4], root[:, :].unsqueeze(2), col[3], ALU.mult))
                mark(tt(first, first, col[3].to_broadcast([P, TT, NE]), ALU.mult))
                link(tt(second, second, col[4].to_broadcast([P, TT, NE]), ALU.mult))
                link(tt(gate[:, :, :], first, second, ALU.add))
                dve.wait_ge(*ranks_ready.at(l, 1))
                dve.wait_ge(*chosen_set.at(l, 1))
                dve.tensor_copy(counts[0:1, :], bank[2][0:1, 64:64 + NE]).then_inc(routed.sem, 1)
                stt(place[:, :, :], bank[2][:, 0:2 * NE].rearrange("p (a e) -> p a e", a=TT), 1.0, chosen[:, :, :],
                    ALU.add, ALU.mult).then_inc(routed.sem, 1)

            def experts(l, w):
                def expert(e, slot, loads, passes):
                    def body(base, n):
                        numbers = const("iota")[:, bass.ds(base.with_bounds(max_val=T - PASS), PASS)]
                        for a in range(TT):
                            ts(pick[:, a, :], numbers, place[:, a, bass.ds(e, 1)], None, ALU.is_equal).then_inc(picked, 1)
                        for a in range(TT):
                            ts(spread[:, a, :].rearrange("p (q s) -> p q s", q=Q), numbers.unsqueeze(1).to_broadcast([P, Q, PASS]),
                               place[:, a, bass.ds(e, 1)], gate[:, a, bass.ds(e, 1)], ALU.is_equal, ALU.mult).then_inc(spread_set, 1)
                        dve.wait_ge(got_turned, n + 1)
                        tt(got_T[:, :, :, :], bank[5][:, 0:T].rearrange("p (s q t) -> p s q t", s=2, q=Q),
                           w.rearrange("p (q s) -> p s q", s=2).unsqueeze(3).to_broadcast([P, 2, Q, PASS]),
                           ALU.mult).then_inc(got_scaled, 1)
                        dve.wait_ge(silu_done, n + 1)
                        tt(hid[:, :], silu[:, :], bank[6][:, P:2 * P], ALU.mult).then_inc(hid_ready, 1)
                        dve.wait_ge(hid_turned, n + 1)
                        dve.tensor_copy(hid_T[:, :, :].rearrange("p c t -> p (c t)"), bank[7][:, 0:P]).then_inc(hid_kept, 1)

                    passes(body)

                total = over_experts(dve, l, expert, lambda: dve.wait_ge(*routed.at(l, 2)))
                dve.wait_ge(scattered, total)
                for a in range(TT):
                    for q in range(Q):
                        part = x[:, a, q * T:(q + 1) * T]
                        ins = tt(part, part, bank[q][:, a * T:(a + 1) * T], ALU.add)
                        if q % 2:
                            ins.then_inc(x_added.sem, 1)

            dve.wait_ge(x_loaded, 16)
            norm(0)
            for a in range(TT):
                ts(tok[:, a, :].rearrange("p (k c) -> p c k", k=KC), x[:, a, :].rearrange("p (c k) -> p c k", k=KC),
                   scale[:, a:a + 1], None, ALU.mult).then_inc(normed.sem, 1)
            dve.wait_ge(vecs_loaded, 16)
            for b in (0, 1):
                dve.wait_ge(*turned.at(0, b + 1))
                tt(act_T[:, 2 * b:2 * b + 2, :], bank[4 + b][:, :].rearrange("p (k t) -> p k t", k=2),
                   vec("norm_mix", 2 * b, 2 * b + 2).unsqueeze(2).to_broadcast([P, 2, T]), ALU.mult).then_inc(scaled_v.sem, 1)
            lower_bound()
            softplus()
            even_mixer()
            norm_tokens(1, vec("norm_ffn", 0, 8))
            route(0)
            experts(0, vec("norm_ffn", 0, 8))
            norm_tokens(2, vec("norm_mix", 8, 16))
            odd_mixer()
            norm_tokens(3, vec("norm_ffn", 8, 16))
            route(1)
            experts(1, vec("norm_ffn", 8, 16))
            norm(4)
            dve.wait_ge(final_w_loaded, 16)
            for a in range(TT):
                stt(tok[:, a, :], x[:, a, :], scale[:, a:a + 1], gates[:, 0, :], ALU.mult, ALU.mult).then_inc(normed.sem, 1)


def kernel(**inputs):
    import concourse.bacc as bacc
    from concourse.bass_utils import run_bass_kernel_spmd

    a = {name: np.ascontiguousarray(v) for name, v in inputs.items()}

    def chunks(v):
        return v.reshape(P, -1)

    def columns(v):
        return v.reshape(-1, P).T

    def everywhere(v):
        return np.broadcast_to(v.reshape(1, -1), (P, v.size))

    parts = {
        "norm_mix": np.concatenate([chunks(v) for v in a["norm_mix"]], 1),
        "norm_ffn": np.concatenate([chunks(v) for v in a["norm_ffn"]], 1),
        "lb": np.concatenate([columns(v) for v in a["hgrn_lb_logits"]], 1),
        "even_w": np.concatenate([columns(a["hgrn_norm_w"]), columns(a["gla_norm_w"])], 1),
        "gla_b": columns(a["gla_b_up"]), "ret_w": columns(a["ret_norm_w"]), "conv_w": columns(a["conv_w"]),
        "conv_b": columns(a["conv_b"]), "b_r": columns(a["rglru_b_r"]), "b_i": columns(a["rglru_b_i"]),
        "lam": columns(a["rglru_lambda"]),
        "w_route": np.concatenate([chunks(v) for v in np.concatenate([a["moe_w_group"], a["moe_w_expert"]], 2)], 1),
        "b_route": everywhere(np.concatenate([a["moe_b_group"], a["moe_b_expert"]], 1)),
    }
    assert all(parts[n].shape == (P, w) for n, w in VECTORS.items())
    packed, masks = shape_constants()
    feeds = {n: a[n] for n in ("x", "even_w_in", "even_w_out", "odd_w_in", "odd_w_out", "gla_w_up", "rglru_w_r",
                               "rglru_w_i", "moe_w1", "moe_w3", "moe_w2", "norm_final")}
    feeds["vectors"] = np.ascontiguousarray(np.concatenate([parts[n] for n in VECTORS], axis=1))
    feeds["shape_consts"] = packed
    feeds["masks"] = masks

    nc = bacc.Bacc("TRN2", target_bir_lowering=False, num_devices=1)
    args, arrays = [], {}
    for name, v in feeds.items():
        arrays[f"in_{name}_dram"] = v
        args.append(nc.dram_tensor(f"in_{name}_dram", v.shape, mybir.dt.from_np(v.dtype), kind="ExternalInput").ap())
    args.append(nc.dram_tensor("out_dram", (1, T, D), F32, kind="ExternalOutput").ap())
    trunk(nc, *args)
    r = run_bass_kernel_spmd(nc, [arrays], core_ids=[0])
    return r.results[0]["out_dram"]
```

```python
from contextlib import ExitStack

import numpy as np

import concourse.bass as bass
from concourse import mybir

F32 = mybir.dt.float32
F32R = mybir.dt.float32r
I32 = mybir.dt.int32
U8 = mybir.dt.uint8
BF16 = mybir.dt.bfloat16
ACT = mybir.ActivationFunctionType
ALU = mybir.AluOpType
AX = mybir.AxisListType

P = 128
T = 256
TT = T // P
D = 1024
KC = D // P
EPS = 1e-6
HEADS = 4
CONV = 4
RG_C = 8.0
NG, NE_G = 4, 8
NE = NG * NE_G
ROUTE = NG + NE
FF = 512
PASS = 32
Q = P // PASS
SLOTS = 3
SLOT = 3 * D * FF // P
PIECE = KC * 512
ORDER = (2, 0, 1)
HALF = PIECE // 2
LOW_AT = 7680
LEVELS = (64, 32, 16, 8, 4, 2, 1)
GROUPS = ((0, 0), (1, 0), (0, 1), (1, 1))
OUT_BANKS = ((0, 2, 4, 5), (4, 6, 5, 7))
TURN_BANKS = ((1, 3, 6, 7), (0, 1, 2, 3))
PROJECT_AT = (0, 1, 2, 3, 4, 5, 7)
UNITS = ((1, 0), (1, PIECE), (1, 2 * PIECE), (0, 0))
STEPS = tuple([(n, u, h) for n, u in order for h in range(1 if n == "b_low" else 2)] for order in (
    (("a_f", 0), ("a_q", 1), ("b_low", None), ("b_qk", 2), ("a_i", 3), ("b_v", 0), ("a_g", 1), ("b_r", 3),
     ("even_out0", 0), ("even_out1", 3)),
    (("d_x", 0), ("c_qk", 1), ("d_gate", 2), ("c_v", 0), ("c_g", 3), ("odd_out1", 0), ("odd_out0", 3))))


POOL_STEPS = (range(9, 16), ())
SPLIT = ("a_f", "even_out1", "odd_out0")


def last_step(l, name):
    return max(i for i, step in enumerate(STEPS[l], 1) if step[0] == name)


BIG1, BIG2 = 1.0e30, 1.0e32
EVEN_COLS = {"a_q": 0, "a_f": 512, "a_i": 1024, "a_g": 1536, "b_qk": 2048, "b_v": 2560, "b_low": 3072, "b_r": 3088}
ODD_COLS = {"c_qk": 0, "c_v": 512, "c_g": 1024, "d_x": 1536, "d_gate": 2048}

SHAPE_CONSTS = {"ident": 128, "before": 128, "ones": 128, "swap": 128, "rope": 1024, "decay": 1536,
                "iota": 256, "down32": 32, "down4": 4}
VECTORS = {"norm_mix": 16, "norm_ffn": 16, "norm_route": 16, "lb": 12, "even_w": 8, "gla_b": 2, "ret_w": 4, "conv_w": 16,
           "conv_b": 4, "b_r": 4, "b_i": 4, "lam": 4, "w_route": 2 * KC * ROUTE, "b_route": 2 * ROUTE}


def places(widths):
    at, out = 0, {}
    for name, w in widths.items():
        out[name] = (at, w)
        at += w
    return out, at


def shape_constants():
    p = np.arange(P)
    half = 32
    inv = np.float32(10000.0) ** (-np.arange(half, dtype=np.float32) / np.float32(half))
    ang = (np.arange(T, dtype=np.float32)[:, None] * inv[None, :]).astype(np.float32)
    cos, sin = np.cos(ang).T.astype(np.float32), np.sin(ang).T.astype(np.float32)
    cos, sin = cos[p % half], sin[p % half] * np.where(p % 64 < half, -1.0, 1.0)[:, None]
    k_scale = 64.0 ** -0.5
    rope = np.concatenate([cos, cos * k_scale, sin, sin * k_scale], axis=1)
    log_gamma = np.log1p(-np.exp2(-5.0 - np.arange(HEADS)))
    decay = np.zeros((P, 2, 3, 2, P))
    for parity in range(2):
        for block in range(3):
            for pair in range(2):
                gap = p[None, :] - p[:, None] + (P if block == 2 else 0)
                decay[:, parity, block, pair] = np.where(gap >= 0, np.exp(np.maximum(gap, 0) * log_gamma[2 * pair + parity]), 0)
    parts = {"ident": np.eye(P), "before": (p[:, None] < p[None, :]), "ones": np.ones((P, P)),
             "swap": (p[:, None] == (p[None, :] ^ half)), "rope": rope, "decay": decay.reshape(P, -1),
             "iota": np.broadcast_to(np.arange(1, T + 1), (P, T)),
             "down32": np.broadcast_to(np.arange(NE, 0, -1), (P, NE)),
             "down4": np.broadcast_to(np.arange(NG, 0, -1), (P, NG))}
    packed = np.concatenate([np.asarray(parts[n], np.float32) for n in SHAPE_CONSTS], axis=1)
    masks = np.stack([(p[:, None] // (2 * h) == p[None, :] // (2 * h)) & (p[:, None] % (2 * h) < h) & (p[None, :] % (2 * h) >= h)
                      for h in LEVELS], axis=1)
    return np.ascontiguousarray(packed), np.ascontiguousarray(masks.astype(np.float32).reshape(P, -1))


class Staged:

    def __init__(self, sem, each):
        self.sem, self.each = sem, each

    def at(self, stage, value):
        return self.sem, self.each * stage + value


def trunk(nc, x_in, even_w_in, even_w_out, odd_w_in, odd_w_out, gla_w_up, rglru_w_r, rglru_w_i,
          moe_w1, moe_w3, moe_w2, norm_final, vectors, shape_consts, masks_in, out):
    const_at, n_const = places(SHAPE_CONSTS)
    vec_at, n_vec = places(VECTORS)

    with ExitStack() as ctx:
        def sb(name, shape, dt=F32):
            return ctx.enter_context(nc.sbuf_tensor(name, shape, dt))

        def sem(name):
            return ctx.enter_context(nc.semaphore(name))

        bank = [ctx.enter_context(nc.psum_tensor(f"bank{i}", [P, 512], F32)) for i in range(8)]

        weights_at = -(-nc.sbuf_base // 32) * 32
        weights = sb("weights", [P, SLOTS, SLOT])
        act_at = -(-nc.sbuf_base // 32) * 32
        act_T = sb("act_T", [P, KC, T])
        y_at = -(-nc.sbuf_base // 32) * 32
        y_T = sb("y_T", [P, KC, T])
        consts = sb("consts", [P, n_const])
        vecs = sb("vecs", [P, n_vec])
        masks = sb("masks", [P, len(LEVELS) * P], U8)
        x = sb("x", [P, TT, D])
        tok = sb("tok", [P, TT, D])
        gates = sb("gates", [P, TT, D])
        sums = sb("sums", [P, 2])
        root = sb("root", [P, 2])
        scale = sb("scale", [P, 2])
        lb_e = sb("lb_e", [P, 3, 4])
        lb_t = sb("lb_t", [P, 3, 4])
        head_ss = sb("head_ss", [P, 16])
        head_r = sb("head_r", [P, 16])
        head_m = sb("head_m", [P, 8])
        w_rg = sb("w_rg", [P, 2, 4, P])
        sp = sb("sp", [P, 8, 4])
        counts = sb("counts", [1, NE], I32)
        zeros = sb("zeros", [P, 512], BF16)
        spare = sb("spare", [P, 4])

        def const(name, a=0, b=None):
            at, w = const_at[name]
            return consts[:, at + a:at + (w if b is None else b)]

        def vec(name, a=0, b=None):
            at, w = vec_at[name]
            return vecs[:, at + a:at + (w if b is None else b)]

        ident = const("ident")

        rests = {unit: nc.alloc_sbuf_tensor_at(f"w_lo{unit}", [P, PIECE], F32R, offset=weights_at + 4 * (UNITS[unit][0] * SLOT + UNITS[unit][1]))
                 for unit in range(len(UNITS))}
        rests[None] = nc.alloc_sbuf_tensor_at("low_lo", [P, KC * P], F32R, offset=weights_at + 4 * (2 * SLOT + LOW_AT))
        act_lo = nc.alloc_sbuf_tensor_at("act_lo", [P, KC, T], F32R, offset=act_at)
        y_lo = nc.alloc_sbuf_tensor_at("y_lo", [P, KC, T], F32R, offset=y_at)
        w_hi = nc.alloc_sbuf_tensor_at("w_hi", [P, 2, HALF], F32R, offset=weights_at + 4 * PIECE)
        act_hi = nc.alloc_sbuf_tensor_at("act_hi", [P, KC, T], F32R, offset=weights_at + 4 * 2 * PIECE)
        low_hi = nc.alloc_sbuf_tensor_at("low_hi", [P, KC * P], F32R, offset=weights_at + 4 * (2 * PIECE + HALF))
        y_hi = nc.alloc_sbuf_tensor_at("y_hi", [P, KC, T], F32R, offset=weights_at + 4 * (2 * PIECE + HALF))

        def work(at, size):
            return weights[:, 2, at:at + size]

        qA, kA, bA = (work(i * 1024, 1024) for i in range(3))
        qB, kB, bB = (work(3072 + i * 512, 512) for i in range(3))
        decA = [work(4608 + i * 1024, 1024) for i in range(2)]
        decB = [work(6656 + i * 512, 512) for i in range(2)]
        SA = work(7680, 1536)
        SB = work(9216, 1536)
        low = weights[0:16, 2, 10752:10752 + T]
        w_up = weights[0:16, 2, 11008:11008 + T]
        masks_wide = weights[:, 2, 11264:11264 + len(LEVELS) * P]
        restart = decA[1]

        def buffer_of(l, i):
            return 2 if STEPS[l][i - 1][1] is None else (i - (l == 0 and i > last_step(0, "b_low"))) % 2

        def step_parts(l, i):
            name, unit, half = STEPS[l][i - 1]
            slot, at, size = (2, LOW_AT, KC * P) if unit is None else (*UNITS[unit], HALF)
            part = slice(half * HALF, half * HALF + size)
            return name, weights[:, slot, at + part.start:at + part.stop], rests[unit][:, part], (
                low_hi[:, :] if buffer_of(l, i) == 2 else w_hi[:, buffer_of(l, i), :])

        raw, rot, tmp = (work(i * 1024, 1024) for i in range(3))
        SC = work(3072, 1536)
        DXW = T + 4
        dx = work(4608, 4 * DXW).rearrange("p (m t) -> p m t", m=4)
        o1 = 4608 + 4 * DXW
        xc, rr, ii, th, dg, gl = (work(o1 + i * 1024, 1024) for i in range(6))
        assert o1 + 6 * 1024 <= SLOT

        def put_turned(l, g, copy):
            a, h = GROUPS[g]
            return copy(act_T[:, 4 * h:4 * h + 4, a * P:(a + 1) * P],
                        bank[TURN_BANKS[l][g]][:, :].rearrange("p (k t) -> p k t", k=4))

        free = {"y_T": (y_T[:, :, :].rearrange("p k t -> p (k t)"), 0), "gates": (gates[:, :, :].rearrange("p a d -> p (a d)"), 0)}

        def over(host, *shape):
            flat, at = free[host]
            size = int(np.prod(shape))
            free[host] = (flat, at + size)
            assert at + size <= TT * D
            v = flat[:, at:at + size]
            names = "abcd"[:len(shape)]
            return v.rearrange(f"p ({' '.join(names)}) -> p {' '.join(names)}", **dict(zip(names[1:], shape[1:])))

        r_small = over("y_T", 2, 8, 4)
        r_wide = over("y_T", 8, TT, NE)
        chosen = over("y_T", TT, NE)
        gate = over("y_T", TT, NE)
        logits_T = over("y_T", T)[0:ROUTE]
        place = over("y_T", TT, NE)
        pick = over("gates", TT, PASS)
        spread = over("gates", TT, P)
        spread_T = over("gates", TT * P)
        got = over("gates", T)
        got_T = over("gates", 2, Q, PASS)
        silu = over("gates", P)
        hid = over("gates", P)
        hid_T = over("gates", Q, PASS)
        y_tok = over("gates", T)

        ident_loaded, vecs_loaded, w_up_loaded = map(sem, ("ident_loaded", "vecs_loaded", "w_up_loaded"))
        consts_loaded, rg_loaded, final_w_loaded = map(sem, ("consts_loaded", "rg_loaded", "final_w_loaded"))
        x_loaded = [sem(f"x_loaded{a}") for a in range(TT)]
        half_loaded = {(n, half): sem(f"loaded_{n}_half{half}") for n in SPLIT for half in range(2)}
        piece_loaded = {n: sem(f"loaded_{n}") for n in list(EVEN_COLS) + list(ODD_COLS) + ["even_out0", "odd_out1"] if n not in SPLIT}
        hi_set, step_done = Staged(sem("hi_set"), len(STEPS[0])), Staged(sem("step_done"), len(STEPS[0]) - 1)
        lo_set = Staged(sem("lo_set"), len(STEPS[0]) - len(POOL_STEPS[0]))
        lo_set_pool = Staged(sem("lo_set_pool"), len(POOL_STEPS[0]))

        first_rest = sem("first_rest")

        def rest_is_set(l, i):
            mine = lo_set_pool if i in POOL_STEPS[l] else lo_set
            return mine.at(l, len([j for j in range(1, i + 1) if (j in POOL_STEPS[l]) == (i in POOL_STEPS[l])]))
        up_early = sem("up_early")
        up_loaded = [sem(f"up_loaded_slot{s}") for s in range(SLOTS)]
        down_loaded = [sem(f"down_loaded_slot{s}") for s in range(SLOTS)]
        masks_loaded, masks_set = sem("masks_loaded"), sem("masks_set")
        pool_set, vector_step, scalar_step = map(sem, ("pool_set", "vector_step", "scalar_step"))
        squared = Staged(sem("squared"), 2)
        mean_set = Staged(sem("mean_set"), 1)
        rooted = Staged(sem("rooted"), 1)
        normed = Staged(sem("normed"), 2)
        turned = Staged(sem("turned"), 4)
        scaled_v = Staged(sem("scaled_v"), 2)
        scaled_a = Staged(sem("scaled_a"), 4)
        act_rest = sem("act_rest")
        y_rest = Staged(sem("y_rest"), 8)
        x_added = Staged(sem("x_added"), 4)
        x_turned = Staged(sem("x_turned"), 4)
        x_kept_v, x_kept_a = Staged(sem("x_kept_v"), 3), Staged(sem("x_kept_a"), 1)
        scale_set, logits_kept, logits_turned = (Staged(sem(n), 1) for n in ("scale_set", "logits_kept", "logits_turned"))
        w_folded = sem("w_folded")
        z_ready = sem("z_ready")
        sig_done, aq_kept, bqk_kept, low_kept = map(sem, ("sig_done", "aq_kept", "bqk_kept", "low_kept"))
        f_ready, f_logged, key_ready = map(sem, ("f_ready", "f_logged", "key_ready"))
        z_set, z_abs, z_exped, z_logged = map(sem, ("z_set", "z_abs", "z_exped", "z_logged"))
        lb_set, lb_exped = map(sem, ("lb_set", "lb_exped"))
        gap_ready, gap_exped, decayed = map(sem, ("gap_ready", "gap_exped", "decayed"))
        scores_ready, scores_kept, cross_kept = map(sem, ("scores_ready", "scores_kept", "cross_kept"))
        qk_kept, swapped, rotated = map(sem, ("qk_kept", "swapped", "rotated"))
        dx_kept, dg_kept, conv_done = map(sem, ("dx_kept", "dg_kept", "conv_done"))
        ret_ready, ret_kept, rg_ready, rg_gated = map(sem, ("ret_ready", "ret_kept", "rg_ready", "rg_gated"))
        th_done, a_done, th_root, lam_set, lam_exped = map(sem, ("th_done", "a_done", "th_root", "lam_set", "lam_exped"))
        dg_squared, dg_inner, dg_tanh = map(sem, ("dg_squared", "dg_inner", "dg_tanh"))
        centred = sem("centred")
        proj_kept = Staged(sem("proj_kept"), 8)
        gates_open = sem("gates_open")
        heads_ready = Staged(sem("heads_ready"), 4)
        heads_squared = Staged(sem("heads_squared"), 4)
        heads_mean = Staged(sem("heads_mean"), 2)
        heads_root = Staged(sem("heads_root"), 2)
        y_ready = Staged(sem("y_ready"), 16)
        y_turned = Staged(sem("y_turned"), 4)
        y_scaled_v = Staged(sem("y_scaled_v"), 2)
        y_scaled_a = Staged(sem("y_scaled_a"), 4)
        mix_ready = Staged(sem("mix_ready"), 4)
        logits_ready = Staged(sem("logits_ready"), 1)
        group_gap = Staged(sem("group_gap"), 1)
        group_exped = Staged(sem("group_exped"), 1)
        pair_gap = Staged(sem("pair_gap"), 1)
        pair_exped = Staged(sem("pair_exped"), 1)
        chosen_set = Staged(sem("chosen_set"), 1)
        ranks_ready = Staged(sem("ranks_ready"), 1)
        routed = Staged(sem("routed"), 2)
        picked = sem("picked")
        spread_set = sem("spread_set")
        gathered = sem("gathered")
        got_kept = sem("got_kept")
        got_turned = sem("got_turned")
        got_scaled = sem("got_scaled")
        spread_turned = sem("spread_turned")
        spread_kept = sem("spread_kept")
        up_done = sem("up_done")
        silu_done = sem("silu_done")
        hid_ready = sem("hid_ready")
        hid_turned = sem("hid_turned")
        hid_kept = sem("hid_kept")
        down_done = sem("down_done")
        y_kept = sem("y_kept")
        scattered = sem("scattered")
        weighed, final_scale, final_set, final_set_v = map(sem, ("weighed", "final_scale", "final_set", "final_set_v"))
        out_stored = sem("out_stored")

        def loads_before(slot, l):
            return l * len([e for e in range(NE) if ORDER[e % 3] == slot])

        def by_group(heads, grp):
            return heads[:, :].rearrange("p (a g h) -> p a g h", a=TT, g=2)[:, :, grp, :]

        pass_count = {}

        def over_experts(eng, l, expert, counts_ready):
            if l == 0:
                pass_count[eng.engine] = eng.alloc_register(f"passes_{eng.engine.name}")
                eng.reg_mov(pass_count[eng.engine], 0)
            n = pass_count[eng.engine]
            counts_ready()

            def one(e, slot, loads):
                tokens = eng.value_load(counts[0:1, bass.ds(e, 1)], min_val=0, max_val=T)

                def passes(body):
                    with eng.Fori(0, tokens, PASS) as base:
                        body(base, eng.snap(n, min_val=0, max_val=2 * NE * T // PASS))
                        eng.reg_add(n, n, 1)

                expert(e, slot, loads, passes)

            with eng.Fori(0, NE // 3) as i:
                for s in range(3):
                    one(3 * i + s, ORDER[s], loads_before(ORDER[s], l) + 1 + i)
            for e in range(NE // 3 * 3, NE):
                one(e, ORDER[e % 3], loads_before(ORDER[e % 3], l) + 1 + e // 3)
            return eng.snap(n, min_val=0, max_val=2 * NE * T // PASS)

        block = ctx.enter_context(nc.Block())

        @block.sync
        def _(sp_q):
            for a in range(TT):
                sp_q.dma_start(x[:, a, :], x_in[0, a * P:(a + 1) * P, :]).then_inc(x_loaded[a], 16)

            def piece(name, unit, w_in, cols, width=512):
                slot, at = (2, LOW_AT) if unit is None else UNITS[unit]
                dst = weights[:, slot, at:at + KC * width].rearrange("p (k c) -> p k c", k=KC)
                src = w_in[0, :, cols:cols + width].rearrange("(p k) c -> p k c", k=KC)
                if name in SPLIT:
                    for half in range(2):
                        part = slice(half * KC // 2, (half + 1) * KC // 2)
                        sp_q.dma_start(dst[:, part, :], src[:, part, :]).then_inc(half_loaded[name, half], 16)
                else:
                    sp_q.dma_start(dst, src).then_inc(piece_loaded[name], 16)

            def out_half(name, unit, w_out, first, half):
                slot, at = UNITS[unit]
                dst = weights[:, slot, at + half * HALF:at + (half + 1) * HALF].rearrange("p (k c) -> p k c", k=2)
                first += 2 * half
                src = w_out[0, first * P:(first + 2) * P, :].rearrange("(k p) c -> p k c", p=P)
                sp_q.dma_start(dst, src).then_inc(half_loaded[name, half], 16)

            def out_weights(name, unit, w_out, first):
                slot, at = UNITS[unit]
                dst = weights[:, slot, at:at + PIECE].rearrange("p (k c) -> p k c", k=4)
                src = w_out[0, first * P:(first + 4) * P, :].rearrange("(k p) c -> p k c", p=P)
                sp_q.dma_start(dst, src).then_inc(piece_loaded[name], 16)

            passes = sp_q.alloc_register("passes_SP")
            sp_q.reg_mov(passes, 0)

            def up_to(e):
                tokens = sp_q.value_load(counts[0:1, bass.ds(e, 1)], min_val=0, max_val=T)
                with sp_q.Fori(0, tokens, PASS):
                    sp_q.reg_add(passes, passes, 1)
                return sp_q.snap(passes, min_val=1, max_val=2 * NE * T // PASS)

            def up_of(slot):
                return weights[:, slot, 0:2 * PIECE].rearrange("p (k w f) -> p k w f", k=KC, w=2)

            def load_up(l, e, slot):
                for w, src in enumerate((moe_w1, moe_w3)):
                    sp_q.dma_start(up_of(slot)[:, :, w, :], src[l, bass.ds(e, 1)].rearrange("o (p k) f -> p (o k) f", k=KC)
                                   ).then_inc(up_loaded[slot], 16)

            def load_down(l, e, slot):
                down = weights[:, slot, 2 * PIECE:].rearrange("p (c d) -> p c d", c=Q)
                sp_q.dma_start(down, moe_w2[l, bass.ds(e, 1)].rearrange("o (c p) d -> p (o c) d", p=P)
                               ).then_inc(down_loaded[slot], 16)

            def early_up(l):
                for w, src in enumerate((moe_w1, moe_w3)):
                    sp_q.dma_start(up_of(ORDER[2])[:, KC // 2:, w, :],
                                   src[l, 2].rearrange("(p k) f -> p k f", k=KC)[:, KC // 2:, :]).then_inc(up_early, 16)

            def first_experts(l):
                load_up(l, 0, ORDER[0])
                load_down(l, 0, ORDER[0])
                sp_q.wait_ge(*step_done.at(l, last_step(l, ("even_out0", "odd_out1")[l])))
                for w, src in enumerate((moe_w1, moe_w3)):
                    sp_q.dma_start(up_of(ORDER[2])[:, :KC // 2, w, :],
                                   src[l, 2].rearrange("(p k) f -> p k f", k=KC)[:, :KC // 2, :]).then_inc(up_loaded[ORDER[2]], 16)
                sp_q.wait_ge(*mix_ready.at(l, 4))
                load_up(l, 1, ORDER[1])
                load_down(l, 1, ORDER[1])

            def take_over(l, e, slot, before):
                sp_q.wait_ge(up_done, before)
                load_up(l, e, slot)
                sp_q.wait_ge(down_done, before)
                load_down(l, e, slot)

            def load_experts(l):
                sp_q.wait_ge(*routed.at(l, 2))
                with sp_q.Fori(1, NE // 3) as i:
                    for s in range(3):
                        take_over(l, 3 * i + s, ORDER[s], up_to(3 * i + (s - 3)))
                for e in range(NE // 3 * 3, NE):
                    take_over(l, e, ORDER[e % 3], up_to(e - 3))

            C = EVEN_COLS
            sp_q.dma_start(consts[:, 0:P], shape_consts[:, 0:P]).then_inc(ident_loaded, 16)
            sp_q.dma_start(vecs[:, :], vectors).then_inc(vecs_loaded, 16)
            piece("a_f", 0, even_w_in, C["a_f"])
            piece("a_q", 1, even_w_in, C["a_q"])
            piece("b_low", None, even_w_in, C["b_low"], P)
            sp_q.dma_start(w_up, gla_w_up[0]).then_inc(w_up_loaded, 16)
            piece("b_qk", 2, even_w_in, C["b_qk"])
            sp_q.dma_start(masks_wide, masks_in).then_inc(masks_loaded, 16)
            piece("a_i", 3, even_w_in, C["a_i"])
            sp_q.dma_start(consts[:, P:], shape_consts[:, P:]).then_inc(consts_loaded, 16)
            sp_q.wait_ge(*step_done.at(0, last_step(0, "a_f")))
            piece("b_v", 0, even_w_in, C["b_v"])
            sp_q.wait_ge(*step_done.at(0, last_step(0, "a_q")))
            piece("a_g", 1, even_w_in, C["a_g"])
            sp_q.wait_ge(*step_done.at(0, last_step(0, "b_qk")))
            load_down(0, 2, ORDER[2])
            sp_q.wait_ge(*step_done.at(0, last_step(0, "a_i")))
            piece("b_r", 3, even_w_in, C["b_r"])
            sp_q.wait_ge(*step_done.at(0, last_step(0, "b_v")))
            out_weights("even_out0", 0, even_w_out, 0)
            sp_q.wait_ge(*step_done.at(0, last_step(0, "a_g")))
            early_up(0)
            for half in range(2):
                sp_q.wait_ge(*step_done.at(0, last_step(0, "b_r") - 1 + half))
                out_half("even_out1", 3, even_w_out, 4, half)
            sp_q.wait_ge(*heads_mean.at(0, 2))
            first_experts(0)
            load_experts(0)
            C = ODD_COLS
            sp_q.wait_ge(down_done, up_to(NE - 3))
            piece("d_x", 0, odd_w_in, C["d_x"])
            piece("c_qk", 1, odd_w_in, C["c_qk"])
            piece("d_gate", 2, odd_w_in, C["d_gate"])
            up_to(NE - 2)
            sp_q.wait_ge(down_done, up_to(NE - 1))
            piece("c_g", 3, odd_w_in, C["c_g"])
            sp_q.wait_ge(*step_done.at(1, last_step(1, "d_x")))
            piece("c_v", 0, odd_w_in, C["c_v"])
            sp_q.wait_ge(*step_done.at(1, last_step(1, "c_qk")))
            early_up(1)
            sp_q.wait_ge(*step_done.at(1, last_step(1, "d_gate")))
            load_down(1, 2, ORDER[2])
            sp_q.wait_ge(*step_done.at(1, last_step(1, "c_v")))
            out_weights("odd_out1", 0, odd_w_out, 4)
            sp_q.wait_ge(ret_kept, 4)
            sp_q.dma_start(const("rope"), norm_final.rearrange("(o d) -> o d", o=1).to_broadcast([P, D])).then_inc(final_w_loaded, 16)
            for half in range(2):
                sp_q.wait_ge(*step_done.at(1, last_step(1, "c_g") - 1 + half))
                out_half("odd_out0", 3, odd_w_out, 0, half)
            sp_q.wait_ge(*heads_mean.at(1, 1))
            sp_q.wait_ge(*y_rest.at(1, 4))
            first_experts(1)
            load_experts(1)

        @block.gpsimd
        def _(pool):
            pool.memset(restart, 1.0).then_inc(pool_set, 1)
            pool.wait_ge(pool_set, 1)
            pool.memset(restart.rearrange("p (n t) -> p n t", t=P)[:, :, 0:1], 0.0).then_inc(pool_set, 1)
            pool.memset(zeros[:, :], 0.0).then_inc(pool_set, 1)
            pool.memset(w_rg[:, :, :, :], 0.0).then_inc(pool_set, 1)
            pool.wait_ge(pool_set, 4)
            for g, w in enumerate((rglru_w_r, rglru_w_i)):
                for half in range(2):
                    pool.dma_start(w_rg[64 * half:64 * half + 64, g, :, 64 * half:64 * half + 64],
                                   w[0, half:8:2].rearrange("m d e -> d m e")).then_inc(rg_loaded, 16)

            def first_half(l):
                _, raw_w, lo, hi = step_parts(l, 1)
                part = slice(0, HALF // 2)
                pool.wait_ge(*hi_set.at(l, 1))
                pool.tensor_tensor(lo[:, part], raw_w[:, part], hi[:, part].bitcast(F32), ALU.subtract).then_inc(first_rest, 1)

            first_half(0)
            pool.wait_ge(masks_loaded, 16)
            pool.tensor_copy(masks[:, :], masks_wide).then_inc(masks_set, 1)
            for l in range(2):
                if l:
                    first_half(l)
                for i in POOL_STEPS[l]:
                    _, raw_w, lo, hi = step_parts(l, i)
                    pool.wait_ge(*hi_set.at(l, i))
                    pool.tensor_tensor(lo, raw_w, hi.bitcast(F32), ALU.subtract).then_inc(lo_set_pool.sem, 1)

        @block.tensor
        def _(pe):
            def turn_tokens(s):
                pe.wait_ge(*normed.at(s, 2))
                for b in range(4):
                    for k in (2 * b, 2 * b + 1):
                        for a in range(TT):
                            at = (k % 2) * T + a * P
                            ins = pe.transpose(bank[4 + b][:, at:at + P], tok[:, a, k * P:(k + 1) * P], ident)
                    ins.then_inc(turned.sem, 1)

            def wait_act(l, b):
                pe.wait_ge(*(scaled_a.at(l, 4) if b else scaled_v.at(l, 2)))
                pe.wait_ge(act_rest, 8 * l + 4 * (b + 1))

            def three(dst, a_hi, a_lo, b_hi, b_lo, start, stop):
                pe.matmul(dst, a_hi, b_hi, start=start, stop=False)
                pe.matmul(dst, a_hi, b_lo, start=False, stop=False)
                return pe.matmul(dst, a_lo, b_hi, start=False, stop=stop)

            def by_channel(l, i, banks):
                name, _, lo, hi = step_parts(l, i)
                half, width = STEPS[l][i - 1][2], P if name == "b_low" else 512
                pe.wait_ge(*rest_is_set(l, i))
                if i == 1:
                    pe.wait_ge(first_rest, l + 1)
                n = lo.shape[1] // width
                for m, b in enumerate(banks):
                    for j in range(n):
                        k, cols = half * n + j, slice(j * width + m * P, j * width + m * P + P)
                        ins = three(bank[b][:, 0:T], hi[:, cols], lo[:, cols], act_hi[:, k, :], act_lo[:, k, :],
                                    k == 0, k == KC - 1)
                ins.then_inc(step_done.sem, 1)

            def by_token(l, i, banks, midway=None):
                _, _, lo, hi = step_parts(l, i)
                half = STEPS[l][i - 1][2]
                pe.wait_ge(*rest_is_set(l, i))
                for a, b in enumerate(banks):
                    if midway and a:
                        midway()
                    for j in range(4):
                        k, cols, rows = half * 4 + j, slice(j * 512, (j + 1) * 512), slice(a * P, (a + 1) * P)
                        ins = three(bank[b][:, :], act_hi[:, k, rows], act_lo[:, k, rows], hi[:, cols], lo[:, cols],
                                    k == 0, k == KC - 1)
                ins.then_inc(step_done.sem, 1)

            def turn_y(l, first, at_bank):
                for b in range(2):
                    for j in range(2):
                        k = first + 2 * b + j
                        for a in range(TT):
                            at = j * T + a * P
                            ins = pe.transpose(bank[at_bank + b][:, at:at + P], gates[:, a, k * P:(k + 1) * P], ident)
                    ins.then_inc(y_turned.sem, 1)

            def project_out(l, i, first=False, midway=None):
                name, _, lo, hi = step_parts(l, i)
                pe.wait_ge(*rest_is_set(l, i))
                for g, (a, h) in enumerate(GROUPS):
                    if midway and g == 2:
                        midway()
                    for j in range(2):
                        k = 4 * int(name[-1]) + 2 * STEPS[l][i - 1][2] + j
                        cols, rows = slice(j * D + h * 512, j * D + h * 512 + 512), slice(a * P, (a + 1) * P)
                        ins = three(bank[OUT_BANKS[l][g]][:, :], y_hi[:, k, rows], y_lo[:, k, rows], hi[:, cols], lo[:, cols],
                                    first and j == 0, False)
                ins.then_inc(step_done.sem, 1)

            def finish_out(l, i):
                name, _, lo, hi = step_parts(l, i)
                w = vec("w_route", l * KC * ROUTE, (l + 1) * KC * ROUTE).rearrange("p (k g) -> p k g", k=KC)
                logits = bank[OUT_BANKS[l][0]]

                def group(g):
                    a, h = GROUPS[g]
                    for j in range(2):
                        k = 4 * int(name[-1]) + 2 * STEPS[l][i - 1][2] + j
                        cols, rows = slice(j * D + h * 512, j * D + h * 512 + 512), slice(a * P, (a + 1) * P)
                        ins = three(bank[OUT_BANKS[l][g]][:, :], y_hi[:, k, rows], y_lo[:, k, rows], hi[:, cols], lo[:, cols],
                                    False, j == 1)
                    ins.then_inc(mix_ready.sem, 1)

                def turn(g):
                    a, h = GROUPS[g]
                    pe.wait_ge(*x_added.at(2 * l, g + 1))
                    for k in range(4):
                        at = h * 512 + k * P
                        ins = pe.transpose(bank[TURN_BANKS[l][g]][:, k * P:(k + 1) * P], x[:, a, at:at + P], ident)
                    ins.then_inc(x_turned.sem, 1)

                def logits_of(h):
                    for k in range(4 * h, 4 * h + 4):
                        ins = pe.matmul(logits[0:ROUTE, 0:T], w[:, k, :], act_T[:, k, :], start=(k == 0), stop=(k == KC - 1))
                    return ins

                pe.wait_ge(*rest_is_set(l, i))
                group(0)
                group(1)
                turn(0)
                group(2)
                turn(1)
                group(3)
                turn(2)
                pe.wait_ge(w_folded, l + 1)
                pe.wait_ge(*x_kept_v.at(l, 2))
                logits_of(0)
                turn(3)
                pe.wait_ge(*x_kept_v.at(l, 3))
                pe.wait_ge(*x_kept_a.at(l, 1))
                logits_of(1).then_inc(logits_ready.sem, 1)
                pe.wait_ge(*logits_kept.at(l, 1))
                for a in range(TT):
                    ins = pe.transpose(bank[OUT_BANKS[l][1]][:, a * 64:a * 64 + ROUTE], logits_T[:, a * P:(a + 1) * P],
                                       ident[0:ROUTE, 0:ROUTE])
                ins.then_inc(logits_turned.sem, 1)

            def zero(b):
                pe.matmul(bank[b][:, :], zeros[:, 0:P], zeros[:, :], start=True, stop=True, skip_group_check=True)

            def keep_warm(n, b):
                for _ in range(n):
                    zero(b)

            def even_mixer():
                for i in (1, 2):
                    wait_act(0, i - 1)
                    by_channel(0, i, range(4))
                for i in (3, 4):
                    by_channel(0, i, range(4, 8))
                pe.wait_ge(sig_done, 4)
                by_channel(0, 5, (0,))
                pe.wait_ge(aq_kept, 4)
                by_channel(0, 6, range(4, 8))
                pe.wait_ge(low_kept, 1)
                pe.wait_ge(w_up_loaded, 16)
                for m in range(2):
                    ins = pe.matmul(bank[1][:, m * T:(m + 1) * T], w_up[:, m * P:(m + 1) * P], low, start=True, stop=True)
                ins.then_inc(z_ready, 1)
                by_channel(0, 7, range(4, 8))

                def project(i, midway=None):
                    if i == 8:
                        pe.wait_ge(bqk_kept, 2)
                    elif i % 2 == 0:
                        pe.wait_ge(*proj_kept.at(0, i - 8))
                    by_token(0, i, (4, 5), midway)

                def scores(i):
                    A = decA[i % 2].rearrange("p (h t) -> p h t", h=HEADS)
                    B = decB[i % 2].rearrange("p (m t) -> p m t", m=2)
                    keysA, keysB, queriesA, queriesB = A, B, A, B
                    if i == 0:
                        keysA, queriesA = (z.rearrange("p (h t) -> p h t", h=HEADS) for z in (kA, qA))
                        keysB, queriesB = (z.rearrange("p (m t) -> p m t", m=2) for z in (kB, qB))
                        pe.wait_ge(key_ready, 1)
                        pe.wait_ge(bqk_kept, 4)
                        pe.wait_ge(z_set, 2)
                    else:
                        pe.wait_ge(decayed, 4 * (i - 1) + 2)
                    if i > 1:
                        pe.wait_ge(scores_kept, 4 * (i - 2) + 2)
                    cross = i == len(LEVELS) + 1
                    tiles = (0,) if cross else range(TT)
                    for a in tiles:
                        for h in range(HEADS):
                            t0 = P if cross else a * P
                            ins = pe.matmul(bank[6 * (i % 2) + a][:, h * P:(h + 1) * P], keysA[:, h, a * P:(a + 1) * P],
                                            queriesA[:, h, t0:t0 + P], start=True, stop=True)
                        ins.then_inc(scores_ready, 1)
                    if i:
                        pe.wait_ge(decayed, 4 * i)
                    if cross:
                        pe.wait_ge(scores_kept, 4 * (i - 1) + 2)
                    elif i:
                        pe.wait_ge(scores_kept, 4 * i)
                    for a in tiles:
                        for m in range(2):
                            for parity in range(2):
                                rows = slice(64 * parity, 64 * parity + 64)
                                at = (a * 2 + m) * P
                                t0 = P if cross else a * P
                                ins = pe.matmul(bank[2 + parity][:, at:at + P], keysB[rows, m, a * P:(a + 1) * P],
                                                queriesB[rows, m, t0:t0 + P], start=True, stop=True)
                                if a == tiles[-1] and m == 1:
                                    ins.then_inc(scores_ready, 1)

                for i in range(len(LEVELS) + 2):
                    if i in PROJECT_AT:
                        project(8 + PROJECT_AT.index(i))
                    scores(i)

                SAv = SA.rearrange("p (b h t) -> p b h t", b=3, h=HEADS)
                SBv = SB.rearrange("p (q b m t) -> p q b m t", q=2, b=3, m=2)
                pe.wait_ge(scores_kept, 4 * 8)
                pe.wait_ge(cross_kept, 3)
                pe.wait_ge(*proj_kept.at(0, 4))
                for grp in range(2):
                    for a in range(TT):
                        for h in range(HEADS):
                            blocks = [(0, 0)] if a == 0 else [(2, 0), (1, 1)]
                            for j, (b, src) in enumerate(blocks):
                                S = SAv[:, b, h, :] if grp == 0 else SBv[:, h % 2, b, h // 2, :]
                                v = tok[:, src, grp * 512 + h * P:grp * 512 + (h + 1) * P]
                                ins = pe.matmul(bank[2 * a + grp][:, h * P:(h + 1) * P], S, v,
                                                start=(j == 0), stop=(j == len(blocks) - 1))
                        ins.then_inc(heads_ready.sem, 1)
                def turn_first():
                    pe.wait_ge(*y_ready.at(0, 8))
                    turn_y(0, 0, 6)

                def turn_second():
                    pe.wait_ge(*y_ready.at(0, 16))
                    turn_y(0, 4, 6)

                project(15, turn_first)
                pe.wait_ge(*y_rest.at(0, 4))
                project_out(0, 16, first=True, midway=lambda: pe.wait_ge(*proj_kept.at(0, 8)))
                project_out(0, 17, midway=turn_second)
                pe.wait_ge(*y_rest.at(0, 8))
                project_out(0, 18)
                finish_out(0, 19)

            def odd_mixer():
                for i in (1, 2):
                    wait_act(1, i - 1)
                    by_channel(1, i, range(4))
                for i in (3, 4):
                    by_channel(1, i, range(4, 8))
                pe.wait_ge(rg_loaded, 64)
                pe.wait_ge(conv_done, 4)
                for g in range(2):
                    for m in range(4):
                        ins = pe.matmul(bank[2 * g + m // 2][:, m % 2 * T:m % 2 * T + T], w_rg[:, g, m, :],
                                        xc[:, m * T:(m + 1) * T], start=True, stop=True)
                    ins.then_inc(rg_ready, 1)
                pe.wait_ge(qk_kept, 4)
                for j in range(2):
                    pe.matmul(bank[4 + j][:, :], const("swap"), raw[:, j * 512:(j + 1) * 512],
                              start=True, stop=True).then_inc(swapped, 1)
                pe.wait_ge(rg_gated, 4)
                for i in (5, 6):
                    by_channel(1, i, (6, 7, 0, 1))
                rotv = rot.rearrange("p (z m t) -> p z m t", z=2, m=2)
                pe.wait_ge(rg_gated, 8)
                pe.wait_ge(rotated, 1)
                for b, (s0, t0) in enumerate(((0, 0), (P, P), (0, P))):
                    for m in range(2):
                        for parity in range(2):
                            rows = slice(64 * parity, 64 * parity + 64)
                            at = (b % 2 * 2 + m) * P
                            ins = pe.matmul(bank[(4 if b == 2 else 2) + parity][:, at:at + P], rotv[rows, 1, m, s0:s0 + P],
                                            rotv[rows, 0, m, t0:t0 + P], start=True, stop=True)
                            if b and m == 1:
                                ins.then_inc(ret_ready, 1)
                pe.wait_ge(dg_kept, 4)
                for i in (7, 8):
                    by_token(1, i, (6, 7))
                by_token(1, 9, (0, 1))
                SCv = SC.rearrange("p (q b m t) -> p q b m t", q=2, b=3, m=2)
                pe.wait_ge(ret_kept, 4)
                pe.wait_ge(*proj_kept.at(1, 2))
                for a in range(TT):
                    for h in range(HEADS):
                        blocks = [(0, 0)] if a == 0 else [(2, 0), (1, 1)]
                        for j, (b, src) in enumerate(blocks):
                            ins = pe.matmul(bank[2 + a][:, h * P:(h + 1) * P], SCv[:, h % 2, b, h // 2, :],
                                            tok[:, src, h * P:(h + 1) * P], start=(j == 0), stop=(j == len(blocks) - 1))
                    ins.then_inc(heads_ready.sem, 1)
                by_token(1, 10, (0, 1))
                pe.wait_ge(*y_rest.at(1, 4))
                project_out(1, 11, first=True)

                def turn_retention():
                    pe.wait_ge(*y_ready.at(1, 8))
                    pe.wait_ge(*proj_kept.at(1, 4))
                    turn_y(1, 0, 0)

                project_out(1, 12, midway=turn_retention)
                pe.wait_ge(*y_rest.at(1, 8))
                project_out(1, 13)
                finish_out(1, 14)

            def route(l):
                keep_warm(20, 4)
                pe.wait_ge(*chosen_set.at(l, 1))
                pe.wait_ge(consts_loaded, 16)
                pe.matmul(bank[5][:, 0:NE], const("before"), chosen[:, 0, :], start=True, stop=True)
                pe.matmul(bank[5][:, NE:2 * NE], const("before"), chosen[:, 1, :], start=True, stop=False)
                pe.matmul(bank[5][:, NE:2 * NE], const("ones"), chosen[:, 0, :], start=False, stop=True)
                pe.matmul(bank[5][:, 64:64 + NE], const("ones"), chosen[:, 0, :], start=True, stop=False)
                pe.matmul(bank[5][:, 64:64 + NE], const("ones"), chosen[:, 1, :], start=False, stop=True).then_inc(ranks_ready.sem, 1)

            def experts(l):
                def start():
                    keep_warm(4, 4)
                    pe.wait_ge(*routed.at(l, 2))
                    pe.wait_ge(*normed.at(2 * l + 1, 2))
                    pe.wait_ge(up_early, 32 * (l + 1))
                    for q in range(Q):
                        zero(q)

                def expert(e, slot, loads, passes):
                    up = weights[:, slot, 0:2 * PIECE].rearrange("p (k w f) -> p k w f", k=KC, w=2)
                    down = weights[:, slot, 2 * PIECE:].rearrange("p (c d) -> p c d", c=Q)

                    def body(base, n):
                        pe.wait_ge(picked, 2 * n + 2)
                        for a in range(TT):
                            for q in range(Q):
                                ins = pe.matmul(bank[4][PASS * q:PASS * (q + 1), 0:T], pick[:, a, :], tok[:, a, q * T:(q + 1) * T],
                                                start=(a == 0), stop=(a == TT - 1), tile_position=(0, PASS * q), skip_group_check=True)
                        ins.then_inc(gathered, 1)
                        pe.wait_ge(spread_set, 2 * n + 2)
                        for a in range(TT):
                            ins = pe.transpose(bank[7][:, T + a * P:T + (a + 1) * P], spread[:, a, :], ident)
                        ins.then_inc(spread_turned, 1)
                        pe.wait_ge(got_kept, n + 1)
                        for s in range(2):
                            ins = pe.transpose(bank[5][:, s * P:(s + 1) * P], got[:, s * P:(s + 1) * P], ident)
                        ins.then_inc(got_turned, 1)
                        pe.wait_ge(got_scaled, n + 1)
                        pe.wait_ge(up_loaded[slot], 32 * loads)
                        for k in range(KC):
                            for j in range(Q):
                                ins = pe.matmul(bank[6][PASS * j:PASS * (j + 1), 0:T], got_T[:, k % 2, k // 2, :],
                                                up[:, k, :, j * P:(j + 1) * P], start=(k == 0), stop=(k == KC - 1),
                                                tile_position=(0, PASS * j), skip_group_check=True)
                        ins.then_inc(up_done, 1)
                        pe.wait_ge(hid_ready, n + 1)
                        pe.wait_ge(spread_kept, n + 1)
                        pe.transpose(bank[7][:, 0:P], hid[:, :], ident).then_inc(hid_turned, 1)
                        pe.wait_ge(hid_kept, n + 1)
                        pe.wait_ge(down_loaded[slot], 16 * loads)
                        for c in range(Q):
                            for q in range(Q):
                                ins = pe.matmul(bank[7][PASS * q:PASS * (q + 1), T:2 * T], hid_T[:, c, :],
                                                down[:, c, q * T:(q + 1) * T], start=(c == 0), stop=(c == Q - 1),
                                                tile_position=(0, PASS * q), skip_group_check=True)
                        ins.then_inc(down_done, 1)
                        pe.wait_ge(y_kept, n + 1)
                        for a in range(TT):
                            for q in range(Q):
                                rows = slice(PASS * q, PASS * (q + 1))
                                ins = pe.matmul(bank[q][:, a * T:(a + 1) * T], spread_T[rows, a * P:(a + 1) * P], y_tok[rows, :],
                                                start=False, stop=True, tile_position=(PASS * q, 0), skip_group_check=True)
                        ins.then_inc(scattered, 1)

                    passes(body)

                over_experts(pe, l, expert, start)

            pe.wait_ge(pool_set, 3)
            keep_warm(22, 0)
            pe.wait_ge(ident_loaded, 16)
            turn_tokens(0)
            keep_warm(12, 0)
            even_mixer()
            route(0)
            experts(0)
            keep_warm(26, 5)
            turn_tokens(2)
            keep_warm(5, 0)
            odd_mixer()
            route(1)
            experts(1)

        @block.scalar
        def _(act):
            steps = [0]

            def link(ins):
                steps[0] += 1
                ins.then_inc(scalar_step, 1)
                act.wait_ge(scalar_step, steps[0])

            def f(out_, in_, fn, **kw):
                return act.activation(out_, in_, fn, **kw)

            def square(s, a):
                f(tok[:, a, :], x[:, a, :], ACT.Square, accum_out=sums[:, a:a + 1]).then_inc(squared.sem, 1)

            def norm_root(s):
                act.wait_ge(*mean_set.at(s, 1))
                f(root[:, :], sums[:, :], ACT.Sqrt).then_inc(rooted.sem, 1)

            def norm(s):
                act.wait_ge(pool_set, 3)
                act.activation(spare[:, s // 2:s // 2 + 1], zeros[:, 0:1], ACT.Sqrt)
                for a in range(TT):
                    if s:
                        act.wait_ge(*x_added.at(s - 1, 2 * a + 2))
                    else:
                        act.wait_ge(x_loaded[a], 16)
                    square(s, a)
                norm_root(s)

            def norm_route(l):
                s = 2 * l + 1
                act.wait_ge(*x_added.at(s - 1, 3))
                square(s, 0)
                act.wait_ge(*x_turned.at(l, 3))
                put_turned(l, 2, act.copy).then_inc(x_kept_a.sem, 1)
                act.wait_ge(*x_added.at(s - 1, 4))
                square(s, 1)
                norm_root(s)
                act.wait_ge(*scale_set.at(l, 1))
                for a in range(TT):
                    f(tok[:, a, :].rearrange("p (k c) -> p c k", k=KC), x[:, a, :].rearrange("p (c k) -> p c k", k=KC),
                      ACT.Copy, scale=scale[:, a:a + 1]).then_inc(normed.sem, 1)

            def norm_scale(s, w):
                for b in (2, 3):
                    act.wait_ge(*turned.at(s // 2, b + 1))
                    for k in (2 * b, 2 * b + 1):
                        f(act_hi[:, k, :], bank[4 + b][:, k % 2 * T:k % 2 * T + T], ACT.Copy,
                          scale=w[:, k:k + 1]).then_inc(scaled_a.sem, 1)

            def y_scale(l, b, at_bank, w):
                act.wait_ge(*y_turned.at(l, b + 1))
                for k in (2 * b, 2 * b + 1):
                    f(y_hi[:, k, :], bank[at_bank][:, k % 2 * T:k % 2 * T + T], ACT.Copy,
                      scale=w[:, k:k + 1]).then_inc(y_scaled_a.sem, 1)

            def round_step(l, i):
                name, raw_w, _, hi = step_parts(l, i)
                act.wait_ge(half_loaded[name, STEPS[l][i - 1][2]] if name in SPLIT else piece_loaded[name], 16)
                before = [j for j in range(1, i) if buffer_of(l, j) == buffer_of(l, i)]
                if before:
                    act.wait_ge(*step_done.at(l, before[-1]))
                act.copy(hi, raw_w).then_inc(hi_set.sem, 1)

            def even_mixer():
                round_step(0, 3)
                act.wait_ge(*step_done.at(0, 2))
                for m in range(4):
                    f(kA[:, m * T:(m + 1) * T], bank[m][:, 0:T], ACT.Sigmoid).then_inc(sig_done, 1)
                for i in (4, 5, 6):
                    round_step(0, i)
                act.wait_ge(*step_done.at(0, 4))
                for m in range(4):
                    act.copy(qA[:, m * T:(m + 1) * T], bank[4 + m][:, 0:T]).then_inc(aq_kept, 1)
                act.wait_ge(*step_done.at(0, 5))
                act.copy(low, bank[0][0:16, 0:T]).then_inc(low_kept, 1)
                round_step(0, 7)
                act.wait_ge(f_ready, 4)
                f(decA[0], kA, ACT.Ln).then_inc(f_logged, 1)
                round_step(0, 8)
                act.wait_ge(z_set, 2)
                f(decB[0], bB, ACT.Abs).then_inc(z_abs, 1)
                act.wait_ge(z_abs, 1)
                f(decB[0], decB[0], ACT.Exp, scale=-1.0).then_inc(z_exped, 1)
                act.wait_ge(z_exped, 1)
                f(decB[0], decB[0], ACT.Ln, bias=1.0).then_inc(z_logged, 1)
                act.wait_ge(*step_done.at(0, 7))
                for m in range(4):
                    dst = (qB, kB)[m // 2][:, m % 2 * T:m % 2 * T + T]
                    f(dst, bank[4 + m][:, 0:T], ACT.Copy, scale=(64.0 ** -0.5, 1.0)[m // 2]).then_inc(bqk_kept, 1)
                round_step(0, 9)

                def keep(g):
                    act.wait_ge(*step_done.at(0, 9 + 2 * g))
                    dst, at = ((tok, 0), (tok, 512), (gates, 0))[g]
                    for a in range(TT):
                        act.copy(dst[:, a, at:at + 512], bank[4 + a][:, :]).then_inc(proj_kept.sem, 1)

                for i in range(1, len(LEVELS) + 2):
                    h = (LEVELS + (P,))[i - 1]
                    if i in (2, 4):
                        keep(i // 2 - 1)
                    for buf, b_run, j in ((decA[i % 2], bA, 1), (decB[i % 2], bB, 2)):
                        act.wait_ge(gap_ready, 2 * (i - 1) + j)
                        v = buf.rearrange("p (n c) -> p n c", c=2 * h)
                        if h == P:
                            first, scale_first = v[:, :, 0:h], 1.0
                            second = b_run.rearrange("p (n c) -> p n c", c=2 * h)[:, :, h:]
                        else:
                            first, scale_first, second = v[:, :, 0:h], -1.0, v[:, :, h:]
                        f(v[:, :, h:], second, ACT.Exp).then_inc(gap_exped, 1)
                        f(v[:, :, 0:h], first, ACT.Exp, scale=scale_first).then_inc(gap_exped, 1)
                    if i == 6:
                        keep(2)
                    if i < 7:
                        round_step(0, 9 + i)
                round_step(0, 16)
                for j, (dst, src) in enumerate(((SA[:, 1024:1536], bank[0][:, :]), (SB[:, 512:768], bank[2][:, 0:256]),
                                                (SB[:, 1280:1536], bank[3][:, 0:256]))):
                    act.wait_ge(scores_ready, 4 * (len(LEVELS) + 1) + j + 1)
                    act.copy(dst, src).then_inc(cross_kept, 1)
                act.wait_ge(*proj_kept.at(0, 6))
                f(gates[:, :, 0:512], gates[:, :, 0:512], ACT.Silu).then_inc(gates_open, 1)
                act.wait_ge(scores_ready, 35)
                act.wait_ge(decayed, 32)
                for grp in range(2):
                    for a in range(TT):
                        b = 2 * a + grp
                        act.wait_ge(*heads_ready.at(0, 2 * grp + a + 1))
                        f(work(4608 + 512 * b, 512), bank[b][:, :], ACT.Square).then_inc(heads_squared.sem, 1)
                    if grp == 0:
                        act.wait_ge(*heads_mean.at(0, 1))
                        f(by_group(head_r, 0), by_group(head_ss, 0), ACT.Sqrt).then_inc(heads_root.sem, 1)
                act.wait_ge(*heads_mean.at(0, 2))
                f(by_group(head_r, 1), by_group(head_ss, 1), ACT.Sqrt).then_inc(heads_root.sem, 1)
                y_scale(0, 1, 7, vec("even_w"))
                act.wait_ge(*step_done.at(0, 15))
                for a in range(TT):
                    f(gates[:, a, 512:1024], bank[4 + a][:, :], ACT.Silu).then_inc(proj_kept.sem, 1)
                for i in (17, 18):
                    round_step(0, i)
                y_scale(0, 3, 7, vec("even_w"))
                round_step(0, 19)

            def odd_mixer():
                round_step(1, 3)
                act.wait_ge(*step_done.at(1, 2))
                for m in range(4):
                    act.copy(dx[:, m, 3:3 + T], bank[m][:, 0:T]).then_inc(dx_kept, 1)
                for i in (4, 5):
                    round_step(1, i)
                act.wait_ge(*step_done.at(1, 4))
                for m in range(4):
                    act.copy(raw[:, m * T:(m + 1) * T], bank[4 + m][:, 0:T]).then_inc(qk_kept, 1)
                round_step(1, 6)
                for g, (dst, name) in enumerate(((rr, "b_r"), (ii, "b_i"))):
                    act.wait_ge(rg_ready, g + 1)
                    for m in range(4):
                        f(dst[:, m * T:(m + 1) * T], bank[2 * g + m // 2][:, m % 2 * T:m % 2 * T + T], ACT.Sigmoid,
                          bias=vec(name, m, m + 1)).then_inc(rg_gated, 1)
                act.wait_ge(rg_gated, 4)
                for m in range(4):
                    f(th[:, m * T:(m + 1) * T], rr[:, m * T:(m + 1) * T], ACT.Tanh, scale=sp[:, 0, m:m + 1]).then_inc(th_done, 1)
                act.wait_ge(th_done, 4)
                for m in range(4):
                    f(rr[:, m * T:(m + 1) * T], rr[:, m * T:(m + 1) * T], ACT.Exp, scale=sp[:, 6, m:m + 1]).then_inc(a_done, 1)
                round_step(1, 7)
                f(th, th, ACT.Sqrt).then_inc(th_root, 1)
                act.wait_ge(*step_done.at(1, 6))
                for m, b in enumerate((6, 7, 0, 1)):
                    act.copy(dg[:, m * T:(m + 1) * T], bank[b][:, 0:T]).then_inc(dg_kept, 1)
                round_step(1, 8)
                act.wait_ge(dg_kept, 4)
                f(gl, dg, ACT.Square).then_inc(dg_squared, 1)
                round_step(1, 9)
                act.wait_ge(dg_inner, 1)
                f(gl, gl, ACT.Tanh, scale=(2.0 / np.pi) ** 0.5).then_inc(dg_tanh, 1)
                act.wait_ge(*step_done.at(1, 8))
                for a in range(TT):
                    act.copy(tok[:, a, 0:512], bank[6 + a][:, :]).then_inc(proj_kept.sem, 1)
                for i in (10, 11):
                    round_step(1, i)
                for a in range(TT):
                    act.wait_ge(centred, a + 1)
                    f(tmp[:, a * 512:(a + 1) * 512], gates[:, a, 512:1024], ACT.Square).then_inc(heads_squared.sem, 1)
                act.wait_ge(*heads_mean.at(1, 1))
                f(head_r[:, 0:8], head_ss[:, 0:8], ACT.Sqrt).then_inc(heads_root.sem, 1)
                round_step(1, 12)
                for a in range(TT):
                    f(gates[:, a, 0:512], bank[a][:, :], ACT.Silu).then_inc(proj_kept.sem, 1)
                round_step(1, 13)
                y_scale(1, 1, 1, vec("ret_w"))
                round_step(1, 14)

            def route(l):
                gd = r_small[:, :, 1, :]
                act.wait_ge(*group_gap.at(l, 1))
                f(r_small[:, :, 2, :], gd, ACT.Exp).then_inc(group_exped.sem, 1)
                act.wait_ge(*pair_gap.at(l, 1))
                f(root[:, :].unsqueeze(2), r_wide[:, 5, :, 5:6], ACT.Exp).then_inc(pair_exped.sem, 1)

            def experts(l):
                def expert(e, slot, loads, passes):
                    def body(base, n):
                        act.wait_ge(gathered, n + 1)
                        act.copy(got[:, :], bank[4][:, 0:T]).then_inc(got_kept, 1)
                        act.wait_ge(spread_turned, n + 1)
                        act.copy(spread_T[:, :], bank[7][:, T:2 * T]).then_inc(spread_kept, 1)
                        act.wait_ge(up_done, n + 1)
                        f(silu[:, :], bank[6][:, 0:P], ACT.Silu).then_inc(silu_done, 1)
                        act.wait_ge(down_done, n + 1)
                        act.copy(y_tok[:, :], bank[7][:, T:2 * T]).then_inc(y_kept, 1)

                    passes(body)

                over_experts(act, l, expert, lambda: act.wait_ge(*routed.at(l, 2)))

            norm(0)
            round_step(0, 1)
            act.wait_ge(vecs_loaded, 16)
            norm_scale(0, vec("norm_mix", 0, 8))
            round_step(0, 2)
            act.wait_ge(lb_set, 1)
            f(lb_e[:, :, :], lb_t[:, :, :], ACT.Exp).then_inc(lb_exped, 1)
            act.wait_ge(lam_set, 1)
            f(sp[:, 1, :], sp[:, 0, :], ACT.Exp, scale=-1.0).then_inc(lam_exped, 1)
            even_mixer()
            norm_route(0)
            route(0)
            experts(0)
            norm(2)
            round_step(1, 1)
            norm_scale(2, vec("norm_mix", 8, 16))
            round_step(1, 2)
            odd_mixer()
            norm_route(1)
            route(1)
            experts(1)
            norm(4)
            act.wait_ge(weighed, 1)
            act.wait_ge(final_scale, 1)
            f(tok[:, 0, :], x[:, 0, :], ACT.Copy, scale=scale[:, 0:1]).then_inc(final_set, 1)
            act.wait_ge(final_set, 1)
            act.dma_start(out[0, 0:P, :], tok[:, 0, :]).then_inc(out_stored, 16)
            act.wait_ge(final_set_v, 1)
            act.dma_start(out[0, P:2 * P, :], tok[:, 1, :]).then_inc(out_stored, 16)
            act.wait_ge(out_stored, 32)

        @block.vector
        def _(dve):
            steps = [0]

            def mark(ins):
                steps[0] += 1
                ins.then_inc(vector_step, 1)

            def link(ins):
                mark(ins)
                dve.wait_ge(vector_step, steps[0])

            ts, stt, tt = dve.tensor_scalar, dve.scalar_tensor_tensor, dve.tensor_tensor

            def norm_mean(s):
                dve.wait_ge(*squared.at(s, 2))
                ts(sums[:, :], sums[:, :], 1.0 / D, EPS, ALU.mult, ALU.add).then_inc(mean_set.sem, 1)

            def norm(s):
                norm_mean(s)
                dve.wait_ge(*rooted.at(s, 1))
                link(dve.reciprocal(scale[:, :], root[:, :]))

            def split_scaled(hi, lo, k, b, w, rest):
                stt(lo[:, k, :], bank[b][:, k % 2 * T:k % 2 * T + T], w[:, k:k + 1], hi[:, k, :].bitcast(F32),
                    ALU.mult, ALU.subtract).then_inc(rest, 1)

            def norm_tokens(s, w):
                norm(s)
                for a in range(TT):
                    ts(tok[:, a, :].rearrange("p (k c) -> p c k", k=KC), x[:, a, :].rearrange("p (c k) -> p c k", k=KC),
                       scale[:, a:a + 1], None, ALU.mult).then_inc(normed.sem, 1)
                dve.wait_ge(vecs_loaded, 16)
                if s:
                    rest_step(1, 1)
                for b in (0, 1):
                    dve.wait_ge(*turned.at(s // 2, b + 1))
                    tt(act_hi[:, 2 * b:2 * b + 2, :], bank[4 + b][:, :].rearrange("p (k t) -> p k t", k=2),
                       w[:, 2 * b:2 * b + 2].unsqueeze(2).to_broadcast([P, 2, T]), ALU.mult).then_inc(scaled_v.sem, 1)
                for b in (0, 1):
                    dve.wait_ge(*(scaled_a.at(s // 2, 4) if b else scaled_v.at(s // 2, 2)))
                    for k in range(4 * b, 4 * b + 4):
                        split_scaled(act_hi, act_lo, k, 4 + k // 2, w, act_rest)
                    if s == 0 and b == 0:
                        rest_step(0, 1)
                rest_step(s // 2, 2)

            def y_scale(l, b, at_bank, w):
                dve.wait_ge(*y_turned.at(l, b + 1))
                tt(y_hi[:, 2 * b:2 * b + 2, :], bank[at_bank][:, :].rearrange("p (k t) -> p k t", k=2),
                   w[:, 2 * b:2 * b + 2].unsqueeze(2).to_broadcast([P, 2, T]), ALU.mult).then_inc(y_scaled_v.sem, 1)
                dve.wait_ge(*y_scaled_v.at(l, b // 2 + 1))
                for k in range(2 * b, 2 * b + 4):
                    if k == 2 * b + 2:
                        dve.wait_ge(*y_scaled_a.at(l, b + 2))
                    split_scaled(y_hi, y_lo, k, at_bank + (k - 2 * b) // 2, w, y_rest.sem)

            def rest_step(l, i):
                _, raw_w, lo, hi = step_parts(l, i)
                part = slice(HALF // 2 if i == 1 else 0, None)
                dve.wait_ge(*hi_set.at(l, i))
                tt(lo[:, part], raw_w[:, part], hi[:, part].bitcast(F32), ALU.subtract).then_inc(lo_set.sem, 1)

            def finish_mix(l):
                def add(g):
                    a, h = GROUPS[g]
                    dve.wait_ge(*mix_ready.at(l, g + 1))
                    part = x[:, a, h * 512:(h + 1) * 512]
                    tt(part, part, bank[OUT_BANKS[l][g]][:, :], ALU.add).then_inc(x_added.sem, 1)

                def keep(g):
                    dve.wait_ge(*x_turned.at(l, g + 1))
                    put_turned(l, g, dve.tensor_copy).then_inc(x_kept_v.sem, 1)

                add(0)
                add(1)
                keep(0)
                add(2)
                keep(1)
                add(3)
                keep(3)
                dve.wait_ge(*squared.at(2 * l + 1, 2))
                ts(sums[:, :], sums[:, :], 1.0 / D, EPS, ALU.mult, ALU.add).then_inc(mean_set.sem, 1)
                dve.wait_ge(*rooted.at(2 * l + 1, 1))
                dve.reciprocal(scale[:, :], root[:, :]).then_inc(scale_set.sem, 1)
                dve.wait_ge(*logits_ready.at(l, 1))
                dve.tensor_copy(logits_T, bank[OUT_BANKS[l][0]][0:ROUTE, 0:T]).then_inc(logits_kept.sem, 1)

            def fold(l):
                w = vec("w_route", l * KC * ROUTE, (l + 1) * KC * ROUTE).rearrange("p (k g) -> p k g", k=KC)
                tt(w, w, vec("norm_route", l * KC, (l + 1) * KC).unsqueeze(2).to_broadcast([P, KC, ROUTE]),
                   ALU.mult).then_inc(w_folded, 1)

            def lower_bound():
                lb = vec("lb").rearrange("p (r h) -> p r h", r=3)
                link(dve.tensor_reduce(lb_e[:, 0, :], lb.rearrange("p r h -> p h r"), AX.X, ALU.max))
                tt(lb_t[:, :, :], lb, lb_e[:, 0:1, :].to_broadcast([P, 3, 4]), ALU.subtract).then_inc(lb_set, 1)
                dve.wait_ge(lb_exped, 1)
                link(dve.tensor_reduce(lb_t[:, 2, :], lb_e[:, :, :].rearrange("p r h -> p h r"), AX.X, ALU.add))
                link(dve.reciprocal(lb_t[:, 2, :], lb_t[:, 2, :]))
                link(tt(lb_t[:, 0, :], lb_e[:, 0, :], lb_t[:, 2, :], ALU.mult))
                link(ts(lb_t[:, 1, :], lb_t[:, 0, :], -1.0, 1.0, ALU.mult, ALU.add))

            def softplus_start():
                lam = vec("lam")
                link(ts(sp[:, 2, :], lam, -1.0, None, ALU.mult))
                tt(sp[:, 0, :], lam, sp[:, 2, :], ALU.max).then_inc(lam_set, 1)

            def softplus():
                dve.wait_ge(lam_exped, 1)
                link(ts(sp[:, 3, :], sp[:, 1, :], 2.0, None, ALU.add))
                link(dve.reciprocal(sp[:, 3, :], sp[:, 3, :]))
                link(tt(sp[:, 3, :], sp[:, 1, :], sp[:, 3, :], ALU.mult))
                link(tt(sp[:, 4, :], sp[:, 3, :], sp[:, 3, :], ALU.mult))
                link(ts(sp[:, 5, :], sp[:, 4, :], 1.0 / 15, 1.0 / 13, ALU.mult, ALU.add))
                for n in (11, 9, 7, 5, 3, 1):
                    link(tt(sp[:, 5, :], sp[:, 5, :], sp[:, 4, :], ALU.mult))
                    link(ts(sp[:, 5, :], sp[:, 5, :], 1.0 / n, None, ALU.add))
                link(tt(sp[:, 5, :], sp[:, 5, :], sp[:, 3, :], ALU.mult))
                link(ts(sp[:, 2, :], sp[:, 2, :], 0.0, None, ALU.max))
                link(stt(sp[:, 0, :], sp[:, 5, :], 2.0, sp[:, 2, :], ALU.mult, ALU.add))
                link(ts(sp[:, 0, :], sp[:, 0, :], RG_C / 2, None, ALU.mult))
                link(ts(sp[:, 6, :], sp[:, 0, :], -2.0, None, ALU.mult))

            def even_mixer():
                for i in (3, 4):
                    rest_step(0, i)
                dve.wait_ge(sig_done, 4)
                for h in range(HEADS):
                    ts(kA[:, h * T:(h + 1) * T], kA[:, h * T:(h + 1) * T], lb_t[:, 1, h:h + 1], lb_t[:, 0, h:h + 1],
                       ALU.mult, ALU.add).then_inc(f_ready, 1)
                for i in (5, 6):
                    rest_step(0, i)
                softplus()
                for l in range(2):
                    fold(l)
                rest_step(0, 7)
                dve.wait_ge(f_logged, 1)
                ts(kA, kA, -1.0, 1.0, ALU.mult, ALU.add).then_inc(key_ready, 1)
                dve.wait_ge(pool_set, 2)
                mark(dve.tensor_tensor_scan(bA, restart, decA[0], 0.0, ALU.mult, ALU.add))
                dve.wait_ge(z_ready, 1)
                for m in range(2):
                    ts(bB[:, m * T:(m + 1) * T], bank[1][:, m * T:(m + 1) * T], vec("gla_b", m, m + 1), None, ALU.add).then_inc(z_set, 1)
                rest_step(0, 8)
                dve.wait_ge(z_logged, 1)
                dve.wait_ge(z_set, 2)
                link(stt(decB[0], bB, 0.0, decB[0], ALU.min, ALU.subtract))
                link(ts(decB[0], decB[0], 1.0 / 16.0, None, ALU.mult))
                link(dve.tensor_tensor_scan(bB, restart[:, 0:512], decB[0], 0.0, ALU.mult, ALU.add))

                maskv = masks[:, :].rearrange("p (l t) -> p l t", l=len(LEVELS))
                SBp = [SB[:, q * 768:(q + 1) * 768] for q in range(2)]

                def keep(i, banks):
                    dsts = [SA[:, 0:512], SA[:, 512:1024], SBp[0][:, 0:512], SBp[1][:, 0:512]]
                    if i == 1:
                        dve.wait_ge(masks_set, 1)
                    for j in banks:
                        dve.wait_ge(scores_ready, 4 * i + j + 1)
                        if i:
                            dve.wait_ge(scores_kept, 4 * (i - 1) + j + 1)
                        src = bank[j + 6 * (i % 2) if j < 2 else j][:, :].rearrange("p (n t) -> p n t", n=4)
                        dst = dsts[j].rearrange("p (n t) -> p n t", n=4)
                        if i == 0:
                            ins = tt(dst, src, ident.unsqueeze(1).to_broadcast([P, 4, P]), ALU.mult)
                        else:
                            ins = dve.copy_predicated(dst, maskv[:, i - 1:i, :].to_broadcast([P, 4, P]), src)
                        ins.then_inc(scores_kept, 1)

                for i in range(1, len(LEVELS) + 2):
                    h = (LEVELS + (P,))[i - 1]
                    if i >= 3:
                        dve.wait_ge(scores_ready, 4 * (i - 1))
                    for buf, b_run in ((decA[i % 2], bA), (decB[i % 2], bB)):
                        v, bv = (z.rearrange("p (n c) -> p n c", c=2 * h) for z in (buf, b_run))
                        n = v.shape[1]
                        border = bv[:, :, h - 1:h]
                        if h == P:
                            ins = tt(v[:, :, 0:h], border.to_broadcast([P, n, h]), bv[:, :, 0:h], ALU.subtract)
                        else:
                            ins = tt(v, bv, border.to_broadcast([P, n, 2 * h]), ALU.subtract)
                        ins.then_inc(gap_ready, 1)
                    for g, (buf, k_, q_) in enumerate(((decA[i % 2], kA, qA), (decB[i % 2], kB, qB))):
                        if i == 1:
                            dve.wait_ge(aq_kept, 4)
                            dve.wait_ge(bqk_kept, 4)
                        v, kv, qv = (z.rearrange("p (n c) -> p n c", c=2 * h) for z in (buf, k_, q_))
                        dve.wait_ge(gap_exped, 4 * (i - 1) + 2 * g + 2)
                        tt(v[:, :, h:], v[:, :, h:], qv[:, :, h:], ALU.mult).then_inc(decayed, 1)
                        tt(v[:, :, 0:h], v[:, :, 0:h], kv[:, :, 0:h], ALU.mult).then_inc(decayed, 1)
                        if h < P:
                            keep(i - 1, (2 * g, 2 * g + 1))
                keep(len(LEVELS), (2, 3, 0, 1))
                rest_step(0, 16)

                for grp in range(2):
                    for a in range(TT):
                        b = 2 * a + grp
                        dve.wait_ge(*heads_squared.at(0, 2 * grp + a + 1))
                        mark(dve.tensor_reduce(head_ss[:, 4 * b:4 * b + 4],
                                               work(4608 + 512 * b, 512).rearrange("p (h c) -> p h c", h=HEADS), AX.X, ALU.add))
                    dve.wait_ge(vector_step, steps[0])
                    part = by_group(head_ss, grp)
                    ts(part, part, 1.0 / P, EPS, ALU.mult, ALU.add).then_inc(heads_mean.sem, 1)
                for grp in range(2):
                    dve.wait_ge(*heads_root.at(0, grp + 1))
                    part = by_group(head_r, grp)
                    link(dve.reciprocal(part, part))
                    dve.wait_ge(gates_open, 1)
                    for a in range(TT):
                        b = 2 * a + grp
                        if grp:
                            dve.wait_ge(*proj_kept.at(0, 7 + a))
                        for h in range(HEADS):
                            y = gates[:, a, grp * 512 + h * P:grp * 512 + (h + 1) * P]
                            stt(y, bank[b][:, h * P:(h + 1) * P], head_r[:, 4 * b + h:4 * b + h + 1], y,
                                ALU.mult, ALU.mult).then_inc(y_ready.sem, 1)
                    if grp == 0:
                        y_scale(0, 0, 6, vec("even_w"))
                        rest_step(0, 17)
                rest_step(0, 18)
                y_scale(0, 2, 6, vec("even_w"))
                rest_step(0, 19)
                finish_mix(0)

            def odd_mixer():
                mark(dve.memset(dx[:, :, 0:3], 0.0))
                dve.wait_ge(vector_step, steps[0])
                for i in (3, 4):
                    rest_step(1, i)
                for j in range(CONV):
                    for m in range(4):
                        if j == 0:
                            dve.wait_ge(dx_kept, m + 1)
                        o = xc[:, m * T:(m + 1) * T]
                        w = vec("conv_w", 4 * j + m, 4 * j + m + 1)
                        if j == 0:
                            mark(ts(o, dx[:, m, 0:T], w, vec("conv_b", m, m + 1), ALU.mult, ALU.add))
                        else:
                            dve.wait_ge(vector_step, steps[0] - (3 if j < CONV - 1 else 3 - m))
                            ins = stt(o, dx[:, m, j:j + T], w, o, ALU.mult, ALU.add)
                            if j < CONV - 1:
                                mark(ins)
                            else:
                                ins.then_inc(conv_done, 1)
                rest_step(1, 5)
                dve.wait_ge(qk_kept, 4)
                tables = const("rope").rearrange("p (w z t) -> p w z t", w=2, z=2)
                tmpv, rawv, rotv = (z.rearrange("p (z m t) -> p z m t", z=2, m=2) for z in (tmp, raw, rot))
                mark(tt(tmpv, rawv, tables[:, 0].unsqueeze(2).to_broadcast([P, 2, 2, T]), ALU.mult))
                rest_step(1, 6)
                dve.wait_ge(swapped, 2)
                for z in range(2):
                    mark(tt(rotv[:, z], bank[4 + z][:, :].rearrange("p (m t) -> p m t", m=2),
                            tables[:, 1, z:z + 1].to_broadcast([P, 2, T]), ALU.mult))
                dve.wait_ge(vector_step, steps[0])
                tt(rot, rot, tmp, ALU.add).then_inc(rotated, 1)
                dve.wait_ge(rg_gated, 8)
                dve.wait_ge(conv_done, 4)
                link(tt(xc, xc, ii, ALU.mult))
                rest_step(1, 7)
                dve.wait_ge(a_done, 4)
                dve.wait_ge(th_root, 1)
                link(stt(th, rr, 1.0, th, ALU.add, ALU.mult))
                link(tt(xc, xc, th, ALU.mult))
                for m in range(4):
                    part = slice(m * T, (m + 1) * T)
                    mark(dve.tensor_tensor_scan(ii[:, part], rr[:, part], xc[:, part], 0.0, ALU.mult, ALU.add))
                rest_step(1, 8)
                decay = const("decay").rearrange("p (q c) -> p q c", q=2)
                SCq = SC.rearrange("p (q c) -> p q c", q=2)
                for j, (q, a, b, bk) in enumerate(((0, 0, 512, 2), (1, 0, 512, 3), (0, 512, 768, 4), (1, 512, 768, 5))):
                    dve.wait_ge(ret_ready, j + 1)
                    tt(SCq[:, q, a:b], bank[bk][:, 0:b - a], decay[:, q, a:b], ALU.mult).then_inc(ret_kept, 1)
                dve.wait_ge(dg_squared, 1)
                link(ts(gl, gl, 0.044715, 1.0, ALU.mult, ALU.add))
                tt(gl, gl, dg, ALU.mult).then_inc(dg_inner, 1)
                rest_step(1, 9)
                dve.wait_ge(dg_tanh, 1)
                link(stt(gl, gl, 1.0, dg, ALU.add, ALU.mult))
                link(stt(dg, ii, 0.5, gl, ALU.mult, ALU.mult))
                dgv = dg.rearrange("p (k t) -> p k t", k=4)
                link(dve.tensor_copy(y_hi[:, 4:8, :], dgv))
                for k in range(4):
                    tt(y_lo[:, 4 + k, :], dgv[:, k, :], y_hi[:, 4 + k, :].bitcast(F32), ALU.subtract).then_inc(y_rest.sem, 1)
                rest_step(1, 10)
                for a in range(TT):
                    dve.wait_ge(*heads_ready.at(1, a + 1))
                    hv = bank[2 + a][:, :].rearrange("p (h c) -> p h c", h=HEADS)
                    mean = head_m[:, 4 * a:4 * a + 4]
                    link(dve.tensor_reduce(mean, hv, AX.X, ALU.add))
                    link(ts(mean, mean, 1.0 / P, None, ALU.mult))
                    tt(gates[:, a, 512:1024].rearrange("p (h c) -> p h c", h=HEADS), hv,
                       mean.unsqueeze(2).to_broadcast([P, HEADS, P]), ALU.subtract).then_inc(centred, 1)
                rest_step(1, 11)
                for a in range(TT):
                    dve.wait_ge(*heads_squared.at(1, a + 1))
                    mark(dve.tensor_reduce(head_ss[:, 4 * a:4 * a + 4],
                                           tmp[:, a * 512:(a + 1) * 512].rearrange("p (h c) -> p h c", h=HEADS), AX.X, ALU.add))
                dve.wait_ge(vector_step, steps[0])
                ts(head_ss[:, 0:8], head_ss[:, 0:8], 1.0 / P, EPS, ALU.mult, ALU.add).then_inc(heads_mean.sem, 1)
                dve.wait_ge(*heads_root.at(1, 1))
                link(dve.reciprocal(head_r[:, 0:8], head_r[:, 0:8]))
                rest_step(1, 12)
                for a in range(TT):
                    dve.wait_ge(*proj_kept.at(1, 3 + a))
                    for h in range(HEADS):
                        y = gates[:, a, h * P:(h + 1) * P]
                        stt(y, gates[:, a, 512 + h * P:512 + (h + 1) * P], head_r[:, 4 * a + h:4 * a + h + 1], y,
                            ALU.mult, ALU.mult).then_inc(y_ready.sem, 1)
                rest_step(1, 13)
                y_scale(1, 0, 0, vec("ret_w"))
                rest_step(1, 14)
                finish_mix(1)

            def route(l):
                small = [r_small[:, :, j, :] for j in range(8)]
                g, gap, e4, eq, pen = small[0], small[1], small[2], small[3], small[4]
                wide = [r_wide[:, j] for j in range(8)]
                lm, eq1, first, second, lm2 = wide[0], wide[1], wide[2], wide[3], wide[4]
                col = [r_wide[:, 5, :, j:j + 1] for j in range(8)]
                dve.wait_ge(*logits_turned.at(l, 1))
                dve.wait_ge(*scale_set.at(l, 1))
                dve.wait_ge(consts_loaded, 16)
                for a in range(TT):
                    bias, src = vec("b_route", l * ROUTE, (l + 1) * ROUTE), bank[OUT_BANKS[l][1]][:, a * 64:a * 64 + ROUTE]
                    mark(stt(g[:, a], src[:, 0:NG], scale[:, a:a + 1], bias[:, 0:NG], ALU.mult, ALU.add))
                    mark(stt(lm[:, a], src[:, NG:ROUTE], scale[:, a:a + 1], bias[:, NG:ROUTE], ALU.mult, ALU.add))
                dve.wait_ge(vector_step, steps[0])

                def one_hot(dst, values, top, ramp, n):
                    link(dve.tensor_reduce(top, values, AX.X, ALU.max))
                    for a in range(TT):
                        mark(stt(dst[:, a], values[:, a], top[:, a], ramp, ALU.is_equal, ALU.mult))
                    dve.wait_ge(vector_step, steps[0])
                    link(dve.tensor_reduce(col[7], dst, AX.X, ALU.max))
                    link(tt(dst, dst, col[7].to_broadcast([P, TT, n]), ALU.is_equal))

                one_hot(eq, g, col[0], const("down4"), NG)
                tt(gap, g, col[0].to_broadcast([P, TT, NG]), ALU.subtract).then_inc(group_gap.sem, 1)
                link(ts(pen, eq, -1.0, BIG1, ALU.add, ALU.mult))
                for a in range(TT):
                    v = lm[:, a].rearrange("p (g e) -> p g e", g=NG)
                    mark(tt(v, v, pen[:, a].unsqueeze(2).to_broadcast([P, NG, NE_G]), ALU.add))
                dve.wait_ge(vector_step, steps[0])
                one_hot(first, lm, col[1], const("down32"), NE)
                link(stt(lm2, first, -BIG2, lm, ALU.mult, ALU.add))
                one_hot(second, lm2, col[2], const("down32"), NE)
                tt(chosen[:, :, :], first, second, ALU.add).then_inc(chosen_set.sem, 1)
                tt(col[5], col[2], col[1], ALU.subtract).then_inc(pair_gap.sem, 1)
                dve.wait_ge(*group_exped.at(l, 1))
                link(dve.tensor_reduce(col[3], e4, AX.X, ALU.add))
                dve.wait_ge(*pair_exped.at(l, 1))
                link(ts(col[4], root[:, :].unsqueeze(2), 1.0, None, ALU.add))
                link(tt(col[3], col[3], col[4], ALU.mult))
                link(dve.reciprocal(col[3], col[3]))
                link(tt(col[4], root[:, :].unsqueeze(2), col[3], ALU.mult))
                mark(tt(first, first, col[3].to_broadcast([P, TT, NE]), ALU.mult))
                link(tt(second, second, col[4].to_broadcast([P, TT, NE]), ALU.mult))
                link(tt(gate[:, :, :], first, second, ALU.add))
                dve.wait_ge(*ranks_ready.at(l, 1))
                dve.wait_ge(*chosen_set.at(l, 1))
                dve.tensor_copy(counts[0:1, :], bank[5][0:1, 64:64 + NE]).then_inc(routed.sem, 1)
                stt(place[:, :, :], bank[5][:, 0:2 * NE].rearrange("p (a e) -> p a e", a=TT), 1.0, chosen[:, :, :],
                    ALU.add, ALU.mult).then_inc(routed.sem, 1)

            def experts(l, w):
                def expert(e, slot, loads, passes):
                    def body(base, n):
                        numbers = const("iota")[:, bass.ds(base.with_bounds(max_val=T - PASS), PASS)]
                        for a in range(TT):
                            ts(pick[:, a, :], numbers, place[:, a, bass.ds(e, 1)], None, ALU.is_equal).then_inc(picked, 1)
                        for a in range(TT):
                            ts(spread[:, a, :].rearrange("p (q s) -> p q s", q=Q), numbers.unsqueeze(1).to_broadcast([P, Q, PASS]),
                               place[:, a, bass.ds(e, 1)], gate[:, a, bass.ds(e, 1)], ALU.is_equal, ALU.mult).then_inc(spread_set, 1)
                        dve.wait_ge(got_turned, n + 1)
                        tt(got_T[:, :, :, :], bank[5][:, 0:T].rearrange("p (s q t) -> p s q t", s=2, q=Q),
                           w.rearrange("p (q s) -> p s q", s=2).unsqueeze(3).to_broadcast([P, 2, Q, PASS]),
                           ALU.mult).then_inc(got_scaled, 1)
                        dve.wait_ge(silu_done, n + 1)
                        tt(hid[:, :], silu[:, :], bank[6][:, P:2 * P], ALU.mult).then_inc(hid_ready, 1)
                        dve.wait_ge(hid_turned, n + 1)
                        dve.tensor_copy(hid_T[:, :, :].rearrange("p c t -> p (c t)"), bank[7][:, 0:P]).then_inc(hid_kept, 1)

                    passes(body)

                total = over_experts(dve, l, expert, lambda: dve.wait_ge(*routed.at(l, 2)))
                dve.wait_ge(scattered, total)
                for a in range(TT):
                    for q in range(Q):
                        part = x[:, a, q * T:(q + 1) * T]
                        ins = tt(part, part, bank[q][:, a * T:(a + 1) * T], ALU.add)
                        if q % 2:
                            ins.then_inc(x_added.sem, 1)

            for a in range(TT):
                dve.wait_ge(x_loaded[a], 16)
            norm_tokens(0, vec("norm_mix", 0, 8))
            lower_bound()
            softplus_start()
            even_mixer()
            route(0)
            experts(0, vec("norm_ffn", 0, 8))
            norm_tokens(2, vec("norm_mix", 8, 16))
            odd_mixer()
            route(1)
            experts(1, vec("norm_ffn", 8, 16))
            dve.wait_ge(final_w_loaded, 16)
            for a in range(TT):
                dve.wait_ge(*squared.at(4, a + 1))
                if a:
                    norm_mean(4)
                tt(x[:, a, :], x[:, a, :], const("rope"), ALU.mult).then_inc(weighed, 1)
            dve.wait_ge(*rooted.at(4, 1))
            dve.reciprocal(scale[:, :], root[:, :]).then_inc(final_scale, 1)
            dve.wait_ge(final_scale, 1)
            dve.wait_ge(weighed, 2)
            ts(tok[:, 1, :], x[:, 1, :], scale[:, 1:2], None, ALU.mult).then_inc(final_set_v, 1)


def kernel(**inputs):
    import concourse.bacc as bacc
    from concourse.bass_utils import run_bass_kernel_spmd

    a = {name: np.ascontiguousarray(v) for name, v in inputs.items()}

    def chunks(v):
        return v.reshape(P, -1)

    def columns(v):
        return v.reshape(-1, P).T

    def everywhere(v):
        return np.broadcast_to(v.reshape(1, -1), (P, v.size))

    parts = {
        "norm_mix": np.concatenate([chunks(v) for v in a["norm_mix"]], 1),
        "norm_ffn": np.concatenate([chunks(v) for v in a["norm_ffn"]], 1),
        "norm_route": np.concatenate([columns(v) for v in a["norm_ffn"]], 1),
        "lb": np.concatenate([columns(v) for v in a["hgrn_lb_logits"]], 1),
        "even_w": np.concatenate([columns(a["hgrn_norm_w"]), columns(a["gla_norm_w"])], 1),
        "gla_b": columns(a["gla_b_up"]), "ret_w": columns(a["ret_norm_w"]), "conv_w": columns(a["conv_w"]),
        "conv_b": columns(a["conv_b"]), "b_r": columns(a["rglru_b_r"]), "b_i": columns(a["rglru_b_i"]),
        "lam": columns(a["rglru_lambda"]),
        "w_route": np.concatenate([v.reshape(KC, P, ROUTE).transpose(1, 0, 2).reshape(P, -1)
                                   for v in np.concatenate([a["moe_w_group"], a["moe_w_expert"]], 2)], 1),
        "b_route": everywhere(np.concatenate([a["moe_b_group"], a["moe_b_expert"]], 1)),
    }
    assert all(parts[n].shape == (P, w) for n, w in VECTORS.items())
    packed, masks = shape_constants()
    feeds = {n: a[n] for n in ("x", "even_w_in", "even_w_out", "odd_w_in", "odd_w_out", "gla_w_up", "rglru_w_r",
                               "rglru_w_i", "moe_w1", "moe_w3", "moe_w2", "norm_final")}
    feeds["vectors"] = np.ascontiguousarray(np.concatenate([parts[n] for n in VECTORS], axis=1))
    feeds["shape_consts"] = packed
    feeds["masks"] = masks

    nc = bacc.Bacc("TRN2", target_bir_lowering=False, num_devices=1)
    args, arrays = [], {}
    for name, v in feeds.items():
        arrays[f"in_{name}_dram"] = v
        args.append(nc.dram_tensor(f"in_{name}_dram", v.shape, mybir.dt.from_np(v.dtype), kind="ExternalInput").ap())
    args.append(nc.dram_tensor("out_dram", (1, T, D), F32, kind="ExternalOutput").ap())
    trunk(nc, *args)
    r = run_bass_kernel_spmd(nc, [arrays], core_ids=[0])
    return r.results[0]["out_dram"]
```
